# Optimizing a Trainium2 kernel written in Bass

```python
import math
import jax, jax.numpy as jnp
from jax import lax
import numpy as np

D_MODEL = 1024
BATCH = 1
SEQ = 256
DEPTH = 2

MIX_WIDTH = D_MODEL
HEAD_DIM = 64
ATTN_WIDTH = D_MODEL // 2
N_Q_HEADS = ATTN_WIDTH // HEAD_DIM
N_KV_HEADS = N_Q_HEADS // 4
KV_WIDTH = N_KV_HEADS * HEAD_DIM
WINDOW = 128
BLOCK = 128
ROPE_THETA = 500000.0
ROPE_DIM = HEAD_DIM // 4
CONV_WIDTH = D_MODEL // 4
CONV_K = 3
POOL_WIDTH = D_MODEL // 4
POOL_WINDOWS = (2, 4, 8, 16)
POOL_GROUP = POOL_WIDTH // len(POOL_WINDOWS)
IN_WIDTH = ATTN_WIDTH + 2 * KV_WIDTH + 3 * CONV_WIDTH + POOL_WIDTH
IN_SPLITS = (ATTN_WIDTH,
             ATTN_WIDTH + KV_WIDTH,
             ATTN_WIDTH + 2 * KV_WIDTH,
             ATTN_WIDTH + 2 * KV_WIDTH + CONV_WIDTH,
             ATTN_WIDTH + 2 * KV_WIDTH + 2 * CONV_WIDTH,
             ATTN_WIDTH + 2 * KV_WIDTH + 3 * CONV_WIDTH)
PEER_HEADS = 8
PEER_NKEYS = 128
PEER_EXPERTS = PEER_NKEYS * PEER_NKEYS
PEER_QDIM = 256
PEER_TOPK = 16
PEER_CHUNK = 128
EPS = 1e-6
MASK_VALUE = -1e30


def rms_norm(t, g):
    tf = t.astype(jnp.float32)
    y = tf * lax.rsqrt(jnp.mean(tf * tf, axis=-1, keepdims=True) + EPS)
    return (y * g.astype(jnp.float32)).astype(t.dtype)

def rope_tables(positions):
    inv = ROPE_THETA ** (-jnp.arange(0, ROPE_DIM, 2, dtype=jnp.float32) / ROPE_DIM)
    ang = positions.astype(jnp.float32)[..., None] * inv
    return jnp.cos(ang)[:, :, None, :], jnp.sin(ang)[:, :, None, :]

def partial_rope(t, cos, sin):
    half = ROPE_DIM // 2
    t1 = t[..., :half].astype(jnp.float32)
    t2 = t[..., half:ROPE_DIM].astype(jnp.float32)
    rot = jnp.concatenate([t1 * cos - t2 * sin, t2 * cos + t1 * sin], axis=-1).astype(t.dtype)
    return jnp.concatenate([rot, t[..., ROPE_DIM:]], axis=-1)

def windowed_gqa(q, k, v, sink):
    b, s = q.shape[0], q.shape[1]
    nb = s // BLOCK
    grp = N_Q_HEADS // N_KV_HEADS
    qb = q.reshape(b, nb, BLOCK, N_KV_HEADS, grp, HEAD_DIM)

    def bands(t):
        tp = jnp.pad(t, ((0, 0), (BLOCK, BLOCK), (0, 0), (0, 0)))
        tp = tp.reshape(b, nb + 2, BLOCK, N_KV_HEADS, HEAD_DIM)
        return jnp.concatenate([tp[:, :-2], tp[:, 1:-1], tp[:, 2:]], axis=2)

    kb, vb = bands(k), bands(v)
    scores = jnp.einsum('bnqhgd,bnkhd->bnhgqk', qb, kb).astype(jnp.float32) * (HEAD_DIM ** -0.5)
    qpos = jnp.arange(s).reshape(nb, BLOCK, 1)
    kpos = (jnp.arange(nb)[:, None, None] - 1) * BLOCK + jnp.arange(3 * BLOCK)[None, None, :]
    valid = (jnp.abs(qpos - kpos) <= WINDOW) & (kpos >= 0) & (kpos < s)
    scores = jnp.where(valid[None, :, None, None], scores, MASK_VALUE)
    sink_col = jnp.broadcast_to(
        sink.astype(jnp.float32).reshape(1, 1, N_KV_HEADS, grp, 1, 1), scores.shape[:-1] + (1,))
    probs = jax.nn.softmax(jnp.concatenate([scores, sink_col], axis=-1), axis=-1)[..., :-1]
    out = jnp.einsum('bnhgqk,bnkhd->bnqhgd', probs.astype(v.dtype), vb)
    return out.reshape(b, s, N_Q_HEADS * HEAD_DIM)

def short_conv(u, w):
    up = jnp.pad(u, ((0, 0), (1, 1), (0, 0)))
    return w[0] * up[:, :-2] + w[1] * up[:, 1:-1] + w[2] * up[:, 2:]

def multiscale_pool(u):
    s = u.shape[1]
    t = jnp.arange(s)
    uf = u.astype(jnp.float32)
    cs = jnp.pad(jnp.cumsum(uf, axis=1), ((0, 0), (1, 0), (0, 0)))
    outs = []
    for gi, w in enumerate(POOL_WINDOWS):
        lo = jnp.clip(t - w // 2, 0, s)
        hi = jnp.clip(t + w // 2, 0, s)
        csg = cs[..., gi * POOL_GROUP:(gi + 1) * POOL_GROUP]
        cnt = (hi - lo).astype(jnp.float32)[None, :, None]
        mean = (jnp.take(csg, hi, axis=1) - jnp.take(csg, lo, axis=1)) / cnt
        outs.append(mean - uf[..., gi * POOL_GROUP:(gi + 1) * POOL_GROUP])
    return jnp.stack(outs, axis=2).astype(u.dtype)

def peer_ffn(h, w_q, sub_keys, expert_u, expert_v):
    b, s, d = h.shape
    n_tok = b * s
    ht = h.reshape(n_tok, d)
    q = (ht @ w_q).reshape(n_tok, PEER_HEADS, PEER_QDIM)
    half = PEER_QDIM // 2
    s1 = jnp.einsum('thd,kd->thk', q[..., :half], sub_keys[0]).astype(jnp.float32)
    s2 = jnp.einsum('thd,kd->thk', q[..., half:], sub_keys[1]).astype(jnp.float32)
    v1, i1 = lax.top_k(s1, PEER_TOPK)
    v2, i2 = lax.top_k(s2, PEER_TOPK)
    cand = (v1[..., :, None] + v2[..., None, :]).reshape(n_tok, PEER_HEADS, PEER_TOPK * PEER_TOPK)
    cidx = (i1[..., :, None] * PEER_NKEYS + i2[..., None, :]).reshape(n_tok, PEER_HEADS, PEER_TOPK * PEER_TOPK)
    top, pos = lax.top_k(cand, PEER_TOPK)
    eidx = jnp.take_along_axis(cidx, pos, axis=-1)
    gate = jax.nn.softmax(top, axis=-1).astype(h.dtype)
    n_chunks = n_tok // PEER_CHUNK

    def chunk(args):
        hc, ec, gc = args
        u = expert_u[ec]
        act = jax.nn.gelu(jnp.einsum('td,thkd->thk', hc, u), approximate=False)
        return jnp.einsum('thk,thkd->td', gc * act, expert_v[ec])

    y = lax.map(chunk, (ht.reshape(n_chunks, PEER_CHUNK, d),
                        eidx.reshape(n_chunks, PEER_CHUNK, PEER_HEADS, PEER_TOPK),
                        gate.reshape(n_chunks, PEER_CHUNK, PEER_HEADS, PEER_TOPK)))
    return y.reshape(b, s, d)

def first_inputs(seed: int = 0) -> dict:
    key = jax.random.key(seed)
    ks = jax.random.split(key, 20)
    L, D = DEPTH, D_MODEL

    def nrm(k, shape, scale):
        return jax.random.normal(k, shape, jnp.float32) * scale

    return {
        "x": nrm(ks[0], (BATCH, SEQ, D), 1.0),
        "c": nrm(ks[1], (BATCH, D), 1.0),
        "positions": jnp.arange(SEQ, dtype=jnp.int32)[None, :]
                     + jax.random.randint(ks[2], (BATCH, 1), 0, 1024, dtype=jnp.int32),
        "norm1_g": 1.0 + nrm(ks[3], (L, D), 0.02),
        "norm2_g": 1.0 + nrm(ks[4], (L, D), 0.02),
        "w_ada": nrm(ks[5], (L, D, 6 * D), 0.5 * D ** -0.5),
        "b_ada": nrm(ks[6], (L, 6 * D), 0.02),
        "w_in": nrm(ks[7], (L, D, IN_WIDTH), D ** -0.5),
        "q_norm_g": 1.0 + nrm(ks[8], (L, HEAD_DIM), 0.02),
        "k_norm_g": 1.0 + nrm(ks[9], (L, HEAD_DIM), 0.02),
        "attn_sink": nrm(ks[10], (L, N_Q_HEADS), 0.5),
        "conv_w": nrm(ks[11], (L, CONV_K, CONV_WIDTH), CONV_K ** -0.5),
        "pool_w": nrm(ks[12], (L, len(POOL_WINDOWS), POOL_GROUP, POOL_GROUP), POOL_GROUP ** -0.5),
        "pool_scale": 1.0 + nrm(ks[13], (L, POOL_WIDTH), 0.1),
        "w_out": nrm(ks[14], (L, MIX_WIDTH, D), MIX_WIDTH ** -0.5),
        "peer_wq": nrm(ks[15], (L, D, PEER_HEADS * PEER_QDIM), D ** -0.5),
        "peer_keys": nrm(ks[16], (L, 2, PEER_NKEYS, PEER_QDIM // 2), (PEER_QDIM // 2) ** -0.5),
        "peer_u": nrm(ks[17], (L, PEER_EXPERTS, D), D ** -0.5),
        "peer_v": nrm(ks[18], (L, PEER_EXPERTS, D), PEER_HEADS ** -0.5),
    }

def first_block(x, c, positions, norm1_g, norm2_g, w_ada, b_ada, w_in, q_norm_g, k_norm_g,
              attn_sink, conv_w, pool_w, pool_scale, w_out, peer_wq, peer_keys, peer_u, peer_v):
    b, s, d = x.shape
    cos, sin = rope_tables(positions)
    c_act = jax.nn.silu(c)
    for l in range(DEPTH):
        mod = (c_act @ w_ada[l] + b_ada[l])[:, None, :]
        shift1, scale1, gate1, shift2, scale2, gate2 = jnp.split(mod, 6, axis=-1)

        h = rms_norm(x, norm1_g[l]) * (1.0 + scale1) + shift1
        z = h @ w_in[l]
        q, k, v, conv_x, conv_b, conv_c, pool_x = jnp.split(z, IN_SPLITS, axis=-1)

        q = q.reshape(b, s, N_Q_HEADS, HEAD_DIM)
        k = k.reshape(b, s, N_KV_HEADS, HEAD_DIM)
        v = v.reshape(b, s, N_KV_HEADS, HEAD_DIM)
        q = partial_rope(rms_norm(q, q_norm_g[l]), cos, sin)
        k = partial_rope(rms_norm(k, k_norm_g[l]), cos, sin)
        attn_o = windowed_gqa(q, k, v, attn_sink[l])

        conv_o = conv_b * short_conv(conv_c * conv_x, conv_w[l])

        pooled = multiscale_pool(pool_x)
        pool_o = jnp.einsum('bsgc,gce->bsge', pooled, pool_w[l]).reshape(b, s, POOL_WIDTH) * pool_scale[l]

        mix = jnp.concatenate([attn_o, conv_o, pool_o], axis=-1) @ w_out[l]
        x = x + gate1 * mix

        h2 = rms_norm(x, norm2_g[l]) * (1.0 + scale2) + shift2
        x = x + gate2 * peer_ffn(h2, peer_wq[l], peer_keys[l], peer_u[l], peer_v[l])
    return x


RMS_EPS = 1e-6
Q_BLOCK = 128
NEG_INF = -1e30

T5_BUCKETS = 32
T5_MAX_EXACT = T5_BUCKETS // 2
T5_MAX_DISTANCE = 1024

DIFF_HEADS = 4
DIFF_HEAD_DIM = 64
DIFF_QK_WIDTH = DIFF_HEADS * 2 * DIFF_HEAD_DIM
DIFF_V_WIDTH = DIFF_HEADS * 2 * DIFF_HEAD_DIM

MOBA_HEADS = 4
MOBA_HEAD_DIM = 128
MOBA_BLOCK = 256
MOBA_TOPK = 3
MOBA_Q_CHUNK = 32
MOBA_WIDTH = MOBA_HEADS * MOBA_HEAD_DIM

MLA_HEADS = 8
MLA_Q_RANK = 256
MLA_KV_RANK = 128
MLA_NOPE_DIM = 64
MLA_ROPE_DIM = 32
MLA_V_DIM = 64
MLA_WIDTH = MLA_HEADS * MLA_V_DIM
ROPE_THETA_2 = 10000.0

N_BRANCH = 3
BRANCH_WIDTH = 512
N_BIAS_HEADS = DIFF_HEADS + MOBA_HEADS
D_FF = 4 * D_MODEL

IN_SPLITS_2 = (DIFF_QK_WIDTH, DIFF_QK_WIDTH, DIFF_V_WIDTH,
             MOBA_WIDTH, MOBA_WIDTH, MOBA_WIDTH,
             MLA_Q_RANK, MLA_KV_RANK, MLA_ROPE_DIM,
             N_BRANCH * D_MODEL)
IN_OFFSETS = tuple(sum(IN_SPLITS_2[:i + 1]) for i in range(len(IN_SPLITS_2) - 1))
D_IN = sum(IN_SPLITS_2)


def _rms_norm(x, w):
    xf = x.astype(jnp.float32)
    y = xf * lax.rsqrt(jnp.mean(xf * xf, axis=-1, keepdims=True) + RMS_EPS)
    return (y * w.astype(jnp.float32)).astype(x.dtype)

def _t5_bucket(rel):
    n = jnp.maximum(rel, 0)
    nf = jnp.maximum(n, 1).astype(jnp.float32)
    large = T5_MAX_EXACT + (jnp.log(nf / T5_MAX_EXACT)
                            / math.log(T5_MAX_DISTANCE / T5_MAX_EXACT)
                            * (T5_BUCKETS - T5_MAX_EXACT)).astype(jnp.int32)
    large = jnp.minimum(large, T5_BUCKETS - 1)
    return jnp.where(n < T5_MAX_EXACT, n, large)

def _rope(x, positions):
    d = x.shape[-1]
    half = d // 2
    inv_freq = ROPE_THETA_2 ** (-jnp.arange(half, dtype=jnp.float32) * 2.0 / d)
    ang = positions.astype(jnp.float32)[:, :, None, None] * inv_freq
    cos, sin = jnp.cos(ang), jnp.sin(ang)
    xf = x.astype(jnp.float32)
    x1, x2 = xf[..., :half], xf[..., half:]
    return jnp.concatenate([x1 * cos - x2 * sin, x2 * cos + x1 * sin], axis=-1).astype(x.dtype)

def _diff_attention(q1, q2, k1, k2, v, lam, bias_table):
    B, S, H, dh = q1.shape
    scale = 1.0 / math.sqrt(dh)
    k_pos = jnp.arange(S)
    table = bias_table.astype(jnp.float32)

    def block(c):
        start = c * Q_BLOCK
        q_pos = start + jnp.arange(Q_BLOCK)
        rel = q_pos[:, None] - k_pos[None, :]
        bias = jnp.transpose(table[_t5_bucket(rel)], (2, 0, 1))
        visible = rel >= 0

        def probs(q, k):
            qb = lax.dynamic_slice_in_dim(q, start, Q_BLOCK, axis=1)
            s = jnp.einsum('bqhd,bkhd->bhqk', qb, k).astype(jnp.float32) * scale + bias
            return jax.nn.softmax(jnp.where(visible, s, NEG_INF), axis=-1)

        w = probs(q1, k1) - lam * probs(q2, k2)
        return jnp.einsum('bhqk,bkhd->bqhd', w.astype(v.dtype), v)

    out = lax.map(block, jnp.arange(S // Q_BLOCK))
    return jnp.transpose(out, (1, 0, 2, 3, 4)).reshape(B, S, H, v.shape[-1])

def _moba_attention(q, k, v, bias_table):
    B, S, H, d = q.shape
    scale = 1.0 / math.sqrt(d)
    n_blk = -(-S // MOBA_BLOCK)
    s_pad = n_blk * MOBA_BLOCK
    topk = min(MOBA_TOPK, n_blk)
    pad = ((0, 0), (0, s_pad - S), (0, 0), (0, 0))
    kbh = jnp.transpose(jnp.pad(k, pad).reshape(B, n_blk, MOBA_BLOCK, H, d), (0, 3, 1, 2, 4))
    vbh = jnp.transpose(jnp.pad(v, pad).reshape(B, n_blk, MOBA_BLOCK, H, d), (0, 3, 1, 2, 4))
    k_mean = jnp.mean(kbh.astype(jnp.float32), axis=3)
    blk_ids = jnp.arange(n_blk)
    offs = jnp.arange(MOBA_BLOCK)
    table = bias_table.astype(jnp.float32)
    table_t = table.T
    bi = jnp.arange(B)[:, None, None, None]
    hi = jnp.arange(H)[None, :, None, None]
    hi5 = jnp.arange(H)[None, :, None, None, None]

    def chunk(c):
        start = c * MOBA_Q_CHUNK
        own = start // MOBA_BLOCK
        q_pos = start + jnp.arange(MOBA_Q_CHUNK)
        qbt = jnp.transpose(lax.dynamic_slice_in_dim(q, start, MOBA_Q_CHUNK, axis=1), (0, 2, 1, 3))
        gate = jnp.einsum('bhqd,bhnd->bhqn', qbt.astype(jnp.float32), k_mean)
        gate = jnp.where(blk_ids < own, gate, NEG_INF)
        _, idx = lax.top_k(gate, topk)
        valid = idx < own
        k_sel = kbh[bi, hi, idx]
        v_sel = vbh[bi, hi, idx]
        s_sel = jnp.einsum('bhqd,bhqnld->bhqnl', qbt, k_sel).astype(jnp.float32) * scale
        sel_pos = idx[..., None] * MOBA_BLOCK + offs
        rel_sel = q_pos[None, None, :, None, None] - sel_pos
        s_sel = jnp.where(valid[..., None], s_sel + table_t[hi5, _t5_bucket(rel_sel)], NEG_INF)
        k_own = lax.dynamic_index_in_dim(kbh, own, axis=2, keepdims=False)
        v_own = lax.dynamic_index_in_dim(vbh, own, axis=2, keepdims=False)
        rel_own = q_pos[:, None] - (own * MOBA_BLOCK + offs)[None, :]
        bias_own = jnp.transpose(table[_t5_bucket(rel_own)], (2, 0, 1))
        s_own = jnp.einsum('bhqd,bhld->bhql', qbt, k_own).astype(jnp.float32) * scale + bias_own
        s_own = jnp.where(rel_own >= 0, s_own, NEG_INF)
        n_sel = topk * MOBA_BLOCK
        s = jnp.concatenate([s_sel.reshape(B, H, MOBA_Q_CHUNK, n_sel), s_own], axis=-1)
        p = jax.nn.softmax(s, axis=-1).astype(v.dtype)
        p_sel = p[..., :n_sel].reshape(B, H, MOBA_Q_CHUNK, topk, MOBA_BLOCK)
        p_own = p[..., n_sel:]
        return (jnp.einsum('bhqnl,bhqnld->bqhd', p_sel, v_sel)
                + jnp.einsum('bhql,bhld->bqhd', p_own, v_own))

    out = lax.map(chunk, jnp.arange(S // MOBA_Q_CHUNK))
    return jnp.transpose(out, (1, 0, 2, 3, 4)).reshape(B, S, H, d)

def _dense_causal_attention(q, k, v, scale):
    B, S, H, _ = q.shape
    k_pos = jnp.arange(S)

    def block(c):
        start = c * Q_BLOCK
        qb = lax.dynamic_slice_in_dim(q, start, Q_BLOCK, axis=1)
        s = jnp.einsum('bqhd,bkhd->bhqk', qb, k).astype(jnp.float32) * scale
        rel = (start + jnp.arange(Q_BLOCK))[:, None] - k_pos[None, :]
        p = jax.nn.softmax(jnp.where(rel >= 0, s, NEG_INF), axis=-1).astype(v.dtype)
        return jnp.einsum('bhqk,bkhd->bqhd', p, v)

    out = lax.map(block, jnp.arange(S // Q_BLOCK))
    return jnp.transpose(out, (1, 0, 2, 3, 4)).reshape(B, S, H, v.shape[-1])

def second_inputs(seed: int = 0) -> dict:
    key = jax.random.key(seed)
    ks = jax.random.split(key, 20)

    def nrm(k, shape, scale):
        return jax.random.normal(k, shape, jnp.float32) * scale

    x = nrm(ks[0], (BATCH, SEQ, D_MODEL), 1.0)
    offsets = jax.random.randint(ks[1], (BATCH, 1), 0, 4096, dtype=jnp.int32)
    positions = offsets + jnp.arange(SEQ, dtype=jnp.int32)[None, :]
    return {
        'x': x,
        'positions': positions,
        'rel_bias': nrm(ks[2], (T5_BUCKETS, N_BIAS_HEADS), 0.5),
        'norm_mix_pre': 1.0 + nrm(ks[3], (DEPTH, D_MODEL), 0.05),
        'norm_mix_post': 1.0 + nrm(ks[4], (DEPTH, D_MODEL), 0.05),
        'norm_mlp_pre': 1.0 + nrm(ks[5], (DEPTH, D_MODEL), 0.05),
        'norm_mlp_post': 1.0 + nrm(ks[6], (DEPTH, D_MODEL), 0.05),
        'w_in': nrm(ks[7], (DEPTH, D_MODEL, D_IN), D_MODEL ** -0.5),
        'diff_lambda': nrm(ks[8], (DEPTH, 4, DIFF_HEAD_DIM), 0.1),
        'diff_subln': 1.0 + nrm(ks[9], (DEPTH, 2 * DIFF_HEAD_DIM), 0.05),
        'mla_q_norm': 1.0 + nrm(ks[10], (DEPTH, MLA_Q_RANK), 0.05),
        'mla_w_uq': nrm(ks[11], (DEPTH, MLA_Q_RANK, MLA_HEADS * (MLA_NOPE_DIM + MLA_ROPE_DIM)), MLA_Q_RANK ** -0.5),
        'mla_kv_norm': 1.0 + nrm(ks[12], (DEPTH, MLA_KV_RANK), 0.05),
        'mla_w_ukv': nrm(ks[13], (DEPTH, MLA_KV_RANK, MLA_HEADS * (MLA_NOPE_DIM + MLA_V_DIM)), MLA_KV_RANK ** -0.5),
        'w_branch': nrm(ks[14], (DEPTH, N_BRANCH, BRANCH_WIDTH, D_MODEL), BRANCH_WIDTH ** -0.5),
        'w_out': nrm(ks[15], (DEPTH, D_MODEL, D_MODEL), D_MODEL ** -0.5),
        'w_up': nrm(ks[16], (DEPTH, D_MODEL, D_FF), D_MODEL ** -0.5),
        'w_down': nrm(ks[17], (DEPTH, D_FF, D_MODEL), D_FF ** -0.5),
    }

def second_block(x, positions, rel_bias, norm_mix_pre, norm_mix_post, norm_mlp_pre, norm_mlp_post,
              w_in, diff_lambda, diff_subln, mla_q_norm, mla_w_uq, mla_kv_norm, mla_w_ukv,
              w_branch, w_out, w_up, w_down):
    B, S, _ = x.shape
    for l in range(DEPTH):
        lam_init = 0.8 - 0.6 * math.exp(-0.3 * l)
        h = _rms_norm(x, norm_mix_pre[l])
        proj = jnp.einsum('bsd,de->bse', h, w_in[l])
        dq, dk, dv, mq, mk, mv, c_q, c_kv, k_pe, g = jnp.split(proj, IN_OFFSETS, axis=-1)

        dq = dq.reshape(B, S, DIFF_HEADS, 2, DIFF_HEAD_DIM)
        dk = dk.reshape(B, S, DIFF_HEADS, 2, DIFF_HEAD_DIM)
        dv = dv.reshape(B, S, DIFF_HEADS, 2 * DIFF_HEAD_DIM)
        lam_vecs = diff_lambda[l].astype(jnp.float32)
        lam = (jnp.exp(jnp.sum(lam_vecs[0] * lam_vecs[1]))
               - jnp.exp(jnp.sum(lam_vecs[2] * lam_vecs[3])) + lam_init)
        oa = _diff_attention(dq[..., 0, :], dq[..., 1, :], dk[..., 0, :], dk[..., 1, :], dv,
                             lam, rel_bias[:, :DIFF_HEADS])
        oa = (_rms_norm(oa, diff_subln[l]) * (1.0 - lam_init)).reshape(B, S, DIFF_V_WIDTH)

        ob = _moba_attention(mq.reshape(B, S, MOBA_HEADS, MOBA_HEAD_DIM),
                             mk.reshape(B, S, MOBA_HEADS, MOBA_HEAD_DIM),
                             mv.reshape(B, S, MOBA_HEADS, MOBA_HEAD_DIM),
                             rel_bias[:, DIFF_HEADS:]).reshape(B, S, MOBA_WIDTH)

        q = jnp.einsum('bsr,re->bse', _rms_norm(c_q, mla_q_norm[l]), mla_w_uq[l])
        q = q.reshape(B, S, MLA_HEADS, MLA_NOPE_DIM + MLA_ROPE_DIM)
        q = jnp.concatenate([q[..., :MLA_NOPE_DIM], _rope(q[..., MLA_NOPE_DIM:], positions)], axis=-1)
        kv = jnp.einsum('bsr,re->bse', _rms_norm(c_kv, mla_kv_norm[l]), mla_w_ukv[l])
        kv = kv.reshape(B, S, MLA_HEADS, MLA_NOPE_DIM + MLA_V_DIM)
        k_rope = jnp.broadcast_to(_rope(k_pe[:, :, None, :], positions), (B, S, MLA_HEADS, MLA_ROPE_DIM))
        k = jnp.concatenate([kv[..., :MLA_NOPE_DIM], k_rope], axis=-1)
        oc = _dense_causal_attention(q, k, kv[..., MLA_NOPE_DIM:],
                                     1.0 / math.sqrt(MLA_NOPE_DIM + MLA_ROPE_DIM)).reshape(B, S, MLA_WIDTH)

        branches = jnp.stack([oa, ob, oc], axis=2)
        br = jnp.einsum('bsgc,gcd->bsgd', branches, w_branch[l])
        gates = jax.nn.sigmoid(g.reshape(B, S, N_BRANCH, D_MODEL))
        mixed = jnp.einsum('bsd,de->bse', jnp.sum(gates * br, axis=2), w_out[l])
        x = x + _rms_norm(mixed, norm_mix_post[l])

        h = _rms_norm(x, norm_mlp_pre[l])
        u = jnp.square(jax.nn.relu(jnp.einsum('bsd,df->bsf', h, w_up[l])))
        x = x + _rms_norm(jnp.einsum('bsf,fd->bsd', u, w_down[l]), norm_mlp_post[l])
    return x


def setup_inputs(seed=0):
    out = dict(first_inputs(seed))
    for name, value in second_inputs(seed + 1).items():
        if name != "x":
            out[name + "_2"] = value
    return out


def reference(
    x, c, positions, norm1_g, norm2_g, w_ada, b_ada, w_in, q_norm_g, k_norm_g, attn_sink,
    conv_w, pool_w, pool_scale, w_out, peer_wq, peer_keys, peer_u, peer_v, positions_2,
    rel_bias_2, norm_mix_pre_2, norm_mix_post_2, norm_mlp_pre_2, norm_mlp_post_2, w_in_2,
    diff_lambda_2, diff_subln_2, mla_q_norm_2, mla_w_uq_2, mla_kv_norm_2, mla_w_ukv_2,
    w_branch_2, w_out_2, w_up_2, w_down_2,
):
    x = first_block(
        x, c, positions, norm1_g, norm2_g, w_ada, b_ada, w_in, q_norm_g, k_norm_g, attn_sink,
        conv_w, pool_w, pool_scale, w_out, peer_wq, peer_keys, peer_u, peer_v,
    )
    return second_block(
        x, positions_2, rel_bias_2, norm_mix_pre_2, norm_mix_post_2, norm_mlp_pre_2,
        norm_mlp_post_2, w_in_2, diff_lambda_2, diff_subln_2, mla_q_norm_2, mla_w_uq_2,
        mla_kv_norm_2, mla_w_ukv_2, w_branch_2, w_out_2, w_up_2, w_down_2,
    )


_drawn_inputs = setup_inputs


def setup_inputs(seed=0):
    import zlib

    import numpy as np

    out = dict(_drawn_inputs(seed))
    spreads = {}
    factors = {'norm1_g': 3.192,
     'norm2_g': 20.043,
     'q_norm_g': 8.0,
     'k_norm_g': 8.0,
     'attn_sink': 8.0,
     'mla_q_norm_2': 5.907,
     'mla_kv_norm_2': 2.963,
     'pool_scale': 2.942,
     'rel_bias_2': 3.349,
     'norm_mix_post_2': 6.021,
     'norm_mlp_pre_2': 5.667,
     'norm_mlp_post_2': 6.268,
     'diff_lambda_2': 6.849,
     'diff_subln_2': 8.0}
    for name, (base, spread) in spreads.items():
        noise = np.random.default_rng([zlib.crc32(name.encode()), seed]).standard_normal(out[name].shape)
        drawn = base * np.exp(spread * noise) if base else spread * noise
        out[name] = __import__('jax').numpy.asarray(drawn.astype(out[name].dtype))
    for name, factor in factors.items():
        out[name] = (out[name] * factor).astype(out[name].dtype)
    return out
```

```python
from contextlib import ExitStack

import numpy as np

import concourse.bass as bass
from concourse import mybir

F32 = mybir.dt.float32
I32 = mybir.dt.int32
U32 = mybir.dt.uint32
ALU = mybir.AluOpType
ACT = mybir.ActivationFunctionType
X = mybir.AxisListType.X

P = 128
D = 1024
S = 256
T = S // P
KD = D // P
DEPTH = 2
EPS = 1e-6
NEG = -1e30

HD = 64
QW, KVW, CW, PW = 512, 128, 256, 256
QKH = (QW + KVW) // HD
PH, PK = 8, 16
NKEYS = 128
PLACES = 4
TOKG = 4
DH, MH, LH = 4, 4, 8
NOPE, ROPE2, VD = 64, 32, 64
LQ = NOPE + ROPE2
QR, KVR = 256, 128
FF = 4096
NB = 3
BW = 512
BUCKETS = 32
GC = D // 512

TWO_PI_HI = 6.28125
TWO_PI_MID = 0.0019340515136718750
TWO_PI_LO = 2 * np.pi - TWO_PI_HI - TWO_PI_MID
ARENA = 39424
N_CONSTS = 7
ROUND_MAGIC = 1.5 * 2 ** 23



class Ring:

    def __init__(self, full, free, uses, per_full=1):
        self.full, self.free, self.per_full = full, free, per_full
        self.at, self.per, self.base = {}, {}, {}
        n, base = len(full), 0
        for block, names in uses.items():
            assert len(names) % n == 0, (block, len(names), n)
            self.base[block], self.per[block] = base, len(names) // n
            base += DEPTH * self.per[block]
            for i, name in enumerate(names):
                self.at[block, name] = (i % n, i // n)

    def buf(self, block, name):
        return self.at[block, name][0]

    def count(self, block, l, name):
        return self.base[block] + l * self.per[block] + self.at[block, name][1] + 1

    def free_at(self, block, l, name):
        return self.free[self.buf(block, name)], self.count(block, l, name)

    def full_at(self, block, l, name, more=0):
        return self.full[self.buf(block, name)], (self.count(block, l, name) + more) * self.per_full

    def emptied_at(self, block, l, name):
        return self.free[self.buf(block, name)], self.count(block, l, name) + 1

    def full_sem(self, block, name):
        return self.full[self.buf(block, name)]

    def free_sem(self, block, name):
        return self.free[self.buf(block, name)]


class Signal:

    def __init__(self, sem, a=0, b=0, step=1, primed=0):
        self.sem, self.step, self.primed = sem, step, primed
        self.per = {"a": a, "b": b}
        self.base = {"a": 0, "b": DEPTH * a}

    def at(self, block, l, k):
        return self.sem, (self.base[block] + l * self.per[block] + k) * self.step + self.primed

    def two_before(self, block, l, k):
        return self.sem, self.base[block] + l * self.per[block] + k


class Region:

    def __init__(self, tensor, start=0):
        self.t, self.at = tensor, start

    def take(self, *shape):
        n = int(np.prod(shape))
        v = self.t[:, self.at:self.at + n]
        self.at += n
        if len(shape) == 2:
            v = v.rearrange("p (a b) -> p a b", a=shape[0])
        elif len(shape) == 3:
            v = v.rearrange("p (a b c) -> p a b c", a=shape[0], b=shape[1])
        elif len(shape) == 4:
            v = v.rearrange("p (a b c d) -> p a b c d", a=shape[0], b=shape[1], c=shape[2])
        return v


def spread(ap, axis, n):
    v = ap.unsqueeze(axis)
    shape = list(v.shape)
    shape[axis] = n
    return v.broadcast_to(shape)



SLABS = {
    "a": [f"ada{i}" for i in range(12)] + [f"in{i}" for i in range(4)] + ["out0", "out1"]
         + [f"wq{i}" for i in range(4)],
    "b": ["dq", "dk", "dv", "mq", "mk", "mv", "misc", "g0", "uq", "g1", "ukv", "g2", "g3", "g4", "g5"]
         + [f"br{c}" for c in range(NB)] + ["wo0", "wo1"] + [f"up{i}" for i in range(8)]
         + [f"dn{i}" for i in range(8)],
}
ACCS = {
    "a": [f"ada{i}" for i in range(12)] + [f"in{i}" for i in range(4)] + ["pool0", "pool1"]
         + [f"sc{i}" for i in range(4)] + ["out0", "out1", "wq0", "wq1", "s0", "wq2", "s1", "wq3", "s2", "s3"],
    "b": ["dq", "dk", "sc0", "dv", "sc1", "mq", "sc2", "mk", "sc3", "mv", "sc4", "misc0", "sc5", "misc1",
          "g0", "uq0", "uq1", "g1", "ukv0", "ukv1", "g2", "sc6", "g3", "sc7", "g4", "sc8", "g5", "sc9"]
         + [f"br{c}_{n}" for c in range(NB) for n in range(GC)] + ["wo0", "wo1"]
         + [f"up{i}" for i in range(8)] + ["dn0", "dn1"],
}
TURNS = {
    "a": [f"h1_{i}" for i in range(4)] + ["keys", "q0", "q1", "k"] + [f"pv{g}" for g in range(4)]
         + ["mix0", "mix1"] + [f"h2_{i}" for i in range(4)] + ["pairs0", "pairs1"],
    "b": [f"h_{i}" for i in range(4)] + [f"pv{g}" for g in range(4)] + ["cq", "ckv", "pv4", "pv5"]
         + [f"qm{i}" for i in range(4)] + [f"km{i}" for i in range(4)] + [f"pv{g}" for g in range(6, 10)]
         + [f"bt{i}" for i in range(6)] + [f"mx_{i}" for i in range(4)] + [f"hm_{i}" for i in range(4)],
}
PROBS = {
    "a": [f"pt{g}_{i}" for g in range(4) for i in range(2)],
    "b": [f"pt{g}_{i}" for g in range(10) for i in range(2)],
}
SLAB_ENDS = {
    "a": {},
    "b": {"misc": "misc1", "uq": "uq1", "ukv": "ukv1", "br0": "br0_1", "br1": "br1_1", "br2": "br2_1", "dn7": "dn1"},
}


def two_blocks(nc, io, out):
    ctx = ExitStack()
    with ctx:
        def sem(name):
            return ctx.enter_context(nc.semaphore(name))

        def sb(name, shape, dt=F32):
            return ctx.enter_context(nc.sbuf_tensor(name, shape, dt))

        acc = ctx.enter_context(nc.psum_tensor("acc", [P, 2, 4, S], F32))
        prob_ps = ctx.enter_context(nc.psum_tensor("prob_ps", [P, 2, 512], F32))
        turn_ps = ctx.enter_context(nc.psum_tensor("turn_ps", [P, 2, 512], F32))
        y_ps = acc[:].rearrange("p b (n x) s -> p b n (x s)", n=2)

        slabs = Ring([sem("slab_full0"), sem("slab_full1")], [None, None], SLABS, per_full=32)
        accs = Ring([sem("acc_full0"), sem("acc_full1")], [sem("acc_free0"), sem("acc_free1")], ACCS)
        turns = Ring([sem("turn_full0"), sem("turn_full1")], [sem("turn_free0"), sem("turn_free1")], TURNS)
        probs = Ring([sem("prob_full0"), sem("prob_full1")], [sem("prob_free0"), sem("prob_free1")], PROBS)
        consts_in = sem("consts_in")
        x_in = sem("x_in")
        c_ready = sem("c_ready")
        c_exp = sem("c_exp")
        angle_ready = sem("angle_ready")
        trig_done = sem("trig_done")
        half_ready = sem("half_ready")
        params = Signal(sem("params"), a=15, b=9, step=16)
        var_ready = Signal(sem("var_ready"), a=3, b=6)
        rstd_ready = Signal(sem("rstd_ready"), a=3, b=6)
        h_ready = Signal(sem("h_ready"), a=2, b=2)
        qk_ready = Signal(sem("qk_ready"), a=1, b=4)
        sm_ready = Signal(sem("sm_ready"), a=4, b=10)
        p_ready = Signal(sem("p_ready"), a=4, b=10)
        sink_ready = Signal(sem("sink_ready"), a=4, b=0)
        sink_exp = Signal(sem("sink_exp"), a=4, b=0)
        conv_ready = Signal(sem("conv_ready"), a=1, b=0)
        mix_ready = Signal(sem("mix_ready"), a=1, b=4)
        top_ready = Signal(sem("top_ready"), a=1)
        top_exp = Signal(sem("top_exp"), a=1)
        pairs_ready = Signal(sem("pairs_ready"), a=2)
        rows_built = Signal(sem("rows_built"), a=S // TOKG)
        gates_full = Signal(sem("gates_full"), a=S // TOKG, primed=2)
        gates_kept = Signal(sem("gates_kept"), a=S // TOKG, primed=2)
        ut_full = Signal(sem("ut_full"), a=NKEYS)
        ut_act = Signal(sem("ut_act"), a=NKEYS)
        ut_dve = Signal(sem("ut_dve"), a=NKEYS)
        am_full = Signal(sem("am_full"), a=NKEYS)
        gelu_done = Signal(sem("gelu_done"), a=NKEYS)
        wt_ready = Signal(sem("wt_ready"), a=NKEYS)
        v_used = Signal(sem("v_used"), a=NKEYS)
        u_in = [Signal(sem(f"u_in{q}"), a=NKEYS // PLACES, step=16) for q in range(PLACES)]
        v_in = [Signal(sem(f"v_in{q}"), a=NKEYS // PLACES, step=16) for q in range(PLACES)]
        y_full = Signal(sem("y_full"), a=1)
        layer_done = Signal(sem("layer_done"), a=1, b=1)
        down_used = Signal(sem("down_used"), b=8)
        lam_dot = Signal(sem("lam_dot"), b=1)
        lam_exp = Signal(sem("lam_exp"), b=1)
        relu_done = Signal(sem("relu_done"), b=8)
        u_ready = Signal(sem("u_ready"), b=8)
        t5_in = sem("t5_in")
        t5_row = sem("t5_row")
        t5_kept = sem("t5_kept")
        t5_out = sem("t5_out")
        t5_skew = sem("t5_skew")
        t5_flip = sem("t5_flip")
        t5_done = sem("t5_done")
        stored = sem("stored")
        passed = {e: sem(f"passed_{e}") for e in ("sp", "pe", "dve")}

        x = sb("x", [P, T, D])
        hT = sb("hT", [P, KD, S])
        slab = sb("slab", [P, 2, 4096])
        expert_u = slab[:, 0].rearrange("p (q d) -> p q d", q=PLACES)
        expert_v = slab[:, 1].rearrange("p (q d) -> p q d", q=PLACES)
        ident = sb("ident", [P, P])
        iota = sb("iota", [P, P])
        small = sb("small", [P, 1024])
        arena = sb("arena", [P, ARENA])
        sr = Region(small)
        var = sr.take(32)
        rstd = sr.take(32)
        neghalf = sr.take(32)
        cosA, sinA = sr.take(T, 8), sr.take(T, 8)
        cosB, sinB = sr.take(T, 16), sr.take(T, 16)
        den = sr.take(2, 4)
        rden = sr.take(2, 4)
        mx = sr.take(4)
        nm = sr.take(2, 4)
        esink = sr.take(2, 4)
        sinks = sr.take(8)
        dsum = sr.take(16)
        conv_w = sr.take(2, 3)
        pool_s = sr.take(2)
        lamc = sr.take(2)
        ldot = sr.take(2)
        lexp = sr.take(2)
        neglam = sr.take(1)
        cT, csg, cac = sr.take(8), sr.take(8), sr.take(8)
        tmp_small = sr.take(64)
        posi = sr.take(T)
        posf = sr.take(T, 2)
        freqs = sr.take(24)
        ang, turnsN, redu, absr = sr.take(48), sr.take(48), sr.take(48), sr.take(48)
        posi2 = sr.take(T)
        assert sr.at <= 1024

        G = Region(arena).take(NKEYS, S)
        ra = Region(arena)
        mod = ra.take(6, D)
        gain1, gain2 = ra.take(D), ra.take(D)
        hn = ra.take(T, D)
        z = ra.take(T, D)
        zT = ra.take(6, S)
        mixT = ra.take(KD, S)
        sm = ra.take(2, 4, S)
        pT = ra.take(2, 4, 2, P)
        oa = ra.take(T, QW)
        qT = ra.take(4, S)
        kT = ra.take(S)
        plT = ra.take(2, S)
        pool_m = ra.take(T, 4, S)
        pool_wt = ra.take(2, 64)
        window = ra.take(T, S)
        conv_u = ra.take(2, S + 2)
        conv_a = ra.take(2, S)
        sq_a = ra.take(T, QKH * HD)
        rope_t = ra.take(4, T, QKH * 8)
        qg, kg = ra.take(HD), ra.take(HD)
        assert ra.at <= NKEYS * S, ra.at
        rb = Region(arena, 8192 + 2048)
        scores = rb.take(T, 16, NKEYS)
        pqT = rb.take(2, 4, S)
        top_v = rb.take(T, 2 * PH, PK)
        top_i = rb.take(T, 2 * PH, PK)
        top_f = rb.take(T, 2 * PH, PK)
        cand = rb.take(T, PH, PK * PK)
        best = rb.take(T, PH, PK)
        best_p = rb.take(T, PH * PK)
        best_h = rb.take(2, T, PH * PK)
        best_hf = rb.take(2, T, PH * PK)
        pick = rb.take(2, PH * PK * PK)
        pairs = rb.take(3, T, PH * PK)
        assert rb.at <= NKEYS * S, rb.at
        rc = Region(arena, NKEYS * S)
        gate2 = rc.take(D)
        pairsT = rc.take(3, S)
        cbc = rc.take(KD, P)
        ut_at = rc.at
        utT = rc.take(2, KD, P)
        rows = Region(arena, ut_at).take(2, 2, TOKG, P)
        ga = rc.take(2, S)
        wt = rc.take(2, S)
        keys0, keysT = rc.take(2, P), rc.take(2, P)
        assert rc.at <= ARENA, rc.at

        rd = Region(arena)
        bn = rd.take(T, D)
        wpre, wpost, wmpre, wmpost = rd.take(D), rd.take(D), rd.take(D), rd.take(D)
        subln = rd.take(P)
        cqg, ckvg = rd.take(QR), rd.take(KVR)
        dlam = rd.take(4, HD)
        bias = rd.take(8, T, S)
        causal = rd.take(T, S)
        qk4 = Region(arena, rd.at)
        dqT, dkT, mqT, mkT = (rd.take(4, S) for _ in range(4))
        qmT, kmT = qk4.take(LH, S), qk4.take(LH, S)
        dv, mv = rd.take(T, 512), rd.take(T, 512)
        cc = rd.take(T, 416)
        g_at = rd.at
        gates = rd.take(T, NB * D)
        uT_at = g_at
        q_at = rd.at
        qn = rd.take(T, LH * LQ)
        kv = rd.take(T, LH * 128)
        kf = rd.take(T, LH * LQ)
        brT = Region(arena, q_at).take(12, S)
        uT = Region(arena, uT_at).take(FF // P, S)
        ob = rd.take(T, NB * BW)
        smb = rd.take(2, 4, S)
        pTb = rd.take(2, 4, 2, P)
        bt = rd.take(T, 512)
        bt2 = rd.take(T, 256)
        cqT, ckvT = rd.take(2, S), rd.take(S)
        assert rd.at <= ARENA, rd.at
        skewed = Region(arena, q_at).take(8, T, S)
        flip = Region(arena, g_at).take(P)
        onehot = Region(arena, g_at + 128).take(512)
        relb = Region(arena, g_at + 640).take(8)
        t5row = Region(arena, g_at + 704).take(512)
        t5_dram = nc.dram_tensor("t5_rows", [8, 512], F32).ap()

        def qpair(t, j):
            return z[:, t, j * P:j * P + P]

        def acc_nat(b, n=512):
            return acc[:, b].rearrange("p (t x) s -> p t (x s)", t=2)[:, :, 0:n]

        def t5_bank(h):
            return acc[:, h % 2, 0:2].rearrange("p x s -> p (x s)")

        def turn_blocks(b):
            return turn_ps[:, b].rearrange("p (k s) -> p k s", k=2)

        def group(block, g):
            if block == "a":
                return dict(q=lambda hh, t: qT[64 * hh:64 * hh + 64, g, t * P:t * P + P],
                            k=lambda hh: kT[64 * hh:64 * hh + 64, :],
                            v=lambda hh, kt: z[:, kt, 640 + 64 * hh:704 + 64 * hh], dv=64,
                            scale=HD ** -0.5, mask=lambda hh: window)
            if g < 4:
                return dict(q=lambda hh, t: dqT[64 * hh:64 * hh + 64, g, t * P:t * P + P],
                            k=lambda hh: dkT[64 * hh:64 * hh + 64, g, :],
                            v=lambda hh, kt: dv[:, kt, g * P:g * P + P], dv=128,
                            scale=HD ** -0.5, mask=lambda hh: bias[:, g])
            if g < 6:
                h0 = 2 * (g - 4)
                return dict(q=lambda hh, t: mqT[:, h0 + hh, t * P:t * P + P],
                            k=lambda hh: mkT[:, h0 + hh, :],
                            v=lambda hh, kt: mv[:, kt, (h0 + hh) * P:(h0 + hh) * P + P], dv=128,
                            scale=128 ** -0.5, mask=lambda hh: bias[:, DH + h0 + hh])
            h0 = 2 * (g - 6)
            return dict(q=lambda hh, t: qmT[0:LQ, h0 + hh, t * P:t * P + P],
                        k=lambda hh: kmT[0:LQ, h0 + hh, :],
                        v=lambda hh, kt: kv[:, kt, (h0 + hh) * 128 + NOPE:(h0 + hh) * 128 + 128], dv=64,
                        scale=LQ ** -0.5, mask=lambda hh: causal)

        def sm_of(block):
            return sm if block == "a" else smb

        def pT_of(block):
            return pT if block == "a" else pTb

        def slab_at(name, block):
            return slab[:, slabs.buf(block, name), :]

        def wait_slab_free(sp, block, l, i):
            names = SLABS[block]
            if i >= 2:
                lay, prev, blk = l, names[i - 2], block
            elif block == "a":
                return
            else:
                return
            if prev.startswith("dn") and prev not in SLAB_ENDS[blk]:
                sp.wait_ge(*down_used.at(blk, lay, int(prev[2:]) + 1))
            else:
                sp.wait_ge(*accs.full_at(blk, lay, SLAB_ENDS[blk].get(prev, prev)))
            sp.sem_inc(passed["sp"], 1)

        def load_halves(sp, block, name, halves):
            for dst, src in halves:
                sp.dma_start(dst, src).then_inc(slabs.full_sem(block, name), 16)

        def columns(block, name, w, n0, n):
            dst = slab_at(name, block).rearrange("p (k n) -> p k n", k=KD)[:, :, 0:n]
            src = w.rearrange("(k p) n -> p k n", p=P)[:, :, n0:n0 + n]
            return [(dst[:, 4 * i:4 * i + 4], src[:, 4 * i:4 * i + 4]) for i in range(2)]

        def rows512(block, name, w):
            dst = slab_at(name, block).rearrange("p (k n) -> p k n", k=4)
            src = w.rearrange("(k p) n -> p k n", p=P)
            return [(dst[:, 2 * i:2 * i + 2], src[:, 2 * i:2 * i + 2]) for i in range(2)]

        def slabs_a(sp, l):
            for i, name in enumerate(SLABS["a"]):
                wait_slab_free(sp, "a", l, i)
                if name.startswith("ada"):
                    halves = columns("a", name, io["w_ada"][l], 512 * int(name[3:]), 512)
                elif name.startswith("in"):
                    halves = columns("a", name, io["w_in"][l], 512 * int(name[2:]), 256 if name == "in3" else 512)
                elif name.startswith("out"):
                    halves = columns("a", name, io["w_out"][l], 512 * int(name[3:]), 512)
                else:
                    halves = columns("a", name, io["peer_wq"][l], 512 * int(name[2:]), 512)
                load_halves(sp, "a", name, halves)
            u = io["peer_u"][l].rearrange("(n p) d -> n p d", p=P)
            v = io["peer_v"][l].rearrange("(n p) d -> n p d", p=P)
            sp.wait_ge(*accs.full_at("a", l, "wq2"))
            sp.sem_inc(passed["sp"], 1)
            for q in range(PLACES):
                sp.dma_start(expert_u[:, q], u[q]).then_inc(u_in[q].sem, 16)
            sp.wait_ge(*accs.full_at("a", l, "wq3"))
            sp.sem_inc(passed["sp"], 1)
            for q in range(PLACES):
                sp.dma_start(expert_v[:, q], v[q]).then_inc(v_in[q].sem, 16)
            with sp.Fori(0, NKEYS // PLACES - 1) as it:
                for q in range(PLACES):
                    i = it * PLACES + q
                    sp.wait_ge(*ut_full.at("a", l, i + 1))
                    sp.sem_inc(passed["sp"], 1)
                    sp.dma_start(expert_u[:, q], u[i + PLACES]).then_inc(u_in[q].sem, 16)
                    sp.wait_ge(*v_used.at("a", l, i + 1))
                    sp.sem_inc(passed["sp"], 1)
                    sp.dma_start(expert_v[:, q], v[i + PLACES]).then_inc(v_in[q].sem, 16)

        def slabs_b(sp, l):
            w = io["w_in_2"][l]
            cols = {"dq": 0, "dk": 512, "dv": 1024, "mq": 1536, "mk": 2048, "mv": 2560, "misc": 3072}
            for i, name in enumerate(SLABS["b"]):
                wait_slab_free(sp, "b", l, i)
                if name in cols:
                    halves = columns("b", name, w, cols[name], 416 if name == "misc" else 512)
                elif name == "uq":
                    dst = slab_at(name, "b")[:, 0:2 * 768].rearrange("p (k n) -> p k n", k=2)
                    src = io["mla_w_uq_2"][l].rearrange("(k p) n -> p k n", p=P)
                    halves = [(dst[:, k], src[:, k]) for k in range(2)]
                elif name == "ukv":
                    dst = slab_at(name, "b")
                    src = io["mla_w_ukv_2"][l]
                    halves = [(dst[:, 512 * k:512 * k + 512], src[:, 512 * k:512 * k + 512]) for k in range(2)]
                elif name.startswith("g"):
                    halves = columns("b", name, w, 3488 + 512 * int(name[1:]), 512)
                elif name.startswith("br"):
                    halves = rows512("b", name, io["w_branch_2"][l][int(name[2:])])
                elif name.startswith("wo"):
                    halves = columns("b", name, io["w_out_2"][l], 512 * int(name[2:]), 512)
                elif name.startswith("up"):
                    halves = columns("b", name, io["w_up_2"][l], 512 * int(name[2:]), 512)
                else:
                    j = int(name[2:])
                    halves = rows512("b", name, io["w_down_2"][l][512 * j:512 * j + 512, :])
                load_halves(sp, "b", name, halves)

        block_ = ctx.enter_context(nc.Block())

        @block_.sync
        def _(sp):
            sp.dma_start(x[:], io["x"][0].rearrange("(t p) d -> p t d", p=P)).then_inc(x_in, 16)
            with sp.Fori(0, DEPTH) as l:
                slabs_a(sp, l)
                sp.wait_ge(*v_used.at("a", l, NKEYS))
                sp.sem_inc(passed["sp"], 1)
            with sp.Fori(0, DEPTH) as l:
                slabs_b(sp, l)
                sp.wait_ge(*accs.full_at("b", l, "dn0"))
                sp.wait_ge(*accs.full_at("b", l, "dn1"))
                sp.sem_inc(passed["sp"], 1)
            sp.wait_ge(*layer_done.at("b", DEPTH - 1, 1))
            sp.dma_start(out[0].rearrange("(t p) d -> p t d", p=P), x[:]).then_inc(stored, 16)
            sp.wait_ge(stored, 16)

        @block_.tensor
        def _(pe):
            def matmul_nat(dst, lhs, w, name, block, k_of, n, ks=KD, t_only=T, start=True, stop=True):
                for t in range(t_only):
                    for k in range(ks):
                        ins = pe.matmul(dst[:, t, 0:n], lhs[:, k, t * P:t * P + P], w(k),
                                        start=start and k == 0, stop=stop and k == ks - 1)
                return ins

            def w8(block, name):
                v = slab_at(name, block).rearrange("p (k n) -> p k n", k=KD)
                return lambda k, a=0, n=512: v[:, k, a:a + n]

            def gemm_nat(block, l, use, name=None, a=0, n=512, lhs=None):
                name = name or use
                w = w8(block, name)
                pe.wait_ge(*slabs.full_at(block, l, name))
                pe.wait_ge(*accs.free_at(block, l, use))
                dst = acc_nat(accs.buf(block, use))
                matmul_nat(dst, hT if lhs is None else lhs, lambda k: w(k, a, n), name, block, None, n)\
                    .then_inc(accs.full_sem(block, use), 1)

            def columns_T(dst, w, lhs, a):
                for k in range(KD):
                    ins = pe.matmul(dst, w(k, a, P), lhs[:, k, :], start=(k == 0), stop=(k == KD - 1))
                return ins

            def gemm_T(block, l, use):
                w = w8(block, use)
                pe.wait_ge(*slabs.full_at(block, l, use))
                pe.wait_ge(*accs.free_at(block, l, use))
                for j in range(4):
                    ins = columns_T(acc[:, accs.buf(block, use), j, :], w, hT, j * P)
                ins.then_inc(accs.full_sem(block, use), 1)

            def turn(block, l, use, blocks, rows=P):
                pe.wait_ge(*turns.free_at(block, l, use))
                b = turns.buf(block, use)
                for i, src in enumerate(blocks):
                    ins = pe.transpose(turn_ps[0:rows, b, i * P:i * P + P], src, ident[:])
                ins.then_inc(turns.full_sem(block, use), 1)

            def turn_rows(block, l, prefix, src, chunks=KD):
                for g in range(chunks // 2):
                    turn(block, l, f"{prefix}{g}",
                         [src[:, t, (2 * g + c) * P:(2 * g + c + 1) * P] for c in range(2) for t in range(T)])

            def wait_turned(block, l, *uses):
                for u in uses:
                    pe.wait_ge(*turns.emptied_at(block, l, u))

            def score(block, l, g):
                d = group(block, g)
                use = f"sc{g}"
                pe.wait_ge(*accs.free_at(block, l, use))
                b = accs.buf(block, use)
                for hh in range(2):
                    for t in range(T):
                        ins = pe.matmul(acc[:, b, 2 * hh + t, :], d["q"](hh, t), d["k"](hh), start=True, stop=True)
                ins.then_inc(accs.full_sem(block, use), 1)

            def turn_probs(block, l, g):
                p = sm_of(block)[:, g % 2]
                pe.wait_ge(*p_ready.at(block, l, g + 1))
                for i in range(2):
                    use = f"pt{g}_{i}"
                    pe.wait_ge(*probs.free_at(block, l, use))
                    for u in range(2):
                        for kt in range(2):
                            ins = pe.transpose(prob_ps[:, probs.buf(block, use), (2 * u + kt) * P:(2 * u + kt + 1) * P],
                                               p[:, 2 * i + u, kt * P:kt * P + P], ident[:])
                    ins.then_inc(probs.full_sem(block, use), 1)

            def values(block, l, g):
                d = group(block, g)
                use = f"pv{g}"
                pe.wait_ge(*turns.free_at(block, l, use))
                b = turns.buf(block, use)
                pt = pT_of(block)[:, g % 2]
                for hh in range(2):
                    pe.wait_ge(*probs.emptied_at(block, l, f"pt{g}_{hh}"))
                    for t in range(T):
                        for kt in range(2):
                            u = 2 * hh + t
                            ins = pe.matmul(turn_ps[:, b, u * P:u * P + d["dv"]], pt[:, u, kt, :], d["v"](hh, kt),
                                            start=(kt == 0), stop=(kt == 1))
                ins.then_inc(turns.full_sem(block, use), 1)

            pe.wait_ge(consts_in, 16 * N_CONSTS)
            for r in (accs, turns, probs):
                for f in r.free:
                    pe.sem_inc(f, 1)
            pe.sem_inc(gates_full.sem, 2)
            pe.sem_inc(gates_kept.sem, 2)

            pe.wait_ge(c_ready, 1)
            with pe.Fori(0, DEPTH) as l:
                for i in range(12):
                    use = f"ada{i}"
                    w = w8("a", use)
                    pe.wait_ge(*slabs.full_at("a", l, use))
                    pe.wait_ge(*accs.free_at("a", l, use))
                    for k in range(KD):
                        ins = pe.matmul(acc_nat(accs.buf("a", use))[:, 0, :], cbc[:, k, :], w(k),
                                        start=(k == 0), stop=(k == KD - 1))
                    ins.then_inc(accs.full_sem("a", use), 1)
                pe.wait_ge(*h_ready.at("a", l, 1))
                turn_rows("a", l, "h1_", hn)
                pe.wait_ge(*params.at("a", l, params.per["a"]))
                turn("a", l, "keys", [keys0[:, f, :] for f in range(2)])
                wait_turned("a", l, "h1_2", "h1_3")
                gemm_nat("a", l, "in0")
                w = w8("a", "in1")
                pe.wait_ge(*slabs.full_at("a", l, "in1"))
                pe.wait_ge(*accs.free_at("a", l, "in1"))
                b = accs.buf("a", "in1")
                for t in range(T):
                    for k in range(KD):
                        pe.matmul(acc[:, b, t, :], hT[:, k, t * P:t * P + P], w(k, 0, 256),
                                  start=(k == 0), stop=(k == KD - 1))
                for j in range(2):
                    ins = columns_T(acc[:, b, 2 + j, :], w, hT, 256 + j * P)
                ins.then_inc(accs.full_sem("a", "in1"), 1)
                gemm_T("a", l, "in2")
                pe.wait_ge(*slabs.full_at("a", l, "in3"))
                pe.wait_ge(*accs.free_at("a", l, "in3"))
                w = w8("a", "in3")
                b = accs.buf("a", "in3")
                for t in range(T):
                    for k in range(KD):
                        ins = pe.matmul(acc[:, b, t, :], hT[:, k, t * P:t * P + P], w(k, 0, 256),
                                        start=(k == 0), stop=(k == KD - 1))
                ins.then_inc(accs.full_sem("a", "in3"), 1)
                pe.wait_ge(*accs.emptied_at("a", l, "in3"))
                pe.wait_ge(*accs.free_at("a", l, "pool0"))
                b = accs.buf("a", "pool0")
                for g in range(4):
                    r = 64 * (g % 2)
                    for kt in range(T):
                        ins = pe.matmul(acc[r:r + 64, b, g // 2, :], z[:, kt, 768 + 64 * g:832 + 64 * g],
                                        pool_m[:, kt, g, :], start=(kt == 0), stop=(kt == 1))
                ins.then_inc(accs.full_sem("a", "pool0"), 1)
                pe.wait_ge(*accs.emptied_at("a", l, "pool0"))
                pe.sem_inc(passed["pe"], 1)
                pe.wait_ge(*accs.free_at("a", l, "pool1"))
                pe.sem_inc(passed["pe"], 1)
                b = accs.buf("a", "pool1")
                for g in range(4):
                    r = 64 * (g % 2)
                    ins = pe.matmul(acc[r:r + 64, b, g // 2, :], pool_wt[r:r + 64, g // 2, :],
                                    plT[r:r + 64, g // 2, :], start=True, stop=True)
                ins.then_inc(accs.full_sem("a", "pool1"), 1)
                pe.wait_ge(*qk_ready.at("a", l, 1))
                for n in range(2):
                    turn("a", l, f"q{n}", [qpair(t, 2 * n + c) for c in range(2) for t in range(T)])
                turn("a", l, "k", [z[:, t, 512:640] for t in range(T)])
                wait_turned("a", l, "q0", "q1", "k")
                score("a", l, 0)
                score("a", l, 1)
                for g in range(4):
                    turn_probs("a", l, g)
                    if g + 2 < 4:
                        score("a", l, g + 2)
                    values("a", l, g)
                pe.wait_ge(*mix_ready.at("a", l, 1))
                turn_rows("a", l, "mix", oa, chunks=4)
                wait_turned("a", l, "mix0", "mix1")
                pe.wait_ge(*conv_ready.at("a", l, 1))
                pe.wait_ge(*accs.emptied_at("a", l, "pool1"))
                gemm_nat("a", l, "out0", lhs=mixT)
                gemm_nat("a", l, "out1", lhs=mixT)
                pe.wait_ge(*h_ready.at("a", l, 2))
                turn_rows("a", l, "h2_", hn)
                wait_turned("a", l, "h2_2", "h2_3", "keys")

                def route(c):
                    pe.wait_ge(*accs.emptied_at("a", l, f"wq{c}"))
                    pe.wait_ge(*accs.free_at("a", l, f"s{c}"))
                    b = accs.buf("a", f"s{c}")
                    for t in range(T):
                        for j in range(4):
                            ins = pe.matmul(acc[:, b, 2 * t + j // 2, (j % 2) * P:(j % 2) * P + P],
                                            pqT[:, c % 2, j, t * P:t * P + P], keysT[:, j % 2, :],
                                            start=True, stop=True)
                    ins.then_inc(accs.full_sem("a", f"s{c}"), 1)

                gemm_T("a", l, "wq0")
                gemm_T("a", l, "wq1")
                route(0)
                gemm_T("a", l, "wq2")
                route(1)
                gemm_T("a", l, "wq3")
                route(2)
                route(3)
                pe.wait_ge(*pairs_ready.at("a", l, 1))
                turn("a", l, "pairs0", [pairs[:, i, t, :] for i in range(2) for t in range(T)])
                pe.wait_ge(*pairs_ready.at("a", l, 2))
                turn("a", l, "pairs1", [pairs[:, 2, t, :] for t in range(T)])
                with pe.Fori(0, S // TOKG // 2) as it:
                    for j in range(2):
                        n = it * 2 + j
                        pe.wait_ge(*rows_built.at("a", l, n + 1))
                        pe.wait_ge(*gates_kept.two_before("a", l, n + 1))
                        for q in range(TOKG):
                            ins = pe.matmul(prob_ps[:, j, q * P:q * P + P], rows[:, j, 1, q, :], rows[:, j, 0, q, :],
                                            start=True, stop=True)
                        ins.then_inc(gates_full.sem, 1)
                pe.wait_ge(*gates_kept.at("a", l, S // TOKG))
                pe.wait_ge(*accs.emptied_at("a", l, "s2"))
                pe.wait_ge(*accs.emptied_at("a", l, "s3"))
                wait_turned("a", l, "pairs0", "pairs1")

                def turn_u(i, m):
                    u = expert_u[:, m]
                    pe.wait_ge(*u_in[m].at("a", l, 1 if isinstance(i, int) else loop_var[0] + 2))
                    if not (isinstance(i, int) and i == 0):
                        pe.wait_ge(*ut_act.at("a", l, i))
                        pe.wait_ge(*ut_dve.at("a", l, i))
                    for k in range(KD):
                        ins = pe.transpose(turn_ps[:, k // 4, (k % 4) * P:(k % 4 + 1) * P], u[:, k * P:k * P + P], ident[:])
                    ins.then_inc(ut_full.sem, 1)

                loop_var = [None]

                def activations(i, m):
                    pe.wait_ge(*ut_act.at("a", l, i + 1))
                    pe.wait_ge(*ut_dve.at("a", l, i + 1))
                    if not (isinstance(i, int) and i < 2):
                        pe.wait_ge(*gelu_done.at("a", l, i - 1))
                    for k in range(KD):
                        ins = pe.matmul(prob_ps[:, m % 2, 0:S], utT[:, m % 2, k, :], hT[:, k, :],
                                        start=(k == 0), stop=(k == KD - 1))
                    ins.then_inc(am_full.sem, 1)

                def combine(i, m, rounds, first=False, last=False):
                    v = expert_v[:, m]
                    pe.wait_ge(*v_in[m].at("a", l, rounds + 1))
                    pe.wait_ge(*wt_ready.at("a", l, i + 1))
                    for t in range(T):
                        for n in range(2):
                            ins = pe.matmul(y_ps[:, t, n, :], wt[:, m % 2, t * P:t * P + P], v[:, n * 512:n * 512 + 512],
                                            start=first, stop=last)
                    if last:
                        ins.then_inc(y_full.sem, 1)
                    else:
                        ins.then_inc(v_used.sem, 1)

                turn_u(0, 0)
                turn_u(1, 1)
                activations(0, 0)
                turn_u(2, 2)
                activations(1, 1)
                combine(0, 0, 0, first=True)
                turn_u(3, 3)
                activations(2, 2)
                combine(1, 1, 0)
                with pe.Fori(0, NKEYS // 4 - 1) as it:
                    loop_var[0] = it
                    for j in range(4):
                        i = it * 4 + (3 + j)
                        turn_u(i + 1, (4 + j) % 4)
                        activations(i, (3 + j) % 4)
                        combine(i - 1, (2 + j) % 4, it + (0 if j < 2 else 1))
                activations(NKEYS - 1, 3)
                combine(NKEYS - 2, 2, NKEYS // PLACES - 1)
                combine(NKEYS - 1, 3, NKEYS // PLACES - 1, last=True)
                pe.drain().then_inc(v_used.sem, 1)
                pe.wait_ge(*layer_done.at("a", l, 1))

            pe.wait_ge(t5_in, 64)
            pe.matmul(acc_nat(0)[0:8, 0, :], relb[0:BUCKETS, :], onehot[0:BUCKETS, :], start=True, stop=True)\
                .then_inc(t5_row, 1)
            pe.wait_ge(t5_skew, 16 * 16)
            pe.wait_ge(t5_kept, 1)
            for h in range(8):
                if h >= 2:
                    pe.wait_ge(t5_done, h - 1)
                pe.matmul(t5_bank(h), flip, skewed[:, h].rearrange("p t s -> p (t s)"), start=True, stop=True)\
                    .then_inc(t5_flip, 1)
            pe.wait_ge(t5_done, 8)

            with pe.Fori(0, DEPTH) as l:
                pe.wait_ge(*h_ready.at("b", l, 1))
                turn_rows("b", l, "h_", bn)
                wait_turned("b", l, "h_2", "h_3")
                gemm_T("b", l, "dq")
                gemm_T("b", l, "dk")
                pe.wait_ge(*accs.emptied_at("b", l, "dq"))
                pe.wait_ge(*accs.emptied_at("b", l, "dk"))
                score("b", l, 0)
                gemm_nat("b", l, "dv")
                turn_probs("b", l, 0)
                pe.wait_ge(*accs.emptied_at("b", l, "dv"))
                score("b", l, 1)
                values("b", l, 0)
                gemm_T("b", l, "mq")
                turn_probs("b", l, 1)
                score("b", l, 2)
                values("b", l, 1)
                gemm_T("b", l, "mk")
                turn_probs("b", l, 2)
                score("b", l, 3)
                values("b", l, 2)
                gemm_nat("b", l, "mv")
                turn_probs("b", l, 3)
                pe.wait_ge(*accs.emptied_at("b", l, "mk"))
                score("b", l, 4)
                values("b", l, 3)
                gemm_nat("b", l, "misc0", "misc", 0, 384)
                pe.wait_ge(*accs.emptied_at("b", l, "mv"))
                turn_probs("b", l, 4)
                score("b", l, 5)
                gemm_nat("b", l, "misc1", "misc", 384, 32)
                pe.wait_ge(*qk_ready.at("b", l, 1))
                turn("b", l, "cq", [bt2[:, t, c * P:c * P + P] for c in range(2) for t in range(T)])
                pe.wait_ge(*qk_ready.at("b", l, 2))
                turn("b", l, "ckv", [bt[:, t, 0:P] for t in range(T)])
                values("b", l, 4)
                turn_probs("b", l, 5)
                values("b", l, 5)
                gemm_nat("b", l, "g0")
                wait_turned("b", l, "cq", "ckv")
                pe.wait_ge(*slabs.full_at("b", l, "uq"))
                wq2 = slab_at("uq", "b")[:, 0:2 * 768].rearrange("p (k n) -> p k n", k=2)
                for i, (a, n) in enumerate(((0, 512), (512, 256))):
                    use = f"uq{i}"
                    pe.wait_ge(*accs.free_at("b", l, use))
                    dst = acc_nat(accs.buf("b", use))
                    for t in range(T):
                        for k in range(2):
                            ins = pe.matmul(dst[:, t, 0:n], cqT[:, k, t * P:t * P + P], wq2[:, k, a:a + n],
                                            start=(k == 0), stop=(k == 1))
                    ins.then_inc(accs.full_sem("b", use), 1)
                gemm_nat("b", l, "g1")
                pe.wait_ge(*slabs.full_at("b", l, "ukv"))
                wkv = slab_at("ukv", "b")
                for i in range(2):
                    use = f"ukv{i}"
                    pe.wait_ge(*accs.free_at("b", l, use))
                    dst = acc_nat(accs.buf("b", use))
                    for t in range(T):
                        ins = pe.matmul(dst[:, t, :], ckvT[:, t * P:t * P + P], wkv[:, 512 * i:512 * i + 512],
                                        start=True, stop=True)
                    ins.then_inc(accs.full_sem("b", use), 1)
                gemm_nat("b", l, "g2")
                pe.wait_ge(*qk_ready.at("b", l, 3))
                for i in range(4):
                    turn("b", l, f"qm{i}", [qn[:, t, (2 * i + c) * LQ:(2 * i + c + 1) * LQ] for c in range(2) for t in range(T)],
                         rows=LQ)
                pe.wait_ge(*qk_ready.at("b", l, 4))
                for i in range(4):
                    turn("b", l, f"km{i}", [kf[:, t, (2 * i + c) * LQ:(2 * i + c + 1) * LQ] for c in range(2) for t in range(T)],
                         rows=LQ)
                wait_turned("b", l, "km2", "km3")
                score("b", l, 6)
                gemm_nat("b", l, "g3")
                turn_probs("b", l, 6)
                score("b", l, 7)
                values("b", l, 6)
                gemm_nat("b", l, "g4")
                turn_probs("b", l, 7)
                score("b", l, 8)
                values("b", l, 7)
                gemm_nat("b", l, "g5")
                turn_probs("b", l, 8)
                score("b", l, 9)
                values("b", l, 8)
                turn_probs("b", l, 9)
                values("b", l, 9)
                for c in range(NB):
                    pe.wait_ge(*mix_ready.at("b", l, c + 1))
                    for i in range(2):
                        turn("b", l, f"bt{2 * c + i}", [ob[:, t, c * BW + (2 * i + q) * P:c * BW + (2 * i + q + 1) * P]
                                                       for q in range(2) for t in range(T)])
                for c in range(NB):
                    wait_turned("b", l, f"bt{2 * c}", f"bt{2 * c + 1}")
                    pe.wait_ge(*slabs.full_at("b", l, f"br{c}"))
                    w = slab_at(f"br{c}", "b").rearrange("p (k n) -> p k n", k=4)
                    for n in range(GC):
                        use = f"br{c}_{n}"
                        pe.wait_ge(*accs.free_at("b", l, use))
                        dst = acc_nat(accs.buf("b", use))
                        for t in range(T):
                            for k in range(4):
                                ins = pe.matmul(dst[:, t, :], brT[:, 4 * c + k, t * P:t * P + P],
                                                w[:, k, 512 * n:512 * n + 512], start=(k == 0), stop=(k == 3))
                        ins.then_inc(accs.full_sem("b", use), 1)
                pe.wait_ge(*mix_ready.at("b", l, 4))
                turn_rows("b", l, "mx_", bn)
                wait_turned("b", l, "mx_2", "mx_3")
                gemm_nat("b", l, "wo0")
                gemm_nat("b", l, "wo1")
                pe.wait_ge(*h_ready.at("b", l, 2))
                turn_rows("b", l, "hm_", bn)
                wait_turned("b", l, "hm_2", "hm_3")
                for i in range(8):
                    gemm_T("b", l, f"up{i}")
                pe.wait_ge(*accs.free_at("b", l, "dn0"))
                pe.wait_ge(*accs.free_at("b", l, "dn1"))
                for j in range(8):
                    pe.wait_ge(*slabs.full_at("b", l, f"dn{j}"))
                    pe.wait_ge(*u_ready.at("b", l, j + 1))
                    w = slab_at(f"dn{j}", "b").rearrange("p (k n) -> p k n", k=4)
                    for n in range(GC):
                        dst = acc_nat(accs.buf("b", f"dn{n}"))
                        for t in range(T):
                            for k in range(4):
                                ins = pe.matmul(dst[:, t, :], uT[:, 4 * j + k, t * P:t * P + P],
                                                w[:, k, 512 * n:512 * n + 512],
                                                start=(j == 0 and k == 0), stop=(j == 7 and k == 3))
                        if j == 7:
                            ins.then_inc(accs.full_sem("b", f"dn{n}"), 1)
                    if j < 7:
                        ins.then_inc(down_used.sem, 1)
                pe.drain().then_inc(down_used.sem, 1)

        def keep_turned(eng, block, l, use, dst, rows=P, n=512):
            eng.wait_ge(*turns.full_at(block, l, use))
            src = turn_ps[0:rows, turns.buf(block, use), 0:n]
            if len(dst.shape) == 3:
                src = src.rearrange("p (k s) -> p k s", k=dst.shape[1])
            copy(eng, dst, src).then_inc(turns.free_sem(block, use), 1)

        def copy(eng, dst, src):
            return eng.copy(dst, src) if eng is nc.scalar else eng.tensor_copy(dst, src)

        def keep_probs(eng, block, l, g, i):
            use = f"pt{g}_{i}"
            eng.wait_ge(*probs.full_at(block, l, use))
            dst = pT_of(block)[:, g % 2, 2 * i:2 * i + 2].rearrange("p u k s -> p (u k s)")
            copy(eng, dst, prob_ps[:, probs.buf(block, use), :]).then_inc(probs.free_sem(block, use), 1)

        @block_.scalar
        def _(act):
            act = nc.scalar

            def load(sem, dst, src):
                act.dma_start(dst, src).then_inc(sem, 16)

            def wide(row, n):
                return row.unsqueeze(0).broadcast_to([P, n])

            def keep_acc(block, l, use, *pairs):
                act.wait_ge(*accs.full_at(block, l, use))
                for dst, src in pairs[:-1]:
                    act.copy(dst, src)
                act.copy(*pairs[-1]).then_inc(accs.free_sem(block, use), 1)

            def nat(block, use, n=512):
                return acc_nat(accs.buf(block, use), n)

            def whole(block, use):
                return acc[:, accs.buf(block, use)]

            def exps(block, l, g):
                act.wait_ge(*sm_ready.at(block, l, g + 1))
                s = sm_of(block)
                if block == "a":
                    act.activation(esink[:, g % 2], esink[:, g % 2], ACT.Exp)
                for u in range(4):
                    ins = act.activation(s[:, g % 2, u], s[:, g % 2, u], ACT.Exp, bias=nm[:, g % 2, u:u + 1],
                                         accum_out=den[:, g % 2, u:u + 1])
                ins.then_inc(p_ready.sem, 1)

            load(consts_in, ident[:], io["k_ident"])
            load(consts_in, iota[:], io["k_iota"])
            with nc.allow_non_contiguous_dma(reason="a vector with one element a partition"):
                load(consts_in, posi.bitcast(I32), io["positions"][0].rearrange("(t p) -> p t", p=P))
                load(consts_in, posi2.bitcast(I32), io["positions_2"][0].rearrange("(t p) -> p t", p=P))
                load(consts_in, cT, io["c"][0].rearrange("(k p) -> p k", p=P))
            load(consts_in, freqs, wide(io["k_freqs"], 24))
            load(consts_in, neghalf, wide(io["k_neghalf"], 32))
            act.wait_ge(consts_in, 16 * N_CONSTS)
            act.activation(csg, cT, ACT.Exp, scale=-1.0).then_inc(c_exp, 1)
            act.wait_ge(angle_ready, 1)
            act.activation(sinA.rearrange("p t e -> p (t e)"), redu[:, 0:16], ACT.Sin)
            act.activation(sinB.rearrange("p t e -> p (t e)"), redu[:, 16:48], ACT.Sin)
            act.activation(cosA.rearrange("p t e -> p (t e)"), absr[:, 0:16], ACT.Sin)
            act.activation(cosB.rearrange("p t e -> p (t e)"), absr[:, 16:48], ACT.Sin).then_inc(trig_done, 1)

            with act.Fori(0, DEPTH) as l:
                pr = params.sem
                load(pr, mod.rearrange("p a d -> p (a d)"), wide(io["b_ada"][l], 6 * D))
                load(pr, gain1, wide(io["norm1_g"][l], D))
                load(pr, gain2, wide(io["norm2_g"][l], D))
                load(pr, qg, wide(io["q_norm_g"][l], HD))
                load(pr, kg, wide(io["k_norm_g"][l], HD))
                load(pr, sinks, wide(io["attn_sink"][l], 8))
                with nc.allow_non_contiguous_dma(reason="a vector with one element a partition"):
                    for k in range(3):
                        load(pr, conv_w[:, :, k], io["conv_w"][l][k].rearrange("(c p) -> p c", p=P))
                    load(pr, pool_s, io["pool_scale"][l].rearrange("(c p) -> p c", p=P))
                pw = io["pool_w"][l].rearrange("(a b) c e -> b c a e", b=2)
                for b in range(2):
                    load(pr, pool_wt[64 * b:64 * b + 64], pw[b])
                load(pr, keys0, io["peer_keys"][l].rearrange("f k d -> k f d"))
                load(pr, window, io["k_window"])
                load(pr, pool_m.rearrange("p t g s -> p (t g s)"), io["k_pool"])
                for g in (0, 2):
                    keep_turned(act, "a", l, f"h1_{g}", hT[:, 2 * g:2 * g + 2, :])
                keep_turned(act, "a", l, "keys", keysT.rearrange("p f k -> p (f k)"), n=2 * P)
                keep_acc("a", l, "in0", *((z[:, t, 0:QW].rearrange("p (j hh e) -> p hh j e", hh=2, j=4),
                                           nat("a", "in0")[:, t].rearrange("p (hh j e) -> p hh j e", hh=2, j=4))
                                          for t in range(T)))
                keep_acc("a", l, "in1", (z[:, :, 512:768], whole("a", "in1")[:, 0:2]),
                         (zT[:, 0:2], whole("a", "in1")[:, 2:4]))
                keep_acc("a", l, "in2", (zT[:, 2:6], whole("a", "in2")))
                keep_acc("a", l, "in3", (z[:, :, 768:1024], whole("a", "in3")[:, 0:2]))
                keep_acc("a", l, "pool0", (plT, whole("a", "pool0")[:, 0:2]))
                act.wait_ge(*accs.full_at("a", l, "pool1"))
                for c in range(2):
                    ins = act.activation(mixT[:, 6 + c, :], whole("a", "pool1")[:, c], ACT.Copy, scale=pool_s[:, c:c + 1])
                ins.then_inc(accs.free_sem("a", "pool1"), 1)
                keep_turned(act, "a", l, "q0", qT[:, 0:2])
                keep_turned(act, "a", l, "k", kT, n=S)
                exps("a", l, 0)
                exps("a", l, 1)
                for g in range(4):
                    keep_probs(act, "a", l, g, 0)
                    if g + 2 < 4:
                        act.wait_ge(*turns.full_at("a", l, f"pv{g}"))
                        exps("a", l, g + 2)
                keep_turned(act, "a", l, "mix0", mixT[:, 0:2])
                for g in (0, 2):
                    keep_turned(act, "a", l, f"h2_{g}", hT[:, 2 * g:2 * g + 2, :])

                def wq_kept(c):
                    keep_acc("a", l, f"wq{c}", (pqT[:, c % 2], whole("a", f"wq{c}")))

                def s_kept(c):
                    src = whole("a", f"s{c}").rearrange("p (t x) s -> p t (x s)", t=2)
                    keep_acc("a", l, f"s{c}", (scores[:, :, 4 * c:4 * c + 4].rearrange("p t b k -> p t (b k)"), src))

                wq_kept(0)
                wq_kept(1)
                s_kept(0)
                wq_kept(2)
                s_kept(1)
                wq_kept(3)
                s_kept(2)
                s_kept(3)
                act.wait_ge(*top_ready.at("a", l, 1))
                b2 = pairs[:, 2].rearrange("p t k -> p (t k)")
                act.activation(b2, b2, ACT.Exp).then_inc(top_exp.sem, 1)
                keep_turned(act, "a", l, "pairs0", pairsT[:, 0:2])
                act.wait_ge(*turns.emptied_at("a", l, "pairs1"))
                with act.Fori(0, S // TOKG // 2) as it:
                    for j in range(2):
                        n = it * 2 + j
                        act.wait_ge(*gates_full.at("a", l, n + 1))
                        src = prob_ps[:, j, :].rearrange("p (q e) -> p e q", q=TOKG)
                        act.copy(G[:, :, bass.ds(n * TOKG, TOKG)], src).then_inc(gates_kept.sem, 1)

                def ut_kept(i, m):
                    act.wait_ge(*ut_full.at("a", l, i + 1))
                    act.copy(utT[:, m % 2, 0:4, :].rearrange("p k e -> p (k e)"), turn_ps[:, 0, :]).then_inc(ut_act.sem, 1)

                def gelu(i, m):
                    act.wait_ge(*am_full.at("a", l, i + 1))
                    if not (isinstance(i, int) and i < 2):
                        act.wait_ge(*wt_ready.at("a", l, i - 1))
                    act.activation(ga[:, m % 2, :], prob_ps[:, m % 2, 0:S], ACT.Gelu).then_inc(gelu_done.sem, 1)

                ut_kept(0, 0)
                ut_kept(1, 1)
                gelu(0, 0)
                ut_kept(2, 2)
                gelu(1, 1)
                with act.Fori(0, NKEYS // 4 - 1) as it:
                    for j in range(4):
                        i = it * 4 + j
                        ut_kept(i + 3, (3 + j) % 4)
                        gelu(i + 2, (2 + j) % 4)
                ut_kept(NKEYS - 1, 3)
                gelu(NKEYS - 2, 2)
                gelu(NKEYS - 1, 3)
                act.wait_ge(*layer_done.at("a", l, 1))

            load(t5_in, onehot[0:BUCKETS, :], io["k_onehot"])
            load(t5_in, relb[0:BUCKETS, :], io["rel_bias_2"])
            load(t5_in, flip, io["k_flip"])
            load(t5_in, causal, io["k_causal"])
            act.wait_ge(t5_kept, 1)
            load(t5_out, t5_dram, t5row[0:8, :])
            act.wait_ge(t5_out, 16)
            for h in range(8):
                for t in range(T):
                    load(t5_skew, skewed[:, h, t, :],
                         bass.AP(t5_dram.tensor, h * 512 + (P if t == 0 else 0), [[1, P], [1, S]]))
            act.wait_ge(t5_done, 8)

            with act.Fori(0, DEPTH) as l:
                pr = params.sem
                for dst, name in ((wpre, "norm_mix_pre_2"), (wpost, "norm_mix_post_2"), (wmpre, "norm_mlp_pre_2"),
                                  (wmpost, "norm_mlp_post_2")):
                    load(pr, dst, wide(io[name][l], D))
                load(pr, subln, wide(io["diff_subln_2"][l], P))
                load(pr, cqg, wide(io["mla_q_norm_2"][l], QR))
                load(pr, ckvg, wide(io["mla_kv_norm_2"][l], KVR))
                load(pr, dlam.rearrange("p a e -> p (a e)"), wide(io["diff_lambda_2"][l].rearrange("a e -> (a e)"), 4 * HD))
                load(pr, lamc, wide(io["k_lam"][l], 2))
                act.wait_ge(*lam_dot.at("b", l, 1))
                act.activation(lexp, ldot, ACT.Exp).then_inc(lam_exp.sem, 1)
                for g in (0, 2):
                    keep_turned(act, "b", l, f"h_{g}", hT[:, 2 * g:2 * g + 2, :])

                def gate_kept(i):
                    use = f"g{i}"
                    act.wait_ge(*accs.full_at("b", l, use))
                    act.activation(gates[:, :, 512 * i:512 * i + 512], nat("b", use), ACT.Tanh, scale=0.5)\
                        .then_inc(accs.free_sem("b", use), 1)

                keep_acc("b", l, "dq", (dqT, whole("b", "dq")))
                keep_acc("b", l, "dk", (dkT, whole("b", "dk")))
                exps("b", l, 0)
                keep_acc("b", l, "dv", (dv, nat("b", "dv")))
                keep_probs(act, "b", l, 0, 0)
                exps("b", l, 1)
                keep_acc("b", l, "mq", (mqT, whole("b", "mq")))
                keep_probs(act, "b", l, 1, 0)
                act.wait_ge(*turns.full_at("b", l, "pv0"))
                exps("b", l, 2)
                keep_acc("b", l, "mk", (mkT, whole("b", "mk")))
                keep_probs(act, "b", l, 2, 0)
                exps("b", l, 3)
                keep_acc("b", l, "mv", (mv, nat("b", "mv")))
                keep_probs(act, "b", l, 3, 0)
                exps("b", l, 4)
                keep_acc("b", l, "misc0", (cc[:, :, 0:384], nat("b", "misc0", 384)))
                keep_probs(act, "b", l, 4, 0)
                exps("b", l, 5)
                keep_acc("b", l, "misc1", (cc[:, :, 384:416], nat("b", "misc1", 32)))
                keep_turned(act, "b", l, "cq", cqT)
                keep_probs(act, "b", l, 5, 0)
                gate_kept(0)
                keep_acc("b", l, "uq0", (qn[:, :, 0:512], nat("b", "uq0")))
                keep_acc("b", l, "uq1", (qn[:, :, 512:768], nat("b", "uq1", 256)))
                gate_kept(1)
                keep_acc("b", l, "ukv0", (kv[:, :, 0:512], nat("b", "ukv0")))
                keep_acc("b", l, "ukv1", (kv[:, :, 512:1024], nat("b", "ukv1")))
                gate_kept(2)
                for i in (0, 2):
                    keep_turned(act, "b", l, f"qm{i}", qmT[0:LQ, 2 * i:2 * i + 2], rows=LQ)
                for i in (0, 2):
                    keep_turned(act, "b", l, f"km{i}", kmT[0:LQ, 2 * i:2 * i + 2], rows=LQ)
                exps("b", l, 6)
                gate_kept(3)
                keep_probs(act, "b", l, 6, 0)
                exps("b", l, 7)
                gate_kept(4)
                keep_probs(act, "b", l, 7, 0)
                exps("b", l, 8)
                gate_kept(5)
                keep_probs(act, "b", l, 8, 0)
                exps("b", l, 9)
                keep_probs(act, "b", l, 9, 0)
                for c in range(NB):
                    keep_turned(act, "b", l, f"bt{2 * c}", brT[:, 4 * c:4 * c + 2])
                for g in (0, 2):
                    keep_turned(act, "b", l, f"mx_{g}", hT[:, 2 * g:2 * g + 2, :])
                for n in range(GC):
                    keep_acc("b", l, f"wo{n}", (bn[:, :, 512 * n:512 * n + 512], nat("b", f"wo{n}")))
                for g in (0, 2):
                    keep_turned(act, "b", l, f"hm_{g}", hT[:, 2 * g:2 * g + 2, :])
                for i in range(8):
                    use = f"up{i}"
                    act.wait_ge(*accs.full_at("b", l, use))
                    if i >= 2:
                        act.wait_ge(*u_ready.at("b", l, i - 1))
                    act.activation(smb[:, i % 2], whole("b", use), ACT.Relu).then_inc(accs.free_sem("b", use), 1)
                for n in range(GC):
                    keep_acc("b", l, f"dn{n}", (bn[:, :, 512 * n:512 * n + 512], nat("b", f"dn{n}")))
                act.wait_ge(*layer_done.at("b", l, 1))

        @block_.gpsimd
        def _(pool):
            def inverse_roots(block, l, k, n):
                nc.gpsimd.wait_ge(*var_ready.at(block, l, k))
                nc.gpsimd.tensor_tensor(rstd[:, 0:n], var[:, 0:n], neghalf[:, 0:n], ALU.pow).then_inc(rstd_ready.sem, 1)

            nc.gpsimd.wait_ge(consts_in, 16 * N_CONSTS)
            with nc.gpsimd.Fori(0, DEPTH) as l:
                for k, n in enumerate((T, T * QKH, T)):
                    inverse_roots("a", l, k + 1, n)
            with nc.gpsimd.Fori(0, DEPTH) as l:
                for k, n in enumerate((T, 2 * T, T * DH, T, T, T)):
                    inverse_roots("b", l, k + 1, n)

        @block_.vector
        def _(dve_):
            dve = nc.vector

            def mean_squares(rows, scratch, n, at=0):
                for t in range(T):
                    ins = dve.tensor_tensor_reduce(scratch[:, t], rows[:, t], rows[:, t], 1.0 / n, EPS, ALU.mult,
                                                   ALU.add, var[:, at + t:at + t + 1])
                return ins

            def square_means(sq, rows, heads, n, at=0):
                dve.tensor_tensor(sq, rows, rows, ALU.mult)
                dve.drain()
                dve.tensor_reduce(var[:, at:at + heads].rearrange("p (t h) -> p t h", t=T),
                                  sq.rearrange("p t (h e) -> p t h e", e=n), X, ALU.add)
                dve.drain()
                return dve.tensor_scalar(var[:, at:at + heads], var[:, at:at + heads], 1.0 / n, EPS, ALU.mult, ALU.add)

            def scaled(block, l, k, dst, rows, gain):
                dve.wait_ge(*rstd_ready.at(block, l, k))
                for t in range(T):
                    ins = dve.scalar_tensor_tensor(dst[:, t], rows[:, t], rstd[:, t:t + 1], gain, ALU.mult, ALU.mult)
                return ins

            def modulated(block, l, k, gain, shift):
                mean_squares(x, hn, D).then_inc(var_ready.sem, 1)
                scaled(block, l, k, hn, x, gain)
                dve.drain()
                dve.tensor_tensor(hn[:, :, :], hn[:, :, :], spread(shift, 1, T), ALU.add).then_inc(h_ready.sem, 1)

            def rotate(heads1, heads2, cos, sin, tmp):
                n = heads1.shape[2]
                c, s = spread(cos, 2, n), spread(sin, 2, n)
                dve.tensor_tensor(tmp[0], heads1, c, ALU.mult)
                dve.tensor_tensor(tmp[1], heads2, s, ALU.mult)
                dve.tensor_tensor(tmp[2], heads2, c, ALU.mult)
                dve.tensor_tensor(tmp[3], heads1, s, ALU.mult)
                dve.drain()
                dve.tensor_tensor(heads1, tmp[0], tmp[1], ALU.subtract)
                return dve.tensor_tensor(heads2, tmp[2], tmp[3], ALU.add)

            def masked(block, l, g):
                d, s, use = group(block, g), sm_of(block), f"sc{g}"
                dve.wait_ge(*accs.full_at(block, l, use))
                b = accs.buf(block, use)
                for hh in range(2):
                    ins = dve.scalar_tensor_tensor(s[:, g % 2, 2 * hh:2 * hh + 2].rearrange("p t s -> p (t s)"),
                                                   acc[:, b, 2 * hh:2 * hh + 2].rearrange("p t s -> p (t s)"), d["scale"],
                                                   d["mask"](hh).rearrange("p t s -> p (t s)"), ALU.mult, ALU.add)
                ins.then_inc(accs.free_sem(block, use), 1)
                dve.drain()
                dve.tensor_reduce(mx, s[:, g % 2], X, ALU.max)
                dve.drain()
                if block == "a":
                    sink = spread(sinks.rearrange("p (hh j) -> p j hh", hh=2)[:, g], 2, T)
                    mx2, es2, nm2 = (v.rearrange("p (hh t) -> p hh t", t=T) for v in (mx, esink[:, g % 2], nm[:, g % 2]))
                    dve.tensor_tensor(mx2, mx2, sink, ALU.max)
                    dve.drain()
                    dve.tensor_scalar(nm[:, g % 2], mx, -1.0, None, ALU.mult)
                    dve.drain()
                    dve.tensor_tensor(es2, nm2, sink, ALU.add).then_inc(sm_ready.sem, 1)
                else:
                    dve.tensor_scalar(nm[:, g % 2], mx, -1.0, None, ALU.mult).then_inc(sm_ready.sem, 1)

            def sums(block, l, g):
                dve.wait_ge(*p_ready.at(block, l, g + 1))
                if block == "a":
                    dve.tensor_tensor(den[:, g % 2], den[:, g % 2], esink[:, g % 2], ALU.add)
                    dve.drain()
                dve.reciprocal(rden[:, g % 2], den[:, g % 2])
                keep_probs(dve, block, l, g, 1)

            def attended(block, l, g):
                use = f"pv{g}"
                dve.wait_ge(*turns.full_at(block, l, use))
                dvw = group(block, g)["dv"]
                src = turn_ps[:, turns.buf(block, use), :].rearrange("p (u e) -> p u e", u=4)[:, :, 0:dvw]
                r = rden[:, g % 2]
                if block == "a":
                    dst = oa.rearrange("p t (hh j e) -> p j hh t e", hh=2, j=4)[:, g]
                elif g < 4:
                    dve.tensor_scalar(rden[:, g % 2, 2:4], rden[:, g % 2, 2:4], neglam, None, ALU.mult)
                    dve.drain()
                    o4 = bt.rearrange("p t (u e) -> p (t u) e", u=4)[:, 0:4]
                    dve.tensor_tensor(o4, src, spread(r, 2, dvw), ALU.mult).then_inc(turns.free_sem(block, use), 1)
                    dve.drain()
                    dve.tensor_tensor(ob[:, :, g * P:g * P + P], o4[:, 0:2], o4[:, 2:4], ALU.add)
                    return
                elif g < 6:
                    dst = ob[:, :, BW:2 * BW].rearrange("p t (h e) -> p h t e", e=dvw)[:, 2 * (g - 4):2 * (g - 4) + 2]
                else:
                    dst = ob[:, :, 2 * BW:3 * BW].rearrange("p t (h e) -> p h t e", e=dvw)[:, 2 * (g - 6):2 * (g - 6) + 2]
                src = src.rearrange("p (hh t) e -> p hh t e", hh=2)
                r = r.rearrange("p (hh t) -> p hh t", hh=2)
                for hh in range(2):
                    ins = dve.tensor_tensor(dst[:, hh], src[:, hh], spread(r[:, hh], 2, dvw), ALU.mult)
                ins.then_inc(turns.free_sem(block, use), 1)

            dve.wait_ge(consts_in, 16 * N_CONSTS)
            dve.wait_ge(c_exp, 1)
            dve.tensor_scalar(csg, csg, 1.0, None, ALU.add)
            dve.tensor_copy(posf[:, :, 0], posi.bitcast(I32))
            dve.tensor_copy(posf[:, :, 1], posi2.bitcast(I32))
            dve.drain()
            dve.reciprocal(csg, csg)
            dve.drain()
            dve.tensor_tensor(cac, cT, csg, ALU.mult)
            for t in range(T):
                dve.tensor_scalar(ang[:, 8 * t:8 * t + 8], freqs[:, 0:8], posf[:, t, 0:1], None, ALU.mult)
                dve.tensor_scalar(ang[:, 16 + 16 * t:32 + 16 * t], freqs[:, 8:24], posf[:, t, 1:2], None, ALU.mult)
            dve.drain()
            dve.tensor_copy(cbc, spread(cac, 2, P)).then_inc(c_ready, 1)
            dve.tensor_scalar(turnsN, ang, 1.0 / (2 * np.pi), None, ALU.mult)
            dve.drain()
            dve.tensor_scalar(turnsN, turnsN, ROUND_MAGIC, None, ALU.add)
            dve.drain()
            dve.tensor_scalar(turnsN, turnsN, ROUND_MAGIC, None, ALU.subtract)
            dve.drain()
            for part in (TWO_PI_HI, TWO_PI_MID, TWO_PI_LO):
                dve.scalar_tensor_tensor(ang, turnsN, -part, ang, ALU.mult, ALU.add)
                dve.drain()
            dve.tensor_scalar(redu, ang, 3.1415925, -3.1415925, ALU.min, ALU.max)
            dve.drain()
            dve.tensor_scalar(absr, redu, -1.0, None, ALU.mult)
            dve.drain()
            dve.tensor_tensor(absr, absr, redu, ALU.min)
            dve.drain()
            dve.tensor_scalar(absr, absr, float(np.pi / 2), None, ALU.add).then_inc(angle_ready, 1)
            dve.wait_ge(trig_done, 1)
            dve.wait_ge(x_in, 16)

            with dve.Fori(0, DEPTH) as l:
                dve.wait_ge(*params.at("a", l, params.per["a"]))
                for i in range(12):
                    use = f"ada{i}"
                    dve.wait_ge(*accs.full_at("a", l, use))
                    m = mod[:, i // 2, (i % 2) * 512:(i % 2) * 512 + 512]
                    dve.tensor_tensor(m, acc_nat(accs.buf("a", use))[:, 0, :], m, ALU.add)\
                        .then_inc(accs.free_sem("a", use), 1)
                dve.drain()
                for gain, sc in ((gain1, mod[:, 1]), (gain2, mod[:, 4])):
                    dve.scalar_tensor_tensor(gain, sc, 1.0, gain, ALU.add, ALU.mult)
                dve.tensor_copy(gate2, mod[:, 5])
                dve.drain()
                modulated("a", l, 1, gain1, mod[:, 0])
                for g in (1, 3):
                    keep_turned(dve, "a", l, f"h1_{g}", hT[:, 2 * g:2 * g + 2, :])
                dve.memset(conv_u[:, :, 0:1], 0.0)
                dve.memset(conv_u[:, :, S + 1:S + 2], 0.0)
                dve.wait_ge(*accs.emptied_at("a", l, "in0"))
                dve.wait_ge(*accs.emptied_at("a", l, "in1"))
                square_means(sq_a, z[:, :, 0:QKH * HD], T * QKH, HD).then_inc(var_ready.sem, 1)
                dve.wait_ge(*rstd_ready.at("a", l, 2))
                heads = z[:, :, 0:QKH * HD].rearrange("p t (h e) -> p t h e", e=HD)
                for t in range(T):
                    dve.tensor_tensor(heads[:, t], heads[:, t], spread(rstd[:, t * QKH:(t + 1) * QKH], 2, HD), ALU.mult)
                dve.drain()
                for t in range(T):
                    dve.tensor_tensor(heads[:, t, 0:8], heads[:, t, 0:8], spread(qg, 1, 8), ALU.mult)
                    dve.tensor_tensor(heads[:, t, 8:10], heads[:, t, 8:10], spread(kg, 1, 2), ALU.mult)
                dve.drain()
                rt = [rope_t[:, i].rearrange("p t (h e) -> p t h e", e=8) for i in range(4)]
                rotate(heads[:, :, :, 0:8], heads[:, :, :, 8:16], cosA, sinA, rt).then_inc(qk_ready.sem, 1)
                keep_turned(dve, "a", l, "q1", qT[:, 2:4])
                dve.wait_ge(*accs.emptied_at("a", l, "in2"))
                dve.tensor_tensor(conv_u[:, :, 1:S + 1], zT[:, 0:2], zT[:, 4:6], ALU.mult)
                dve.drain()
                for c in range(2):
                    dve.tensor_scalar(conv_a[:, c], conv_u[:, c, 0:S], conv_w[:, c, 0:1], None, ALU.mult)
                dve.drain()
                for k in (1, 2):
                    for c in range(2):
                        dve.scalar_tensor_tensor(conv_a[:, c], conv_u[:, c, k:k + S], conv_w[:, c, k:k + 1], conv_a[:, c],
                                                 ALU.mult, ALU.add)
                    dve.drain()
                dve.tensor_tensor(mixT[:, 4:6], conv_a, zT[:, 2:4], ALU.mult).then_inc(conv_ready.sem, 1)
                masked("a", l, 0)
                masked("a", l, 1)
                for g in range(4):
                    sums("a", l, g)
                    if g + 2 < 4:
                        masked("a", l, g + 2)
                    attended("a", l, g)
                dve.drain().then_inc(mix_ready.sem, 1)
                keep_turned(dve, "a", l, "mix1", mixT[:, 2:4])
                for n in range(GC):
                    use, cols = f"out{n}", slice(512 * n, 512 * n + 512)
                    dve.wait_ge(*accs.full_at("a", l, use))
                    dve.tensor_tensor(hn[:, :, cols], acc_nat(accs.buf("a", use)), spread(mod[:, 2, cols], 1, T), ALU.mult)\
                        .then_inc(accs.free_sem("a", use), 1)
                    dve.drain()
                    dve.tensor_tensor(x[:, :, cols], x[:, :, cols], hn[:, :, cols], ALU.add)
                dve.drain()
                modulated("a", l, 3, gain2, mod[:, 3])
                for g in (1, 3):
                    keep_turned(dve, "a", l, f"h2_{g}", hT[:, 2 * g:2 * g + 2, :])

                for c in (2, 3):
                    dve.wait_ge(*accs.emptied_at("a", l, f"s{c}"))
                dve.sem_inc(passed["dve"], 1)

                def best16(rows):
                    for s, v, i in rows:
                        dve.max(v[:, 0:8], s)
                    dve.drain()
                    for s, v, i in rows:
                        dve.max_index(i[:, 0:8], v[:, 0:8], s)
                    dve.drain()
                    for s, v, i in rows:
                        dve.match_replace(s, v[:, 0:8], s, -3.4e38)
                    dve.drain()
                    for s, v, i in rows:
                        dve.max(v[:, 8:16], s)
                    dve.drain()
                    for s, v, i in rows:
                        dve.max_index(i[:, 8:16], v[:, 8:16], s)
                    dve.drain()

                best16([(scores[:, t, b], top_v[:, t, b], top_i.bitcast(U32)[:, t, b]) for t in range(T) for b in range(16)])
                dve.tensor_copy(top_f.rearrange("p t b k -> p (t b k)"), top_i.bitcast(U32).rearrange("p t b k -> p (t b k)"))
                tv = top_v.rearrange("p t (h f) k -> p t h f k", f=2)
                for t in range(T):
                    for h in range(PH):
                        dve.tensor_tensor(cand[:, t, h].rearrange("p (i j) -> p i j", i=PK), spread(tv[:, t, h, 0], 2, PK),
                                          spread(tv[:, t, h, 1], 1, PK), ALU.add)
                dve.drain()
                best16([(cand[:, t, h], best[:, t, h], best_p.bitcast(U32)[:, t, h * PK:(h + 1) * PK])
                        for t in range(T) for h in range(PH)])
                bflat = best.rearrange("p t h k -> p (t h) k")
                gflat = pairs[:, 2].rearrange("p t (h k) -> p (t h) k", k=PK)
                dve.tensor_tensor(gflat, bflat, bflat[:, :, 0:1].broadcast_to([P, T * PH, PK]), ALU.subtract)\
                    .then_inc(top_ready.sem, 1)
                bp = best_p.bitcast(U32)
                bh = best_h.bitcast(U32)
                dve.tensor_scalar(bh[:, 0], bp, 4, None, ALU.logical_shift_right)
                dve.tensor_scalar(bh[:, 1], bp, 15, None, ALU.bitwise_and)
                dve.drain()
                dve.tensor_copy(best_hf.rearrange("p a t k -> p (a t k)"), bh.rearrange("p a t k -> p (a t k)"))
                dve.drain()
                tf = top_f.rearrange("p t (h f) k -> p t h f k", f=2)
                io16 = iota[:, 0:PK]
                for t in range(T):
                    for f in range(2):
                        pf = pick[:, f].rearrange("p (a m) -> p a m", m=PK)
                        dve.tensor_tensor(pf, spread(best_hf[:, f, t], 2, PK), spread(io16, 1, PH * PK), ALU.is_equal)
                    dve.drain()
                    for f in range(2):
                        p4 = pick[:, f].rearrange("p (h k m) -> p h k m", h=PH, k=PK)
                        dve.tensor_tensor(p4, p4, spread(tf[:, t, :, f], 2, PK), ALU.mult)
                    dve.drain()
                    for f in range(2):
                        ins = dve.tensor_reduce(pairs[:, f, t], pick[:, f].rearrange("p (a m) -> p a m", m=PK), X, ALU.add)
                    if t == 0:
                        dve.drain()
                ins.then_inc(pairs_ready.sem, 1)
                dve.wait_ge(*top_exp.at("a", l, 1))
                dve.tensor_reduce(dsum, gflat, X, ALU.add)
                dve.drain()
                dve.reciprocal(dsum, dsum)
                dve.drain()
                dve.tensor_tensor(gflat, gflat, spread(dsum, 2, PK), ALU.mult).then_inc(pairs_ready.sem, 1)
                keep_turned(dve, "a", l, "pairs1", pairsT[:, 2], n=S)
                dve.wait_ge(*turns.emptied_at("a", l, "pairs0"))
                dve.sem_inc(passed["dve"], 1)
                dve.drain()
                with dve.Fori(0, S // TOKG // 2) as it:
                    for j in range(2):
                        n = it * 2 + j
                        dve.wait_ge(*gates_full.two_before("a", l, n + 1))
                        for q in range(TOKG):
                            tok = n * TOKG + q
                            dve.tensor_scalar(rows[:, j, 0, q, :], iota[:], pairsT[:, 0, bass.ds(tok, 1)],
                                              pairsT[:, 2, bass.ds(tok, 1)], ALU.is_equal, ALU.mult)
                            ins = dve.tensor_scalar(rows[:, j, 1, q, :], iota[:], pairsT[:, 1, bass.ds(tok, 1)], None,
                                                    ALU.is_equal)
                        ins.then_inc(rows_built.sem, 1)
                dve.wait_ge(*gates_kept.at("a", l, S // TOKG))

                def ut_kept(i, m):
                    dve.wait_ge(*ut_full.at("a", l, i + 1))
                    dve.tensor_copy(utT[:, m % 2, 4:8, :].rearrange("p k e -> p (k e)"), turn_ps[:, 1, :])\
                        .then_inc(ut_dve.sem, 1)

                def weighted(i, m):
                    dve.wait_ge(*gelu_done.at("a", l, i + 1))
                    row = G[:, i, :] if isinstance(i, int) else G[:, bass.ds(i, 1), :].rearrange("p a s -> p (a s)")
                    dve.tensor_tensor(wt[:, m % 2, :], ga[:, m % 2, :], row, ALU.mult).then_inc(wt_ready.sem, 1)

                ut_kept(0, 0)
                ut_kept(1, 1)
                weighted(0, 0)
                ut_kept(2, 2)
                weighted(1, 1)
                with dve.Fori(0, NKEYS // 4 - 1) as it:
                    for j in range(4):
                        i = it * 4 + j
                        ut_kept(i + 3, (3 + j) % 4)
                        weighted(i + 2, (2 + j) % 4)
                ut_kept(NKEYS - 1, 3)
                weighted(NKEYS - 2, 2)
                weighted(NKEYS - 1, 3)
                dve.wait_ge(*y_full.at("a", l, 1))
                yflat = y_ps.rearrange("p t n s -> p t (n s)")
                dve.tensor_tensor(hn[:, :, :], yflat, spread(gate2, 1, T), ALU.mult)
                dve.drain()
                dve.tensor_tensor(x[:], x[:], hn[:, :, :], ALU.add).then_inc(layer_done.sem, 1)
                dve.drain()

            dve.wait_ge(t5_in, 64)
            dve.wait_ge(t5_row, 1)
            dve.tensor_copy(t5row[0:8, :], acc_nat(0)[0:8, 0, :]).then_inc(t5_kept, 1)
            for h in range(8):
                dve.wait_ge(t5_flip, h + 1)
                dve.tensor_tensor(bias[:, h].rearrange("p t s -> p (t s)"), t5_bank(h),
                                  causal.rearrange("p t s -> p (t s)"), ALU.add).then_inc(t5_done, 1)
            dve.drain()

            with dve.Fori(0, DEPTH) as l:
                dve.wait_ge(*params.at("b", l, params.per["b"]))
                d4 = dlam.rearrange("p (a b) e -> p a b e", a=2)
                prod = bt[:, 0, 0:2 * HD].rearrange("p (a e) -> p a e", a=2)
                dve.tensor_tensor(prod, d4[:, :, 0], d4[:, :, 1], ALU.mult)
                dve.drain()
                dve.tensor_reduce(ldot, prod, X, ALU.add).then_inc(lam_dot.sem, 1)
                dve.tensor_scalar(subln, subln, lamc[:, 1:2], None, ALU.mult)
                mean_squares(x, bn, D).then_inc(var_ready.sem, 1)
                dve.wait_ge(*lam_exp.at("b", l, 1))
                dve.tensor_tensor(neglam, lexp[:, 1:2], lexp[:, 0:1], ALU.subtract)
                dve.drain()
                dve.tensor_tensor(neglam, neglam, lamc[:, 0:1], ALU.subtract)
                scaled("b", l, 1, bn, x, wpre).then_inc(h_ready.sem, 1)
                for g in (1, 3):
                    keep_turned(dve, "b", l, f"h_{g}", hT[:, 2 * g:2 * g + 2, :])
                masked("b", l, 0)
                for g in range(4):
                    sums("b", l, g)
                    masked("b", l, g + 1)
                    attended("b", l, g)
                sums("b", l, 4)
                masked("b", l, 5)
                dve.wait_ge(*accs.emptied_at("b", l, "misc0"))
                mean_squares(cc[:, :, 0:QR], bt2, QR)
                mean_squares(cc[:, :, QR:QR + KVR], bt[:, :, 0:KVR], KVR, at=T).then_inc(var_ready.sem, 1)
                dve.wait_ge(*rstd_ready.at("b", l, 2))
                for t in range(T):
                    ins = dve.scalar_tensor_tensor(bt2[:, t], cc[:, t, 0:QR], rstd[:, t:t + 1], cqg, ALU.mult, ALU.mult)
                ins.then_inc(qk_ready.sem, 1)
                for t in range(T):
                    ins = dve.scalar_tensor_tensor(bt[:, t, 0:KVR], cc[:, t, QR:QR + KVR], rstd[:, T + t:T + t + 1], ckvg,
                                                   ALU.mult, ALU.mult)
                ins.then_inc(qk_ready.sem, 1)
                keep_turned(dve, "b", l, "ckv", ckvT, n=S)
                attended("b", l, 4)
                sums("b", l, 5)
                attended("b", l, 5)
                dve.drain()
                sq3 = bn[:, :, 0:512]
                square_means(sq3, ob[:, :, 0:BW], T * DH, P).then_inc(var_ready.sem, 1)
                dve.wait_ge(*rstd_ready.at("b", l, 3))
                oh = ob[:, :, 0:BW].rearrange("p t (h e) -> p t h e", e=P)
                for t in range(T):
                    dve.tensor_tensor(oh[:, t], oh[:, t], spread(rstd[:, t * DH:(t + 1) * DH], 2, P), ALU.mult)
                dve.drain()
                for t in range(T):
                    ins = dve.tensor_tensor(oh[:, t], oh[:, t], spread(subln, 1, DH), ALU.mult)
                ins.then_inc(mix_ready.sem, 1)
                dve.drain().then_inc(mix_ready.sem, 1)
                dve.wait_ge(*accs.emptied_at("b", l, "uq0"))
                dve.wait_ge(*accs.emptied_at("b", l, "uq1"))
                q4 = qn.rearrange("p t (h e) -> p t h e", e=LQ)
                rt = [bn[:, i // 2, 256 * (i % 2):256 * (i % 2) + 256].rearrange("p (t h e) -> p t h e", t=T, h=LH) for i in range(4)]
                rotate(q4[:, :, :, NOPE:NOPE + 16], q4[:, :, :, NOPE + 16:LQ], cosB, sinB, rt).then_inc(qk_ready.sem, 1)
                dve.wait_ge(*accs.emptied_at("b", l, "misc1"))
                k1 = cc[:, :, 384:400].unsqueeze(2)
                k2 = cc[:, :, 400:416].unsqueeze(2)
                rt = [bn[:, i // 2, 512 + 32 * (i % 2):512 + 32 * (i % 2) + 32].rearrange("p (t h e) -> p t h e", t=T, h=1) for i in range(4)]
                rotate(k1, k2, cosB, sinB, rt)
                dve.wait_ge(*accs.emptied_at("b", l, "ukv0"))
                dve.wait_ge(*accs.emptied_at("b", l, "ukv1"))
                dve.sem_inc(passed["dve"], 1)
                kf4 = kf.rearrange("p t (h e) -> p t h e", e=LQ)
                kv4 = kv.rearrange("p t (h e) -> p t h e", e=128)
                dve.drain()
                for t in range(T):
                    dve.tensor_copy(kf4[:, t, :, 0:NOPE], kv4[:, t, :, 0:NOPE])
                    ins = dve.tensor_copy(kf4[:, t, :, NOPE:LQ], spread(cc[:, t, 384:416], 1, LH))
                ins.then_inc(qk_ready.sem, 1)
                for i in (1, 3):
                    keep_turned(dve, "b", l, f"qm{i}", qmT[0:LQ, 2 * i:2 * i + 2], rows=LQ)
                for i in (1, 3):
                    keep_turned(dve, "b", l, f"km{i}", kmT[0:LQ, 2 * i:2 * i + 2], rows=LQ)
                masked("b", l, 6)
                for g in range(6, 10):
                    sums("b", l, g)
                    if g < 9:
                        masked("b", l, g + 1)
                    attended("b", l, g)
                dve.drain().then_inc(mix_ready.sem, 1)
                for c in range(NB):
                    keep_turned(dve, "b", l, f"bt{2 * c + 1}", brT[:, 4 * c + 2:4 * c + 4])
                for c in range(NB):
                    for n in range(GC):
                        use, cols = f"br{c}_{n}", slice(512 * n, 512 * n + 512)
                        dve.wait_ge(*accs.full_at("b", l, use))
                        if c == 0 and n == 0:
                            dve.wait_ge(*accs.emptied_at("b", l, "g5"))
                        gcol = gates[:, :, c * D + 512 * n:c * D + 512 * n + 512]
                        for t in range(T):
                            ins = dve.scalar_tensor_tensor(bt[:, t], gcol[:, t], 1.0, acc_nat(accs.buf("b", use))[:, t],
                                                           ALU.add, ALU.mult)
                        ins.then_inc(accs.free_sem("b", use), 1)
                        dve.drain()
                        for t in range(T):
                            if c == 0:
                                ins = dve.tensor_scalar(bn[:, t, cols], bt[:, t], 0.5, None, ALU.mult)
                            else:
                                ins = dve.scalar_tensor_tensor(bn[:, t, cols], bt[:, t], 0.5, bn[:, t, cols], ALU.mult, ALU.add)
                        if c == NB - 1 and n == GC - 1:
                            ins.then_inc(mix_ready.sem, 1)
                        dve.drain()

                def add_normed(k, gain):
                    btf = bt.rearrange("p t e -> p (t e)")
                    for t in range(T):
                        dve.tensor_tensor_reduce(btf, bn[:, t], bn[:, t], 1.0 / D, EPS, ALU.mult, ALU.add, var[:, t:t + 1])
                        dve.drain()
                    dve.drain().then_inc(var_ready.sem, 1)
                    dve.wait_ge(*rstd_ready.at("b", l, k))
                    for t in range(T):
                        dve.scalar_tensor_tensor(bn[:, t], bn[:, t], rstd[:, t:t + 1], gain, ALU.mult, ALU.mult)
                    dve.drain()
                    return dve.tensor_tensor(x[:], x[:], bn[:, :, :], ALU.add)

                for g in (1, 3):
                    keep_turned(dve, "b", l, f"mx_{g}", hT[:, 2 * g:2 * g + 2, :])
                dve.wait_ge(*accs.emptied_at("b", l, "wo0"))
                dve.wait_ge(*accs.emptied_at("b", l, "wo1"))
                add_normed(4, wpost)
                dve.drain()
                mean_squares(x, bn, D).then_inc(var_ready.sem, 1)
                scaled("b", l, 5, bn, x, wmpre).then_inc(h_ready.sem, 1)
                for g in (1, 3):
                    keep_turned(dve, "b", l, f"hm_{g}", hT[:, 2 * g:2 * g + 2, :])
                for i in range(8):
                    dve.wait_ge(*accs.emptied_at("b", l, f"up{i}"))
                    dve.tensor_tensor(uT[:, 4 * i:4 * i + 4], smb[:, i % 2], smb[:, i % 2], ALU.mult).then_inc(u_ready.sem, 1)
                dve.wait_ge(*accs.emptied_at("b", l, "dn0"))
                dve.wait_ge(*accs.emptied_at("b", l, "dn1"))
                add_normed(6, wmpost).then_inc(layer_done.sem, 1)
                dve.drain()


def constants():
    tok = np.arange(S)
    rel = tok[:, None] - tok[None, :]

    def tiles(m):
        return np.ascontiguousarray(m.reshape(T, P, S).transpose(1, 0, 2)).astype(np.float32)

    pool = np.zeros((S, 4, S), np.float32)
    for g, w in enumerate((2, 4, 8, 16)):
        for t in range(S):
            lo, hi = max(t - w // 2, 0), min(t + w // 2, S)
            pool[lo:hi, g, t] = 1.0 / (hi - lo)
            pool[t, g, t] -= 1.0
    n = np.arange(S)
    nf = np.maximum(n, 1).astype(np.float32)
    large = 16 + (np.log(nf / np.float32(16)) / np.float32(np.log(64.0)) * np.float32(16)).astype(np.int32)
    bucket = np.where(n < 16, n, np.minimum(large, BUCKETS - 1))
    onehot = np.zeros((BUCKETS, 512), np.float32)
    for r in range(511):
        onehot[bucket[max(255 - r, 0)], r] = 1.0
    lam = [0.8 - 0.6 * np.exp(-0.3 * l) for l in range(DEPTH)]
    return {
        "k_ident": np.eye(P, dtype=np.float32),
        "k_flip": np.ascontiguousarray(np.eye(P, dtype=np.float32)[::-1]),
        "k_iota": np.broadcast_to(np.arange(P, dtype=np.float32), (P, P)).copy(),
        "k_window": tiles(np.where(np.abs(rel) <= 128, 0.0, NEG)),
        "k_causal": tiles(np.where(rel >= 0, 0.0, NEG)),
        "k_pool": np.ascontiguousarray(pool.reshape(T, P, 4 * S).transpose(1, 0, 2)).reshape(P, T * 4 * S),
        "k_onehot": onehot,
        "k_freqs": np.concatenate([500000.0 ** (-np.arange(0, 16, 2) / 16), 10000.0 ** (-np.arange(16) * 2.0 / 32)]).astype(np.float32),
        "k_neghalf": np.full(32, -0.5, np.float32),
        "k_lam": np.array([[v, 1.0 - v] for v in lam], np.float32),
    }


def kernel(**inputs):
    import concourse.bacc as bacc
    from concourse.bass_utils import run_bass_kernel_spmd

    nc = bacc.Bacc("TRN2", target_bir_lowering=False, num_devices=1)
    arrays, io = {}, {}
    for name, a in {**inputs, **constants()}.items():
        a = np.ascontiguousarray(a)
        arrays[f"in_{name}"] = a
        io[name] = nc.dram_tensor(f"in_{name}", a.shape, mybir.dt.from_np(a.dtype), kind="ExternalInput").ap()
    out = nc.dram_tensor("out_x", (1, S, D), F32, kind="ExternalOutput").ap()
    two_blocks(nc, io, out)
    r = run_bass_kernel_spmd(nc, [arrays], core_ids=[0])
    return r.results[0]["out_x"]
```

```python
from contextlib import ExitStack

import numpy as np

import concourse.bass as bass
from concourse import mybir

F32 = mybir.dt.float32
F32R = mybir.dt.float32r
I32 = mybir.dt.int32
U32 = mybir.dt.uint32
ALU = mybir.AluOpType
ACT = mybir.ActivationFunctionType
X = mybir.AxisListType.X

P = 128
D = 1024
S = 256
T = S // P
KD = D // P
DEPTH = 2
EPS = 1e-6
NEG = -1e30

HD = 64
QW, KVW, CW, PW = 512, 128, 256, 256
QKH = (QW + KVW) // HD
PH, PK = 8, 16
NKEYS = 128
PLACES = 2
HALVES = ((0, 0), (0, 1), (1, 0))
TOKG = 4
STEP = 8
POOLQ = 2
DH, MH, LH = 4, 4, 8
NOPE, ROPE2, VD = 64, 32, 64
LQ = NOPE + ROPE2
QR, KVR = 256, 128
FF = 4096
NB = 3
BW = 512
BUCKETS = 32
GC = D // 512

TWO_PI_HI = 6.28125
TWO_PI_MID = 0.0019340515136718750
TWO_PI_LO = 2 * np.pi - TWO_PI_HI - TWO_PI_MID
ARENA = 39424
N_CONSTS = 7
ROUND_MAGIC = 1.5 * 2 ** 23



class Ring:

    def __init__(self, full, free, uses, per_full=1):
        self.full, self.free, self.per_full = full, free, per_full
        self.at, self.per, self.base = {}, {}, {}
        n, base = len(full), 0
        for block, names in uses.items():
            assert len(names) % n == 0, (block, len(names), n)
            self.base[block], self.per[block] = base, len(names) // n
            base += DEPTH * self.per[block]
            for i, name in enumerate(names):
                self.at[block, name] = (i % n, i // n)

    def buf(self, block, name):
        return self.at[block, name][0]

    def count(self, block, l, name):
        return self.base[block] + l * self.per[block] + self.at[block, name][1] + 1

    def free_at(self, block, l, name):
        return self.free[self.buf(block, name)], self.count(block, l, name)

    def full_at(self, block, l, name, more=0):
        return self.full[self.buf(block, name)], (self.count(block, l, name) + more) * self.per_full

    def emptied_at(self, block, l, name):
        return self.free[self.buf(block, name)], self.count(block, l, name) + 1

    def full_sem(self, block, name):
        return self.full[self.buf(block, name)]

    def free_sem(self, block, name):
        return self.free[self.buf(block, name)]


class Signal:

    def __init__(self, sem, a=0, b=0, step=1, primed=0):
        self.sem, self.step, self.primed = sem, step, primed
        self.per = {"a": a, "b": b}
        self.base = {"a": 0, "b": DEPTH * a}

    def at(self, block, l, k):
        return self.sem, (self.base[block] + l * self.per[block] + k) * self.step + self.primed

    def two_before(self, block, l, k):
        return self.sem, self.base[block] + l * self.per[block] + k


class Region:

    def __init__(self, tensor, start=0):
        self.t, self.at = tensor, start

    def take(self, *shape):
        n = int(np.prod(shape))
        v = self.t[:, self.at:self.at + n]
        self.at += n
        if len(shape) == 2:
            v = v.rearrange("p (a b) -> p a b", a=shape[0])
        elif len(shape) == 3:
            v = v.rearrange("p (a b c) -> p a b c", a=shape[0], b=shape[1])
        elif len(shape) == 4:
            v = v.rearrange("p (a b c d) -> p a b c d", a=shape[0], b=shape[1], c=shape[2])
        return v


def spread(ap, axis, n):
    v = ap.unsqueeze(axis)
    shape = list(v.shape)
    shape[axis] = n
    return v.broadcast_to(shape)



SLABS = {
    "a": [f"ada{i}" for i in range(12)] + [f"in{i}" for i in range(4)] + ["out0", "out1"]
         + [f"wq{i}" for i in range(4)],
    "b": ["dq", "dk", "dv", "mq", "mk", "mv", "misc", "g0", "uq", "g1", "ukv", "g2", "g3", "g4", "g5"]
         + [f"br{c}" for c in range(NB)] + ["wo0", "wo1"] + [f"up{i}" for i in range(8)]
         + [f"dn{i}" for i in range(8)],
}
ACCS = {
    "a": [f"ada{i}" for i in range(12)] + [f"in{i}" for i in range(4)] + ["pool0", "pool1"]
         + [f"sc{i}" for i in range(4)] + ["out0", "out1", "wq0", "s0", "wq1", "s1", "wq2", "s2", "wq3", "s3"],
    "b": ["dq", "dk", "sc0", "dv", "sc1", "mq", "sc2", "mk", "sc3", "mv", "sc4", "misc0", "sc5", "misc1",
          "g0", "uq0", "uq1", "g1", "ukv0", "ukv1", "g2", "sc6", "g3", "sc7", "g4", "sc8", "g5", "sc9"]
         + [f"br{c}_{n}" for c in range(NB) for n in range(GC)] + ["wo0", "wo1"]
         + [f"up{i}" for i in range(8)] + ["dn0", "dn1"],
}
TURNS = {
    "a": [f"h1_{i}" for i in range(4)] + ["keys", "q0", "q1", "k"] + [f"pv{g}" for g in range(4)]
         + ["mix0", "mix1"] + [f"h2_{i}" for i in range(4)] + ["pairs0", "pairs1"],
    "b": [f"h_{i}" for i in range(4)] + [f"pv{g}" for g in range(4)] + ["cq", "ckv", "pv4", "pv5"]
         + [f"qm{i}" for i in range(4)] + [f"km{i}" for i in range(4)] + [f"pv{g}" for g in range(6, 10)]
         + [f"bt{i}" for i in range(6)] + [f"mx_{i}" for i in range(4)] + [f"hm_{i}" for i in range(4)],
}
MLP = SLABS["b"][-16:]
PROBS = {
    "a": [f"pt{g}_{i}" for g in range(4) for i in range(2)],
    "b": [f"pt{g}_{i}" for g in range(10) for i in range(2)],
}
SLAB_ENDS = {
    "a": {},
    "b": {"misc": "misc1", "uq": "uq1", "ukv": "ukv1", "br0": "br0_1", "br1": "br1_1", "br2": "br2_1", "dn7": "dn1"},
}


def two_blocks(nc, io, out):
    ctx = ExitStack()
    with ctx:
        def sem(name):
            return ctx.enter_context(nc.semaphore(name))

        def sb(name, shape, dt=F32):
            return ctx.enter_context(nc.sbuf_tensor(name, shape, dt))

        acc = ctx.enter_context(nc.psum_tensor("acc", [P, 2, 4, S], F32))
        prob_ps = ctx.enter_context(nc.psum_tensor("prob_ps", [P, 2, 512], F32))
        turn_ps = ctx.enter_context(nc.psum_tensor("turn_ps", [P, 2, 512], F32))
        y_ps = acc[:].rearrange("p b (n x) s -> p b n (x s)", n=2)

        slabs = Ring([sem("slab_full0"), sem("slab_full1")], [None, None], SLABS, per_full=32)
        accs = Ring([sem("acc_full0"), sem("acc_full1")], [sem("acc_free0"), sem("acc_free1")], ACCS)
        turns = Ring([sem("turn_full0"), sem("turn_full1")], [sem("turn_free0"), sem("turn_free1")], TURNS)
        probs = Ring([sem("prob_full0"), sem("prob_full1")], [sem("prob_free0"), sem("prob_free1")], PROBS)
        consts_in = sem("consts_in")
        x_in = sem("x_in")
        c_ready = Signal(sem("c_ready"), a=1)
        htr_hi = Signal(sem("htr_hi"), a=1)
        htr_lo = Signal(sem("htr_lo"), a=1)
        v_hi = Signal(sem("v_hi"), a=NKEYS)
        v_lo = Signal(sem("v_lo"), a=NKEYS)
        c_exp = sem("c_exp")
        angle_ready = sem("angle_ready")
        trig_done = sem("trig_done")
        half_ready = sem("half_ready")
        params = Signal(sem("params"), a=14, b=8, step=16)
        mod_bias = Signal(sem("mod_bias"), a=1, step=16)
        pre_gain = Signal(sem("pre_gain"), b=1, step=16)
        var_ready = Signal(sem("var_ready"), a=3, b=6)
        rstd_ready = Signal(sem("rstd_ready"), a=3, b=6)
        h_ready = Signal(sem("h_ready"), a=2, b=2)
        qk_ready = Signal(sem("qk_ready"), a=1, b=4)
        sm_ready = Signal(sem("sm_ready"), a=4, b=10)
        p_ready = Signal(sem("p_ready"), a=4, b=10)
        sink_ready = Signal(sem("sink_ready"), a=4, b=0)
        sink_exp = Signal(sem("sink_exp"), a=4, b=0)
        conv_ready = Signal(sem("conv_ready"), a=1, b=0)
        mix_ready = Signal(sem("mix_ready"), a=1, b=4)
        top_ready = Signal(sem("top_ready"), a=1)
        top_exp = Signal(sem("top_exp"), a=1)
        pairs_ready = Signal(sem("pairs_ready"), a=2)
        gated_rows = Signal(sem("gated_rows"), a=S // TOKG)
        plain_rows = Signal(sem("plain_rows"), a=S // TOKG)
        gates_full = Signal(sem("gates_full"), a=S // TOKG, primed=2)
        gates_kept = Signal(sem("gates_kept"), a=S // TOKG, primed=2)
        ut_full = Signal(sem("ut_full"), a=NKEYS)
        ut_act = Signal(sem("ut_act"), a=NKEYS)
        ut_dve = Signal(sem("ut_dve"), a=NKEYS)
        am_full = Signal(sem("am_full"), a=NKEYS)
        gelu_done = Signal(sem("gelu_done"), a=NKEYS)
        wt_ready = Signal(sem("wt_ready"), a=NKEYS)
        v_used = Signal(sem("v_used"), a=NKEYS)
        u_in = [Signal(sem(f"u_in{q}"), a=NKEYS // PLACES, step=16) for q in range(PLACES)]
        v_in = [Signal(sem(f"v_in{q}"), a=NKEYS // PLACES, step=16) for q in range(PLACES)]
        y_full = Signal(sem("y_full"), a=1)
        layer_done = Signal(sem("layer_done"), a=1, b=1)
        down_used = Signal(sem("down_used"), b=8)
        lam_dot = Signal(sem("lam_dot"), b=1)
        lam_exp = Signal(sem("lam_exp"), b=1)
        hm_hi = Signal(sem("hm_hi"), b=4)
        mlp_hi = Signal(sem("mlp_hi"), b=32)
        mlp_lo = Signal(sem("mlp_lo"), b=32)
        mlp_half = Signal(sem("mlp_half"), b=15)
        u_ready = Signal(sem("u_ready"), b=8)
        t5_in = sem("t5_in")
        t5_row = sem("t5_row")
        t5_kept = sem("t5_kept")
        t5_out = sem("t5_out")
        t5_skew = sem("t5_skew")
        t5_flip = sem("t5_flip")
        t5_done = sem("t5_done")
        stored = sem("stored")
        passed = {e: sem(f"passed_{e}") for e in ("sp", "pe", "dve", "pool")}

        x = sb("x", [P, T, D])
        ident = sb("ident", [P, P])
        iota = sb("iota", [P, P])
        small = sb("small", [P, 1024])
        with ExitStack() as first:
            arena, slab, hT = (first.enter_context(nc.sbuf_tensor(n, shape, F32)) for n, shape in
                               (("arena", [P, ARENA]), ("slab", [P, 2, 4096]), ("hT", [P, KD, S])))
        with ExitStack() as second:
            def half(name, shape, dt=F32R):
                return second.enter_context(nc.sbuf_tensor(name, shape, dt))

            half("beside_gates", [P, NKEYS * S + D + 2 * S], F32)
            hTr = half("hTr", [P, 2, KD, S])
            wtr = half("wtr", [P, 2, 2, S])
            half("beside_experts", [P, 4096], F32)
            utr = half("utr", [P, 2, 2, D])
            vr = half("vr", [P, 2, D])
        expert_u = slab[:, 0, 0:2 * D].rearrange("p (q d) -> p q d", q=PLACES)
        expert_v = slab[:, 0, 2 * D:4 * D].rearrange("p (q d) -> p q d", q=PLACES)
        sr = Region(small)
        var = sr.take(32)
        rstd = sr.take(32)
        neghalf = sr.take(32)
        cosA, sinA = sr.take(T, 8), sr.take(T, 8)
        cosB, sinB = sr.take(T, 16), sr.take(T, 16)
        den = sr.take(2, 4)
        rden = sr.take(2, 4)
        mx = sr.take(4)
        nm = sr.take(2, 4)
        esink = sr.take(2, 4)
        sinks = sr.take(8)
        dsum = sr.take(16)
        conv_w = sr.take(2, 3)
        pool_s = sr.take(2)
        lamc = sr.take(2)
        ldot = sr.take(2)
        lexp = sr.take(2)
        neglam = sr.take(1)
        cT, csg, cac = sr.take(8), sr.take(8), sr.take(8)
        posi = sr.take(T)
        posf = sr.take(T, 2)
        freqs = sr.take(24)
        ang, turnsN, redu, absr = sr.take(48), sr.take(48), sr.take(48), sr.take(48)
        posi2 = sr.take(T)
        turn_keys = sr.take(3, STEP * TOKG)
        second_keys = sr.take(STEP * TOKG)
        assert sr.at <= 1024

        G = Region(arena).take(NKEYS, S)
        ra = Region(arena)
        mod = ra.take(6, D)
        gain1, gain2 = ra.take(D), ra.take(D)
        hn = ra.take(T, D)
        z = ra.take(T, D)
        zT = ra.take(6, S)
        mixT = ra.take(KD, S)
        sm = ra.take(2, 4, S)
        pT = ra.take(2, 4, 2, P)
        oa = ra.take(T, QW)
        qT = ra.take(4, S)
        kT = ra.take(S)
        plT = ra.take(2, S)
        pool_m = ra.take(T, 4, S)
        pool_wt = ra.take(2, 64)
        window = ra.take(T, S)
        conv_u = ra.take(2, S + 2)
        conv_a = ra.take(2, S)
        sq_a = ra.take(T, QKH * HD)
        rope_t = ra.take(4, T, QKH * 8)
        qg, kg = ra.take(HD), ra.take(HD)
        assert ra.at <= NKEYS * S, ra.at
        rb = Region(arena, 8192 + 2048)
        scores = rb.take(T, 16, NKEYS)
        pqT = rb.take(2, 4, S)
        top_v = rb.take(T, 2 * PH, PK)
        top_i = rb.take(T, 2 * PH, PK)
        top_f = rb.take(T, 2 * PH, PK)
        cand = rb.take(T, PH, PK * PK)
        best = rb.take(T, PH, PK)
        best_p = rb.take(T, PH * PK)
        best_h = rb.take(2, T, PH * PK)
        best_hf = rb.take(2, T, PH * PK)
        pick = rb.take(2 * T, 2 * PK * PK)
        pairs = rb.take(3, T, PH * PK)
        assert rb.at <= NKEYS * S, rb.at
        rc = Region(arena, NKEYS * S)
        gate2 = rc.take(D)
        ga = rc.take(2, S)
        cbc = rc.take(KD, P)
        keys0, keysT = rc.take(2, P), rc.take(2, P)
        rs = Region(slab[:, 1, :])
        rows = rs.take(2, 2, TOKG, P)
        pairsT = rs.take(3, S)
        assert rc.at <= ARENA, rc.at

        rd = Region(arena)
        bn = rd.take(T, D)
        wpre, wpost, wmpre, wmpost = rd.take(D), rd.take(D), rd.take(D), rd.take(D)
        subln = rd.take(P)
        cqg, ckvg = rd.take(QR), rd.take(KVR)
        dlam = rd.take(4, HD)
        bias = rd.take(8, T, S)
        causal = rd.take(T, S)
        qk_at = rd.at
        qk4 = Region(arena, qk_at)
        dqT, dkT, mqT, mkT = (rd.take(4, S) for _ in range(4))
        qmT, kmT = qk4.take(LH, S), qk4.take(LH, S)
        dv, mv = rd.take(T, 512), rd.take(T, 512)
        cc = rd.take(T, 416)
        g_at = rd.at
        gates = rd.take(T, NB * D)
        uT_at = g_at
        q_at = rd.at
        qn = rd.take(T, LH * LQ)
        kv = rd.take(T, LH * 128)
        kf = rd.take(T, LH * LQ)
        brT = Region(arena, q_at).take(12, S)
        ob = rd.take(T, NB * BW)
        smb = rd.take(2, 4, S)
        pTb = rd.take(2, 4, 2, P)
        relu_b = Region(arena, rd.at - 2048).take(2, 4, S)
        hi_at = rd.at
        bt = rd.take(T, 512)
        bt2 = rd.take(T, 256)
        cqT, ckvT = rd.take(2, S), rd.take(S)
        assert rd.at <= ARENA, rd.at
        with ExitStack() as third:
            def place(name, *shape, dt=F32R):
                return third.enter_context(nc.sbuf_tensor(name, [P, *shape], dt))

            place("beside_weights", qk_at, dt=F32)
            w_hi01 = place("w_hi01", 2, 2048)
            hm_hi_r = place("hm_hi_r", KD, S)
            place("beside_tokens", uT_at - qk_at - 6144, dt=F32)
            uTr = place("uTr", 2, FF // P, S)
            place("beside_relu", hi_at - uT_at - 2 * (FF // P) * S, dt=F32)
            w_hi2 = place("w_hi2", 2048)
            place("beside_high", ARENA - hi_at - 2048, dt=F32)
            slab_lo = place("slab_lo", 2, 4096)
            hm_lo_r = place("hm_lo_r", KD, S)
        w_hi = [w_hi01[:, 0], w_hi01[:, 1], w_hi2[:]]
        hm_r = [hm_hi_r, hm_lo_r]
        skewed = Region(arena, q_at).take(8, T, S)
        flip = Region(arena, g_at).take(P)
        onehot = Region(arena, g_at + 128).take(512)
        relb = Region(arena, g_at + 640).take(8)
        t5row = Region(arena, g_at + 704).take(512)
        t5_dram = nc.dram_tensor("t5_rows", [8, 512], F32).ap()

        def qpair(t, j):
            return z[:, t, j * P:j * P + P]

        def acc_nat(b, n=512):
            return acc[:, b].rearrange("p (t x) s -> p t (x s)", t=2)[:, :, 0:n]

        def t5_bank(h):
            return acc[:, h % 2, 0:2].rearrange("p x s -> p (x s)")

        def group(block, g):
            if block == "a":
                return dict(q=lambda hh, t: qT[64 * hh:64 * hh + 64, g, t * P:t * P + P],
                            k=lambda hh: kT[64 * hh:64 * hh + 64, :],
                            v=lambda hh, kt: z[:, kt, 640 + 64 * hh:704 + 64 * hh], dv=64,
                            scale=HD ** -0.5, mask=lambda hh: window)
            if g < 4:
                return dict(q=lambda hh, t: dqT[64 * hh:64 * hh + 64, g, t * P:t * P + P],
                            k=lambda hh: dkT[64 * hh:64 * hh + 64, g, :],
                            v=lambda hh, kt: dv[:, kt, g * P:g * P + P], dv=128,
                            scale=HD ** -0.5, mask=lambda hh: bias[:, g])
            if g < 6:
                h0 = 2 * (g - 4)
                return dict(q=lambda hh, t: mqT[:, h0 + hh, t * P:t * P + P],
                            k=lambda hh: mkT[:, h0 + hh, :],
                            v=lambda hh, kt: mv[:, kt, (h0 + hh) * P:(h0 + hh) * P + P], dv=128,
                            scale=128 ** -0.5, mask=lambda hh: bias[:, DH + h0 + hh])
            h0 = 2 * (g - 6)
            return dict(q=lambda hh, t: qmT[0:LQ, h0 + hh, t * P:t * P + P],
                        k=lambda hh: kmT[0:LQ, h0 + hh, :],
                        v=lambda hh, kt: kv[:, kt, (h0 + hh) * 128 + NOPE:(h0 + hh) * 128 + 128], dv=64,
                        scale=LQ ** -0.5, mask=lambda hh: causal)

        def sm_of(block):
            return sm if block == "a" else smb

        def pT_of(block):
            return pT if block == "a" else pTb

        def slab_at(name, block):
            return slab[:, slabs.buf(block, name), :]

        def wait_slab_free(sp, block, l, i):
            names = SLABS[block]
            if i >= 2:
                lay, prev, blk = l, names[i - 2], block
            elif block == "a":
                return
            else:
                return
            if prev.startswith("dn") and prev not in SLAB_ENDS[blk]:
                sp.wait_ge(*down_used.at(blk, lay, int(prev[2:]) + 1))
            else:
                sp.wait_ge(*accs.full_at(blk, lay, SLAB_ENDS[blk].get(prev, prev)))
            sp.sem_inc(passed["sp"], 1)

        def load_halves(sp, block, name, halves):
            for dst, src in halves:
                sp.dma_start(dst, src).then_inc(slabs.full_sem(block, name), 16)

        def columns(block, name, w, n0, n):
            dst = slab_at(name, block).rearrange("p (k n) -> p k n", k=KD)[:, :, 0:n]
            src = w.rearrange("(k p) n -> p k n", p=P)[:, :, n0:n0 + n]
            return [(dst[:, 4 * i:4 * i + 4], src[:, 4 * i:4 * i + 4]) for i in range(2)]

        def rows512(block, name, w):
            dst = slab_at(name, block).rearrange("p (k n) -> p k n", k=4)
            src = w.rearrange("(k p) n -> p k n", p=P)
            return [(dst[:, 2 * i:2 * i + 2], src[:, 2 * i:2 * i + 2]) for i in range(2)]

        def slabs_a(sp, l):
            for i, name in enumerate(SLABS["a"]):
                wait_slab_free(sp, "a", l, i)
                if name.startswith("ada"):
                    halves = columns("a", name, io["w_ada"][l], 512 * int(name[3:]), 512)
                elif name.startswith("in"):
                    halves = columns("a", name, io["w_in"][l], 512 * int(name[2:]), 256 if name == "in3" else 512)
                elif name.startswith("out"):
                    halves = columns("a", name, io["w_out"][l], 512 * int(name[3:]), 512)
                else:
                    halves = columns("a", name, io["peer_wq"][l], 512 * int(name[2:]), 512)
                load_halves(sp, "a", name, halves)
            u = io["peer_u"][l].rearrange("(n p) d -> n p d", p=P)
            v = io["peer_v"][l].rearrange("(n p) d -> n p d", p=P)
            sp.wait_ge(*accs.full_at("a", l, "wq2"))
            sp.sem_inc(passed["sp"], 1)
            for q in range(PLACES):
                sp.dma_start(expert_u[:, q], u[q]).then_inc(u_in[q].sem, 16)
                sp.dma_start(expert_v[:, q], v[q]).then_inc(v_in[q].sem, 16)

            def next_u(i, q):
                sp.wait_ge(*ut_full.at("a", l, i - 1))
                sp.sem_inc(passed["sp"], 1)
                sp.dma_start(expert_u[:, q], u[i]).then_inc(u_in[q].sem, 16)

            def next_v(i, q):
                sp.wait_ge(*v_lo.at("a", l, i - 1))
                sp.sem_inc(passed["sp"], 1)
                sp.dma_start(expert_v[:, q], v[i]).then_inc(v_in[q].sem, 16)

            next_u(2, 0)
            with sp.Fori(0, NKEYS // 2 - 2) as it:
                for q in range(2):
                    next_u(it * 2 + (3 + q), (3 + q) % 2)
                    next_v(it * 2 + (2 + q), q)
            next_u(NKEYS - 1, 1)
            next_v(NKEYS - 2, 0)
            next_v(NKEYS - 1, 1)

        def mlp_raw(name, where=slab):
            ks = KD if name.startswith("up") else 4
            v = where[:, slabs.buf("b", name), :]
            return lambda h: v[:, 2048 * h:2048 * h + 2048].rearrange("p (k n) -> p k n", k=ks)

        def mlp_source(name, l):
            if name.startswith("up"):
                src, a, n = io["w_up_2"][l], 512 * int(name[2:]), 256
            else:
                src, a, n = io["w_down_2"][l][512 * int(name[2:]):512 * int(name[2:]) + 512, :], 0, 512
            src = src.rearrange("(k p) n -> p k n", p=P)
            return lambda h: src[:, :, a + n * h:a + n * h + n]

        def mlp_high(u):
            return w_hi[u % 3].rearrange("p (k n) -> p k n", k=KD if u < 16 else 4)

        def mlp_operand(u, part):
            return mlp_high(u) if part == 0 else mlp_raw(MLP[u // 2], slab_lo)(u % 2)

        def slabs_b(sp, l):
            w = io["w_in_2"][l]
            cols = {"dq": 0, "dk": 512, "dv": 1024, "mq": 1536, "mk": 2048, "mv": 2560, "misc": 3072}
            for i, name in enumerate(SLABS["b"]):
                if name in MLP[2:]:
                    sp.wait_ge(*mlp_half.at("b", l, MLP.index(name) - 1))
                    sp.sem_inc(passed["sp"], 1)
                else:
                    wait_slab_free(sp, "b", l, i)
                if name in cols:
                    halves = columns("b", name, w, cols[name], 416 if name == "misc" else 512)
                elif name == "uq":
                    dst = slab_at(name, "b")[:, 0:2 * 768].rearrange("p (k n) -> p k n", k=2)
                    src = io["mla_w_uq_2"][l].rearrange("(k p) n -> p k n", p=P)
                    halves = [(dst[:, k], src[:, k]) for k in range(2)]
                elif name == "ukv":
                    dst = slab_at(name, "b")
                    src = io["mla_w_ukv_2"][l]
                    halves = [(dst[:, 512 * k:512 * k + 512], src[:, 512 * k:512 * k + 512]) for k in range(2)]
                elif name.startswith("g"):
                    halves = columns("b", name, w, 3488 + 512 * int(name[1:]), 512)
                elif name.startswith("br"):
                    halves = rows512("b", name, io["w_branch_2"][l][int(name[2:])])
                elif name.startswith("wo"):
                    halves = columns("b", name, io["w_out_2"][l], 512 * int(name[2:]), 512)
                if name[:2] in ("up", "dn"):
                    s = MLP.index(name)
                    dst, src = mlp_raw(name), mlp_source(name, l)
                    sp.dma_start(dst(0), src(0)).then_inc(slabs.full_sem("b", name), 16)
                    if s >= 2:
                        wait_slab_free(sp, "b", l, i)
                    sp.dma_start(dst(1), src(1)).then_inc(slabs.full_sem("b", name), 16)
                else:
                    load_halves(sp, "b", name, halves)

        block_ = ctx.enter_context(nc.Block())

        @block_.sync
        def _(sp):
            sp.dma_start(x[:], io["x"][0].rearrange("(t p) d -> p t d", p=P)).then_inc(x_in, 16)
            with sp.Fori(0, DEPTH) as l:
                slabs_a(sp, l)
                sp.wait_ge(*v_used.at("a", l, NKEYS))
                sp.sem_inc(passed["sp"], 1)
            with sp.Fori(0, DEPTH) as l:
                slabs_b(sp, l)
                sp.wait_ge(*accs.full_at("b", l, "dn0"))
                sp.wait_ge(*accs.full_at("b", l, "dn1"))
                sp.sem_inc(passed["sp"], 1)
            sp.wait_ge(*layer_done.at("b", DEPTH - 1, 1))
            sp.dma_start(out[0].rearrange("(t p) d -> p t d", p=P), x[:]).then_inc(stored, 16)
            sp.wait_ge(stored, 16)

        @block_.tensor
        def _(pe):
            def matmul_nat(dst, lhs, w, n):
                for t in range(T):
                    for k in range(KD):
                        ins = pe.matmul(dst[:, t, 0:n], lhs[:, k, t * P:t * P + P], w(k),
                                        start=(k == 0), stop=(k == KD - 1))
                return ins

            def w8(block, name):
                v = slab_at(name, block).rearrange("p (k n) -> p k n", k=KD)
                return lambda k, a=0, n=512: v[:, k, a:a + n]

            def gemm_nat(block, l, use, name=None, a=0, n=512, lhs=None):
                name = name or use
                w = w8(block, name)
                pe.wait_ge(*slabs.full_at(block, l, name))
                pe.wait_ge(*accs.free_at(block, l, use))
                dst = acc_nat(accs.buf(block, use))
                matmul_nat(dst, hT if lhs is None else lhs, lambda k: w(k, a, n), n)\
                    .then_inc(accs.full_sem(block, use), 1)

            def columns_T(dst, w, lhs, a):
                for k in range(KD):
                    ins = pe.matmul(dst, w(k, a, P), lhs[:, k, :], start=(k == 0), stop=(k == KD - 1))
                return ins

            def gemm_T(block, l, use):
                w = w8(block, use)
                pe.wait_ge(*slabs.full_at(block, l, use))
                pe.wait_ge(*accs.free_at(block, l, use))
                for j in range(4):
                    ins = columns_T(acc[:, accs.buf(block, use), j, :], w, hT, j * P)
                ins.then_inc(accs.full_sem(block, use), 1)

            def turn(block, l, use, blocks, rows=P):
                pe.wait_ge(*turns.free_at(block, l, use))
                b = turns.buf(block, use)
                for i, src in enumerate(blocks):
                    ins = pe.transpose(turn_ps[0:rows, b, i * P:i * P + P], src, ident[:])
                ins.then_inc(turns.full_sem(block, use), 1)

            def turn_rows(block, l, prefix, src, chunks=KD):
                for g in range(chunks // 2):
                    turn(block, l, f"{prefix}{g}",
                         [src[:, t, (2 * g + c) * P:(2 * g + c + 1) * P] for c in range(2) for t in range(T)])

            def wait_turned(block, l, *uses):
                for u in uses:
                    pe.wait_ge(*turns.emptied_at(block, l, u))

            def score(block, l, g):
                d = group(block, g)
                use = f"sc{g}"
                pe.wait_ge(*accs.free_at(block, l, use))
                b = accs.buf(block, use)
                for hh in range(2):
                    for t in range(T):
                        ins = pe.matmul(acc[:, b, 2 * hh + t, :], d["q"](hh, t), d["k"](hh), start=True, stop=True)
                ins.then_inc(accs.full_sem(block, use), 1)

            def turn_probs(block, l, g):
                p = sm_of(block)[:, g % 2]
                pe.wait_ge(*p_ready.at(block, l, g + 1))
                for i in range(2):
                    use = f"pt{g}_{i}"
                    pe.wait_ge(*probs.free_at(block, l, use))
                    for u in range(2):
                        for kt in range(2):
                            ins = pe.transpose(prob_ps[:, probs.buf(block, use), (2 * u + kt) * P:(2 * u + kt + 1) * P],
                                               p[:, 2 * i + u, kt * P:kt * P + P], ident[:])
                    ins.then_inc(probs.full_sem(block, use), 1)

            def values(block, l, g):
                d = group(block, g)
                use = f"pv{g}"
                pe.wait_ge(*turns.free_at(block, l, use))
                b = turns.buf(block, use)
                pt = pT_of(block)[:, g % 2]
                for hh in range(2):
                    pe.wait_ge(*probs.emptied_at(block, l, f"pt{g}_{hh}"))
                    for t in range(T):
                        for kt in range(2):
                            u = 2 * hh + t
                            ins = pe.matmul(turn_ps[:, b, u * P:u * P + d["dv"]], pt[:, u, kt, :], d["v"](hh, kt),
                                            start=(kt == 0), stop=(kt == 1))
                ins.then_inc(turns.full_sem(block, use), 1)

            pe.wait_ge(consts_in, 16 * N_CONSTS)
            for r in (accs, turns, probs):
                for f in r.free:
                    pe.sem_inc(f, 1)
            pe.sem_inc(gates_full.sem, 2)
            pe.sem_inc(gates_kept.sem, 2)

            with pe.Fori(0, DEPTH) as l:
                pe.wait_ge(*c_ready.at("a", l, 1))
                for i in range(12):
                    use = f"ada{i}"
                    w = w8("a", use)
                    pe.wait_ge(*slabs.full_at("a", l, use))
                    pe.wait_ge(*accs.free_at("a", l, use))
                    for k in range(KD):
                        ins = pe.matmul(acc_nat(accs.buf("a", use))[:, 0, :], cbc[:, k, :], w(k),
                                        start=(k == 0), stop=(k == KD - 1))
                    ins.then_inc(accs.full_sem("a", use), 1)
                pe.wait_ge(*h_ready.at("a", l, 1))
                turn_rows("a", l, "h1_", hn)
                pe.wait_ge(*params.at("a", l, params.per["a"]))
                turn("a", l, "keys", [keys0[:, f, :] for f in range(2)])
                wait_turned("a", l, "h1_2", "h1_3")
                gemm_nat("a", l, "in0")
                w = w8("a", "in1")
                pe.wait_ge(*slabs.full_at("a", l, "in1"))
                pe.wait_ge(*accs.free_at("a", l, "in1"))
                b = accs.buf("a", "in1")
                for t in range(T):
                    for k in range(KD):
                        pe.matmul(acc[:, b, t, :], hT[:, k, t * P:t * P + P], w(k, 0, 256),
                                  start=(k == 0), stop=(k == KD - 1))
                for j in range(2):
                    ins = columns_T(acc[:, b, 2 + j, :], w, hT, 256 + j * P)
                ins.then_inc(accs.full_sem("a", "in1"), 1)
                gemm_T("a", l, "in2")
                pe.wait_ge(*slabs.full_at("a", l, "in3"))
                pe.wait_ge(*accs.free_at("a", l, "in3"))
                w = w8("a", "in3")
                b = accs.buf("a", "in3")
                for t in range(T):
                    for k in range(KD):
                        ins = pe.matmul(acc[:, b, t, :], hT[:, k, t * P:t * P + P], w(k, 0, 256),
                                        start=(k == 0), stop=(k == KD - 1))
                ins.then_inc(accs.full_sem("a", "in3"), 1)
                pe.wait_ge(*accs.emptied_at("a", l, "in3"))
                pe.wait_ge(*accs.free_at("a", l, "pool0"))
                b = accs.buf("a", "pool0")
                for g in range(4):
                    r = 64 * (g % 2)
                    for kt in range(T):
                        ins = pe.matmul(acc[r:r + 64, b, g // 2, :], z[:, kt, 768 + 64 * g:832 + 64 * g],
                                        pool_m[:, kt, g, :], start=(kt == 0), stop=(kt == 1))
                ins.then_inc(accs.full_sem("a", "pool0"), 1)
                pe.wait_ge(*accs.emptied_at("a", l, "pool0"))
                pe.sem_inc(passed["pe"], 1)
                pe.wait_ge(*accs.free_at("a", l, "pool1"))
                pe.sem_inc(passed["pe"], 1)
                b = accs.buf("a", "pool1")
                for g in range(4):
                    r = 64 * (g % 2)
                    ins = pe.matmul(acc[r:r + 64, b, g // 2, :], pool_wt[r:r + 64, g // 2, :],
                                    plT[r:r + 64, g // 2, :], start=True, stop=True)
                ins.then_inc(accs.full_sem("a", "pool1"), 1)
                pe.wait_ge(*qk_ready.at("a", l, 1))
                for n in range(2):
                    turn("a", l, f"q{n}", [qpair(t, 2 * n + c) for c in range(2) for t in range(T)])
                turn("a", l, "k", [z[:, t, 512:640] for t in range(T)])
                wait_turned("a", l, "q0", "q1", "k")
                score("a", l, 0)
                score("a", l, 1)
                for g in range(4):
                    turn_probs("a", l, g)
                    if g + 2 < 4:
                        score("a", l, g + 2)
                    values("a", l, g)
                pe.wait_ge(*mix_ready.at("a", l, 1))
                turn_rows("a", l, "mix", oa, chunks=4)
                wait_turned("a", l, "mix0", "mix1")
                pe.wait_ge(*conv_ready.at("a", l, 1))
                pe.wait_ge(*accs.emptied_at("a", l, "pool1"))
                gemm_nat("a", l, "out0", lhs=mixT)
                gemm_nat("a", l, "out1", lhs=mixT)
                pe.wait_ge(*h_ready.at("a", l, 2))
                turn_rows("a", l, "h2_", hn)
                wait_turned("a", l, "h2_2", "h2_3", "keys")

                def route(c):
                    pe.wait_ge(*accs.emptied_at("a", l, f"wq{c}"))
                    pe.wait_ge(*accs.free_at("a", l, f"s{c}"))
                    b = accs.buf("a", f"s{c}")
                    for t in range(T):
                        for j in range(4):
                            ins = pe.matmul(acc[:, b, 2 * t + j // 2, (j % 2) * P:(j % 2) * P + P],
                                            pqT[:, c % 2, j, t * P:t * P + P], keysT[:, j % 2, :],
                                            start=True, stop=True)
                    ins.then_inc(accs.full_sem("a", f"s{c}"), 1)

                for c in range(4):
                    gemm_T("a", l, f"wq{c}")
                    route(c)
                pe.wait_ge(*pairs_ready.at("a", l, 1))
                turn("a", l, "pairs0", [pairs[:, i, t, :] for i in range(2) for t in range(T)])
                pe.wait_ge(*pairs_ready.at("a", l, 2))
                turn("a", l, "pairs1", [pairs[:, 2, t, :] for t in range(T)])
                with pe.Fori(0, S // TOKG // STEP) as it:
                    for j in range(STEP):
                        n = it * STEP + j
                        pe.wait_ge(*gated_rows.at("a", l, n + 1))
                        pe.wait_ge(*plain_rows.at("a", l, n + 1))
                        pe.wait_ge(*gates_kept.two_before("a", l, n + 1))
                        for q in range(TOKG):
                            ins = pe.matmul(prob_ps[:, j % 2, q * P:q * P + P], rows[:, j % 2, 1, q, :], rows[:, j % 2, 0, q, :],
                                            start=True, stop=True)
                        ins.then_inc(gates_full.sem, 1)
                pe.wait_ge(*gates_kept.at("a", l, S // TOKG))
                pe.wait_ge(*accs.emptied_at("a", l, "s3"))
                wait_turned("a", l, "pairs0", "pairs1")

                def turn_u(i, m):
                    u = expert_u[:, m % 2]
                    pe.wait_ge(*u_in[m % 2].at("a", l, i // 2 + 1 if isinstance(i, int) else loop_var[0] * 2 + (3 + m // 2)))
                    if not (isinstance(i, int) and i == 0):
                        pe.wait_ge(*ut_act.at("a", l, i))
                        pe.wait_ge(*ut_dve.at("a", l, i))
                    for k in range(KD):
                        ins = pe.transpose(turn_ps[:, k // 4, (k % 4) * P:(k % 4 + 1) * P], u[:, k * P:k * P + P], ident[:])
                    ins.then_inc(ut_full.sem, 1)

                loop_var = [None]

                def activations(i, m):
                    pe.wait_ge(*ut_act.at("a", l, i + 1))
                    pe.wait_ge(*ut_dve.at("a", l, i + 1))
                    if not (isinstance(i, int) and i < 2):
                        pe.wait_ge(*gelu_done.at("a", l, i - 1))
                    for k in range(KD):
                        for n, (uh, hh) in enumerate(HALVES):
                            ins = pe.matmul(prob_ps[:, m % 2, 0:S], utr[:, m % 2, uh, k * P:k * P + P], hTr[:, hh, k, :],
                                            start=(k == 0 and n == 0), stop=(k == KD - 1 and n == 2))
                    ins.then_inc(am_full.sem, 1)

                def combine(i, m, first=False, last=False):
                    pe.wait_ge(*wt_ready.at("a", l, i + 1))
                    pe.wait_ge(*v_lo.at("a", l, i + 1))
                    for t in range(T):
                        for k, (wh, vh) in enumerate(HALVES):
                            for n in range(2):
                                ins = pe.matmul(y_ps[:, t, n, :], wtr[:, m % 2, wh, t * P:t * P + P],
                                                vr[:, vh, n * 512:n * 512 + 512],
                                                start=first and k == 0, stop=last and k == 2)
                    if last:
                        ins.then_inc(y_full.sem, 1)
                    else:
                        ins.then_inc(v_used.sem, 1)

                pe.wait_ge(*htr_lo.at("a", l, 1))
                turn_u(0, 0)
                turn_u(1, 1)
                activations(0, 0)
                turn_u(2, 2)
                activations(1, 1)
                combine(0, 0, first=True)
                turn_u(3, 3)
                activations(2, 2)
                combine(1, 1)
                with pe.Fori(0, NKEYS // 4 - 1) as it:
                    loop_var[0] = it
                    for j in range(4):
                        i = it * 4 + (3 + j)
                        turn_u(i + 1, (4 + j) % 4)
                        activations(i, (3 + j) % 4)
                        combine(i - 1, (2 + j) % 4)
                activations(NKEYS - 1, 3)
                combine(NKEYS - 2, 2)
                combine(NKEYS - 1, 3, last=True)
                pe.drain().then_inc(v_used.sem, 1)
                pe.wait_ge(*layer_done.at("a", l, 1))

            pe.wait_ge(t5_in, 64)
            pe.matmul(acc_nat(0)[0:8, 0, :], relb[0:BUCKETS, :], onehot[0:BUCKETS, :], start=True, stop=True)\
                .then_inc(t5_row, 1)
            pe.wait_ge(t5_skew, 16 * 16)
            pe.wait_ge(t5_kept, 1)
            for h in range(8):
                if h >= 2:
                    pe.wait_ge(t5_done, h - 1)
                pe.matmul(t5_bank(h), flip, skewed[:, h].rearrange("p t s -> p (t s)"), start=True, stop=True)\
                    .then_inc(t5_flip, 1)
            pe.wait_ge(t5_done, 8)

            with pe.Fori(0, DEPTH) as l:
                pe.wait_ge(*h_ready.at("b", l, 1))
                turn_rows("b", l, "h_", bn)
                wait_turned("b", l, "h_2", "h_3")
                gemm_T("b", l, "dq")
                gemm_T("b", l, "dk")
                pe.wait_ge(*accs.emptied_at("b", l, "dq"))
                pe.wait_ge(*accs.emptied_at("b", l, "dk"))
                score("b", l, 0)
                gemm_nat("b", l, "dv")
                turn_probs("b", l, 0)
                pe.wait_ge(*accs.emptied_at("b", l, "dv"))
                score("b", l, 1)
                values("b", l, 0)
                gemm_T("b", l, "mq")
                turn_probs("b", l, 1)
                score("b", l, 2)
                values("b", l, 1)
                gemm_T("b", l, "mk")
                turn_probs("b", l, 2)
                score("b", l, 3)
                values("b", l, 2)
                gemm_nat("b", l, "mv")
                turn_probs("b", l, 3)
                pe.wait_ge(*accs.emptied_at("b", l, "mk"))
                score("b", l, 4)
                values("b", l, 3)
                gemm_nat("b", l, "misc0", "misc", 0, 384)
                pe.wait_ge(*accs.emptied_at("b", l, "mv"))
                turn_probs("b", l, 4)
                score("b", l, 5)
                gemm_nat("b", l, "misc1", "misc", 384, 32)
                pe.wait_ge(*qk_ready.at("b", l, 1))
                turn("b", l, "cq", [bt2[:, t, c * P:c * P + P] for c in range(2) for t in range(T)])
                pe.wait_ge(*qk_ready.at("b", l, 2))
                turn("b", l, "ckv", [bt[:, t, 0:P] for t in range(T)])
                values("b", l, 4)
                turn_probs("b", l, 5)
                values("b", l, 5)
                gemm_nat("b", l, "g0")
                wait_turned("b", l, "cq", "ckv")
                pe.wait_ge(*slabs.full_at("b", l, "uq"))
                wq2 = slab_at("uq", "b")[:, 0:2 * 768].rearrange("p (k n) -> p k n", k=2)
                for i, (a, n) in enumerate(((0, 512), (512, 256))):
                    use = f"uq{i}"
                    pe.wait_ge(*accs.free_at("b", l, use))
                    dst = acc_nat(accs.buf("b", use))
                    for t in range(T):
                        for k in range(2):
                            ins = pe.matmul(dst[:, t, 0:n], cqT[:, k, t * P:t * P + P], wq2[:, k, a:a + n],
                                            start=(k == 0), stop=(k == 1))
                    ins.then_inc(accs.full_sem("b", use), 1)
                gemm_nat("b", l, "g1")
                pe.wait_ge(*slabs.full_at("b", l, "ukv"))
                wkv = slab_at("ukv", "b")
                for i in range(2):
                    use = f"ukv{i}"
                    pe.wait_ge(*accs.free_at("b", l, use))
                    dst = acc_nat(accs.buf("b", use))
                    for t in range(T):
                        ins = pe.matmul(dst[:, t, :], ckvT[:, t * P:t * P + P], wkv[:, 512 * i:512 * i + 512],
                                        start=True, stop=True)
                    ins.then_inc(accs.full_sem("b", use), 1)
                gemm_nat("b", l, "g2")
                pe.wait_ge(*qk_ready.at("b", l, 3))
                for i in range(4):
                    turn("b", l, f"qm{i}", [qn[:, t, (2 * i + c) * LQ:(2 * i + c + 1) * LQ] for c in range(2) for t in range(T)],
                         rows=LQ)
                pe.wait_ge(*qk_ready.at("b", l, 4))
                for i in range(4):
                    turn("b", l, f"km{i}", [kf[:, t, (2 * i + c) * LQ:(2 * i + c + 1) * LQ] for c in range(2) for t in range(T)],
                         rows=LQ)
                wait_turned("b", l, "km2", "km3")
                score("b", l, 6)
                gemm_nat("b", l, "g3")
                turn_probs("b", l, 6)
                score("b", l, 7)
                values("b", l, 6)
                gemm_nat("b", l, "g4")
                turn_probs("b", l, 7)
                score("b", l, 8)
                values("b", l, 7)
                gemm_nat("b", l, "g5")
                turn_probs("b", l, 8)
                score("b", l, 9)
                values("b", l, 8)
                turn_probs("b", l, 9)
                values("b", l, 9)
                for c in range(NB):
                    pe.wait_ge(*mix_ready.at("b", l, c + 1))
                    for i in range(2):
                        turn("b", l, f"bt{2 * c + i}", [ob[:, t, c * BW + (2 * i + q) * P:c * BW + (2 * i + q + 1) * P]
                                                       for q in range(2) for t in range(T)])
                for c in range(NB):
                    wait_turned("b", l, f"bt{2 * c}", f"bt{2 * c + 1}")
                    pe.wait_ge(*slabs.full_at("b", l, f"br{c}"))
                    w = slab_at(f"br{c}", "b").rearrange("p (k n) -> p k n", k=4)
                    for n in range(GC):
                        use = f"br{c}_{n}"
                        pe.wait_ge(*accs.free_at("b", l, use))
                        dst = acc_nat(accs.buf("b", use))
                        for t in range(T):
                            for k in range(4):
                                ins = pe.matmul(dst[:, t, :], brT[:, 4 * c + k, t * P:t * P + P],
                                                w[:, k, 512 * n:512 * n + 512], start=(k == 0), stop=(k == 3))
                        ins.then_inc(accs.full_sem("b", use), 1)
                pe.wait_ge(*mix_ready.at("b", l, 4))
                turn_rows("b", l, "mx_", bn)
                wait_turned("b", l, "mx_2", "mx_3")
                gemm_nat("b", l, "wo0")
                gemm_nat("b", l, "wo1")
                pe.wait_ge(*h_ready.at("b", l, 2))
                turn_rows("b", l, "hm_", bn)
                wait_turned("b", l, "hm_2", "hm_3")
                for i in range(8):
                    use = f"up{i}"
                    pe.wait_ge(*accs.free_at("b", l, use))
                    for h in range(2):
                        u = 2 * i + h
                        pe.wait_ge(*mlp_lo.at("b", l, u + 1))
                        for j in range(2):
                            for k in range(KD):
                                for n, (wp, hp) in enumerate(HALVES):
                                    ins = pe.matmul(acc[:, accs.buf("b", use), 2 * h + j, :],
                                                    mlp_operand(u, wp)[:, k, j * P:j * P + P], hm_r[hp][:, k, :],
                                                    start=(k == 0 and n == 0), stop=(k == KD - 1 and n == 2))
                        ins.then_inc(*((accs.full_sem("b", use), 1) if h else (mlp_half.sem, 1)))
                pe.wait_ge(*accs.free_at("b", l, "dn0"))
                pe.wait_ge(*accs.free_at("b", l, "dn1"))
                for j in range(8):
                    pe.wait_ge(*u_ready.at("b", l, j + 1))
                    for n in range(GC):
                        u = 16 + 2 * j + n
                        pe.wait_ge(*mlp_lo.at("b", l, u + 1))
                        dst = acc_nat(accs.buf("b", f"dn{n}"))
                        for t in range(T):
                            for k in range(4):
                                for m, (wp, up) in enumerate(HALVES):
                                    ins = pe.matmul(dst[:, t, :], uTr[:, up, 4 * j + k, t * P:t * P + P],
                                                    mlp_operand(u, wp)[:, k, :], start=(j == 0 and k == 0 and m == 0),
                                                    stop=(j == 7 and k == 3 and m == 2))
                        if j == 7:
                            ins.then_inc(accs.full_sem("b", f"dn{n}"), 1)
                        elif n == 0:
                            ins.then_inc(mlp_half.sem, 1)
                        else:
                            ins.then_inc(down_used.sem, 1)
                pe.drain().then_inc(down_used.sem, 1)

        def keep_turned(eng, block, l, use, dst, rows=P, n=512):
            eng.wait_ge(*turns.full_at(block, l, use))
            src = turn_ps[0:rows, turns.buf(block, use), 0:n]
            if len(dst.shape) == 3:
                src = src.rearrange("p (k s) -> p k s", k=dst.shape[1])
            copy(eng, dst, src).then_inc(turns.free_sem(block, use), 1)

        def copy(eng, dst, src):
            return eng.copy(dst, src) if eng is nc.scalar else eng.tensor_copy(dst, src)

        def keep_probs(eng, block, l, g, i):
            use = f"pt{g}_{i}"
            eng.wait_ge(*probs.full_at(block, l, use))
            dst = pT_of(block)[:, g % 2, 2 * i:2 * i + 2].rearrange("p u k s -> p (u k s)")
            copy(eng, dst, prob_ps[:, probs.buf(block, use), :]).then_inc(probs.free_sem(block, use), 1)

        @block_.scalar
        def _(act):
            act = nc.scalar

            def load(sem, dst, src):
                act.dma_start(dst, src).then_inc(sem, 16)

            def wide(row, n):
                return row.unsqueeze(0).broadcast_to([P, n])

            def keep_acc(block, l, use, *pairs):
                act.wait_ge(*accs.full_at(block, l, use))
                for dst, src in pairs[:-1]:
                    act.copy(dst, src)
                act.copy(*pairs[-1]).then_inc(accs.free_sem(block, use), 1)

            def nat(block, use, n=512):
                return acc_nat(accs.buf(block, use), n)

            def whole(block, use):
                return acc[:, accs.buf(block, use)]

            def exps(block, l, g):
                act.wait_ge(*sm_ready.at(block, l, g + 1))
                s = sm_of(block)
                if block == "a":
                    act.activation(esink[:, g % 2], esink[:, g % 2], ACT.Exp)
                for u in range(4):
                    ins = act.activation(s[:, g % 2, u], s[:, g % 2, u], ACT.Exp, bias=nm[:, g % 2, u:u + 1],
                                         accum_out=den[:, g % 2, u:u + 1])
                ins.then_inc(p_ready.sem, 1)

            load(consts_in, ident[:], io["k_ident"])
            load(consts_in, iota[:], io["k_iota"])
            with nc.allow_non_contiguous_dma(reason="a vector with one element a partition"):
                load(consts_in, posi.bitcast(I32), io["positions"][0].rearrange("(t p) -> p t", p=P))
                load(consts_in, posi2.bitcast(I32), io["positions_2"][0].rearrange("(t p) -> p t", p=P))
                load(consts_in, cT, io["c"][0].rearrange("(k p) -> p k", p=P))
            load(consts_in, freqs, wide(io["k_freqs"], 24))
            load(consts_in, neghalf, wide(io["k_neghalf"], 32))
            act.wait_ge(consts_in, 16 * N_CONSTS)
            act.activation(csg, cT, ACT.Exp, scale=-1.0).then_inc(c_exp, 1)
            act.wait_ge(angle_ready, 1)
            act.activation(sinA.rearrange("p t e -> p (t e)"), redu[:, 0:16], ACT.Sin)
            act.activation(sinB.rearrange("p t e -> p (t e)"), redu[:, 16:48], ACT.Sin)
            act.activation(cosA.rearrange("p t e -> p (t e)"), absr[:, 0:16], ACT.Sin)
            act.activation(cosB.rearrange("p t e -> p (t e)"), absr[:, 16:48], ACT.Sin).then_inc(trig_done, 1)

            with act.Fori(0, DEPTH) as l:
                pr = params.sem
                load(mod_bias.sem, mod.rearrange("p a d -> p (a d)"), wide(io["b_ada"][l], 6 * D))
                load(pr, gain1, wide(io["norm1_g"][l], D))
                load(pr, gain2, wide(io["norm2_g"][l], D))
                load(pr, qg, wide(io["q_norm_g"][l], HD))
                load(pr, kg, wide(io["k_norm_g"][l], HD))
                load(pr, sinks, wide(io["attn_sink"][l], 8))
                with nc.allow_non_contiguous_dma(reason="a vector with one element a partition"):
                    for k in range(3):
                        load(pr, conv_w[:, :, k], io["conv_w"][l][k].rearrange("(c p) -> p c", p=P))
                    load(pr, pool_s, io["pool_scale"][l].rearrange("(c p) -> p c", p=P))
                pw = io["pool_w"][l].rearrange("(a b) c e -> b c a e", b=2)
                for b in range(2):
                    load(pr, pool_wt[64 * b:64 * b + 64], pw[b])
                load(pr, keys0, io["peer_keys"][l].rearrange("f k d -> k f d"))
                load(pr, window, io["k_window"])
                load(pr, pool_m.rearrange("p t g s -> p (t g s)"), io["k_pool"])
                for g in (0, 2):
                    keep_turned(act, "a", l, f"h1_{g}", hT[:, 2 * g:2 * g + 2, :])
                keep_turned(act, "a", l, "keys", keysT.rearrange("p f k -> p (f k)"), n=2 * P)
                keep_acc("a", l, "in0", *((z[:, t, 0:QW].rearrange("p (j hh e) -> p hh j e", hh=2, j=4),
                                           nat("a", "in0")[:, t].rearrange("p (hh j e) -> p hh j e", hh=2, j=4))
                                          for t in range(T)))
                keep_acc("a", l, "in1", (z[:, :, 512:768], whole("a", "in1")[:, 0:2]),
                         (zT[:, 0:2], whole("a", "in1")[:, 2:4]))
                keep_acc("a", l, "in2", (zT[:, 2:6], whole("a", "in2")))
                keep_acc("a", l, "in3", (z[:, :, 768:1024], whole("a", "in3")[:, 0:2]))
                keep_acc("a", l, "pool0", (plT, whole("a", "pool0")[:, 0:2]))
                act.wait_ge(*accs.full_at("a", l, "pool1"))
                for c in range(2):
                    ins = act.activation(mixT[:, 6 + c, :], whole("a", "pool1")[:, c], ACT.Copy, scale=pool_s[:, c:c + 1])
                ins.then_inc(accs.free_sem("a", "pool1"), 1)
                keep_turned(act, "a", l, "q0", qT[:, 0:2])
                keep_turned(act, "a", l, "k", kT, n=S)
                exps("a", l, 0)
                exps("a", l, 1)
                for g in range(4):
                    keep_probs(act, "a", l, g, 0)
                    if g + 2 < 4:
                        act.wait_ge(*turns.full_at("a", l, f"pv{g}"))
                        exps("a", l, g + 2)
                keep_turned(act, "a", l, "mix0", mixT[:, 0:2])
                for g in (0, 2):
                    keep_turned(act, "a", l, f"h2_{g}", hT[:, 2 * g:2 * g + 2, :])

                def wq_kept(c):
                    keep_acc("a", l, f"wq{c}", (pqT[:, c % 2], whole("a", f"wq{c}")))

                def s_kept(c):
                    src = whole("a", f"s{c}").rearrange("p (t x) s -> p t (x s)", t=2)
                    keep_acc("a", l, f"s{c}", (scores[:, :, 4 * c:4 * c + 4].rearrange("p t b k -> p t (b k)"), src))

                for c in range(4):
                    wq_kept(c)
                    s_kept(c)
                act.copy(hTr[:, 0], hT[:]).then_inc(htr_hi.sem, 1)
                act.wait_ge(*top_ready.at("a", l, 1))
                b2 = pairs[:, 2].rearrange("p t k -> p (t k)")
                act.activation(b2, b2, ACT.Exp).then_inc(top_exp.sem, 1)
                keep_turned(act, "a", l, "pairs0", pairsT[:, 0:2])
                act.wait_ge(*turns.emptied_at("a", l, "pairs1"))
                with act.Fori(0, S // TOKG // STEP) as it:
                    for j in range(STEP):
                        n = it * STEP + j
                        act.wait_ge(*gates_full.at("a", l, n + 1))
                        src = prob_ps[:, j % 2, :].rearrange("p (q e) -> p e q", q=TOKG)
                        act.copy(G[:, :, bass.ds(n * TOKG, TOKG)], src).then_inc(gates_kept.sem, 1)

                def u_high(i, m):
                    act.wait_ge(*ut_full.at("a", l, i + 1))
                    act.copy(utr[:, m % 2, 0], turn_ps[:].rearrange("p b s -> p (b s)")).then_inc(ut_act.sem, 1)

                def gelu(i, m):
                    act.wait_ge(*am_full.at("a", l, i + 1))
                    if not (isinstance(i, int) and i < 2):
                        act.wait_ge(*wt_ready.at("a", l, i - 1))
                    act.activation(ga[:, m % 2, :], prob_ps[:, m % 2, 0:S], ACT.Gelu).then_inc(gelu_done.sem, 1)

                def v_high(i, m, place):
                    act.wait_ge(*v_in[m % 2].at("a", l, place + 1))
                    if not (isinstance(i, int) and i == 0):
                        act.wait_ge(*v_used.at("a", l, i))
                    act.copy(vr[:, 0], expert_v[:, m % 2]).then_inc(v_hi.sem, 1)

                u_high(0, 0)
                act.wait_ge(*htr_lo.at("a", l, 1))
                for i in range(3):
                    u_high(i + 1, i + 1)
                    gelu(i, i)
                    v_high(i, i, i // 2)
                with act.Fori(0, NKEYS // 4 - 1) as it:
                    for j in range(4):
                        i = it * 4 + (3 + j)
                        u_high(i + 1, j)
                        gelu(i, (3 + j) % 4)
                        v_high(i, (3 + j) % 4, it * 2 + (3 + j) // 2)
                gelu(NKEYS - 1, 3)
                v_high(NKEYS - 1, 3, (NKEYS - 1) // 2)
                act.wait_ge(*layer_done.at("a", l, 1))

            load(t5_in, onehot[0:BUCKETS, :], io["k_onehot"])
            load(t5_in, relb[0:BUCKETS, :], io["rel_bias_2"])
            load(t5_in, flip, io["k_flip"])
            load(t5_in, causal, io["k_causal"])
            act.wait_ge(t5_kept, 1)
            load(t5_out, t5_dram, t5row[0:8, :])
            act.wait_ge(t5_out, 16)
            for h in range(8):
                for t in range(T):
                    load(t5_skew, skewed[:, h, t, :],
                         bass.AP(t5_dram.tensor, h * 512 + (P if t == 0 else 0), [[1, P], [1, S]]))
            act.wait_ge(t5_done, 8)

            with act.Fori(0, DEPTH) as l:
                pr = params.sem
                load(pre_gain.sem, wpre, wide(io["norm_mix_pre_2"][l], D))
                for dst, name in ((wpost, "norm_mix_post_2"), (wmpre, "norm_mlp_pre_2"),
                                  (wmpost, "norm_mlp_post_2")):
                    load(pr, dst, wide(io[name][l], D))
                load(pr, subln, wide(io["diff_subln_2"][l], P))
                load(pr, cqg, wide(io["mla_q_norm_2"][l], QR))
                load(pr, ckvg, wide(io["mla_kv_norm_2"][l], KVR))
                load(pr, dlam.rearrange("p a e -> p (a e)"), wide(io["diff_lambda_2"][l].rearrange("a e -> (a e)"), 4 * HD))
                load(pr, lamc, wide(io["k_lam"][l], 2))
                for g in (0, 2):
                    keep_turned(act, "b", l, f"h_{g}", hT[:, 2 * g:2 * g + 2, :])
                act.wait_ge(*lam_dot.at("b", l, 1))
                act.activation(lexp, ldot, ACT.Exp).then_inc(lam_exp.sem, 1)

                def gate_kept(i):
                    use = f"g{i}"
                    act.wait_ge(*accs.full_at("b", l, use))
                    act.activation(gates[:, :, 512 * i:512 * i + 512], nat("b", use), ACT.Tanh, scale=0.5)\
                        .then_inc(accs.free_sem("b", use), 1)

                keep_acc("b", l, "dq", (dqT, whole("b", "dq")))
                keep_acc("b", l, "dk", (dkT, whole("b", "dk")))
                exps("b", l, 0)
                keep_acc("b", l, "dv", (dv, nat("b", "dv")))
                keep_probs(act, "b", l, 0, 0)
                exps("b", l, 1)
                keep_acc("b", l, "mq", (mqT, whole("b", "mq")))
                keep_probs(act, "b", l, 1, 0)
                act.wait_ge(*turns.full_at("b", l, "pv0"))
                exps("b", l, 2)
                keep_acc("b", l, "mk", (mkT, whole("b", "mk")))
                keep_probs(act, "b", l, 2, 0)
                exps("b", l, 3)
                keep_acc("b", l, "mv", (mv, nat("b", "mv")))
                keep_probs(act, "b", l, 3, 0)
                exps("b", l, 4)
                keep_acc("b", l, "misc0", (cc[:, :, 0:384], nat("b", "misc0", 384)))
                keep_probs(act, "b", l, 4, 0)
                exps("b", l, 5)
                keep_acc("b", l, "misc1", (cc[:, :, 384:416], nat("b", "misc1", 32)))
                keep_turned(act, "b", l, "cq", cqT)
                keep_probs(act, "b", l, 5, 0)
                gate_kept(0)
                keep_acc("b", l, "uq0", (qn[:, :, 0:512], nat("b", "uq0")))
                keep_acc("b", l, "uq1", (qn[:, :, 512:768], nat("b", "uq1", 256)))
                gate_kept(1)
                keep_acc("b", l, "ukv0", (kv[:, :, 0:512], nat("b", "ukv0")))
                keep_acc("b", l, "ukv1", (kv[:, :, 512:1024], nat("b", "ukv1")))
                gate_kept(2)
                for i in (0, 2):
                    keep_turned(act, "b", l, f"qm{i}", qmT[0:LQ, 2 * i:2 * i + 2], rows=LQ)
                for i in (0, 2):
                    keep_turned(act, "b", l, f"km{i}", kmT[0:LQ, 2 * i:2 * i + 2], rows=LQ)
                exps("b", l, 6)
                gate_kept(3)
                keep_probs(act, "b", l, 6, 0)
                exps("b", l, 7)
                gate_kept(4)
                keep_probs(act, "b", l, 7, 0)
                exps("b", l, 8)
                gate_kept(5)
                keep_probs(act, "b", l, 8, 0)
                exps("b", l, 9)
                keep_probs(act, "b", l, 9, 0)
                for c in range(NB):
                    keep_turned(act, "b", l, f"bt{2 * c}", brT[:, 4 * c:4 * c + 2])
                for g in (0, 2):
                    keep_turned(act, "b", l, f"mx_{g}", hT[:, 2 * g:2 * g + 2, :])
                for n in range(GC):
                    keep_acc("b", l, f"wo{n}", (bn[:, :, 512 * n:512 * n + 512], nat("b", f"wo{n}")))

                def slab_high(i):
                    act.wait_ge(*slabs.full_at("b", l, MLP[i]))
                    for u in (2 * i, 2 * i + 1):
                        if u >= 3:
                            before = MLP[(u - 3) // 2]
                            if (u - 3) % 2 == 0:
                                act.wait_ge(*mlp_half.at("b", l, (u - 3) // 2 + 1))
                            elif before.startswith("up"):
                                act.wait_ge(*accs.full_at("b", l, before))
                            else:
                                act.wait_ge(*down_used.at("b", l, int(before[2:]) + 1))
                        act.copy(mlp_high(u), mlp_raw(MLP[i])(u % 2)).then_inc(mlp_hi.sem, 1)

                slab_high(0)
                for g in range(4):
                    act.wait_ge(*turns.full_at("b", l, f"hm_{g}"))
                    act.copy(hm_r[0][:, 2 * g:2 * g + 2].rearrange("p k s -> p (k s)"),
                             turn_ps[:, turns.buf("b", f"hm_{g}"), :]).then_inc(hm_hi.sem, 1)
                for i in range(16):
                    if i < 15:
                        slab_high(i + 1)
                    if i < 8:
                        use = f"up{i}"
                        act.wait_ge(*accs.full_at("b", l, use))
                        if i >= 2:
                            act.wait_ge(*u_ready.at("b", l, i - 1))
                        act.activation(relu_b[:, i % 2], whole("b", use), ACT.Relu).then_inc(accs.free_sem("b", use), 1)
                for n in range(GC):
                    keep_acc("b", l, f"dn{n}", (bn[:, :, 512 * n:512 * n + 512], nat("b", f"dn{n}")))
                act.wait_ge(*layer_done.at("b", l, 1))

        @block_.gpsimd
        def _(pool):
            def inverse_roots(block, l, k, n):
                nc.gpsimd.wait_ge(*var_ready.at(block, l, k))
                nc.gpsimd.tensor_tensor(rstd[:, 0:n], var[:, 0:n], neghalf[:, 0:n], ALU.pow).then_inc(rstd_ready.sem, 1)

            nc.gpsimd.wait_ge(consts_in, 16 * N_CONSTS)
            with nc.gpsimd.Fori(0, DEPTH) as l:
                for k, n in enumerate((T, T * QKH, T)):
                    inverse_roots("a", l, k + 1, n)
                nc.gpsimd.wait_ge(*turns.emptied_at("a", l, "pairs0"))
                nc.gpsimd.sem_inc(passed["pool"], 1)
                with nc.gpsimd.Fori(0, S // TOKG // STEP) as it:
                    nc.gpsimd.tensor_copy(second_keys, pairsT[:, 1, bass.ds(it * (STEP * TOKG), STEP * TOKG)])
                    nc.gpsimd.drain()
                    for j in range(STEP):
                        n = it * STEP + j
                        nc.gpsimd.wait_ge(*gates_full.two_before("a", l, n + 1))
                        nc.gpsimd.sem_inc(passed["pool"], 1)
                        for q in range(POOLQ):
                            tok = j * TOKG + q
                            ins = nc.gpsimd.tensor_scalar(rows[:, j % 2, 1, q, :], iota[:], second_keys[:, tok:tok + 1],
                                                          None, ALU.is_equal)
                        ins.then_inc(plain_rows.sem, 1)
                    nc.gpsimd.drain()
            with nc.gpsimd.Fori(0, DEPTH) as l:
                for k, n in enumerate((T, 2 * T, T * DH, T, T, T)):
                    inverse_roots("b", l, k + 1, n)

        @block_.vector
        def _(dve_):
            dve = nc.vector

            def mean_squares(rows, scratch, n, at=0):
                for t in range(T):
                    ins = dve.tensor_tensor_reduce(scratch[:, t], rows[:, t], rows[:, t], 1.0 / n, EPS, ALU.mult,
                                                   ALU.add, var[:, at + t:at + t + 1])
                return ins

            def square_means(sq, rows, heads, n, at=0):
                dve.tensor_tensor(sq, rows, rows, ALU.mult)
                dve.drain()
                dve.tensor_reduce(var[:, at:at + heads].rearrange("p (t h) -> p t h", t=T),
                                  sq.rearrange("p t (h e) -> p t h e", e=n), X, ALU.add)
                dve.drain()
                return dve.tensor_scalar(var[:, at:at + heads], var[:, at:at + heads], 1.0 / n, EPS, ALU.mult, ALU.add)

            def scaled(block, l, k, dst, rows, gain):
                dve.wait_ge(*rstd_ready.at(block, l, k))
                for t in range(T):
                    ins = dve.scalar_tensor_tensor(dst[:, t], rows[:, t], rstd[:, t:t + 1], gain, ALU.mult, ALU.mult)
                return ins

            def modulated(block, l, k, gain, shift):
                scaled(block, l, k, hn, x, gain)
                dve.drain()
                dve.tensor_tensor(hn[:, :, :], hn[:, :, :], spread(shift, 1, T), ALU.add).then_inc(h_ready.sem, 1)

            def rotate(heads1, heads2, cos, sin, tmp):
                n = heads1.shape[2]
                c, s = spread(cos, 2, n), spread(sin, 2, n)
                dve.tensor_tensor(tmp[0], heads1, c, ALU.mult)
                dve.tensor_tensor(tmp[1], heads2, s, ALU.mult)
                dve.tensor_tensor(tmp[2], heads2, c, ALU.mult)
                dve.tensor_tensor(tmp[3], heads1, s, ALU.mult)
                dve.drain()
                dve.tensor_tensor(heads1, tmp[0], tmp[1], ALU.subtract)
                return dve.tensor_tensor(heads2, tmp[2], tmp[3], ALU.add)

            def masked(block, l, g):
                d, s, use = group(block, g), sm_of(block), f"sc{g}"
                dve.wait_ge(*accs.full_at(block, l, use))
                b = accs.buf(block, use)
                for hh in range(2):
                    ins = dve.scalar_tensor_tensor(s[:, g % 2, 2 * hh:2 * hh + 2].rearrange("p t s -> p (t s)"),
                                                   acc[:, b, 2 * hh:2 * hh + 2].rearrange("p t s -> p (t s)"), d["scale"],
                                                   d["mask"](hh).rearrange("p t s -> p (t s)"), ALU.mult, ALU.add)
                ins.then_inc(accs.free_sem(block, use), 1)
                dve.drain()
                dve.tensor_reduce(mx, s[:, g % 2], X, ALU.max)
                dve.drain()
                if block == "a":
                    sink = spread(sinks.rearrange("p (hh j) -> p j hh", hh=2)[:, g], 2, T)
                    mx2, es2, nm2 = (v.rearrange("p (hh t) -> p hh t", t=T) for v in (mx, esink[:, g % 2], nm[:, g % 2]))
                    dve.tensor_tensor(mx2, mx2, sink, ALU.max)
                    dve.drain()
                    dve.tensor_scalar(nm[:, g % 2], mx, -1.0, None, ALU.mult)
                    dve.drain()
                    dve.tensor_tensor(es2, nm2, sink, ALU.add).then_inc(sm_ready.sem, 1)
                else:
                    dve.tensor_scalar(nm[:, g % 2], mx, -1.0, None, ALU.mult).then_inc(sm_ready.sem, 1)

            def sums(block, l, g):
                dve.wait_ge(*p_ready.at(block, l, g + 1))
                if block == "a":
                    dve.tensor_tensor(den[:, g % 2], den[:, g % 2], esink[:, g % 2], ALU.add)
                    dve.drain()
                dve.reciprocal(rden[:, g % 2], den[:, g % 2])
                keep_probs(dve, block, l, g, 1)

            def attended(block, l, g):
                use = f"pv{g}"
                dve.wait_ge(*turns.full_at(block, l, use))
                dvw = group(block, g)["dv"]
                src = turn_ps[:, turns.buf(block, use), :].rearrange("p (u e) -> p u e", u=4)[:, :, 0:dvw]
                r = rden[:, g % 2]
                if block == "a":
                    dst = oa.rearrange("p t (hh j e) -> p j hh t e", hh=2, j=4)[:, g]
                elif g < 4:
                    dve.tensor_scalar(rden[:, g % 2, 2:4], rden[:, g % 2, 2:4], neglam, None, ALU.mult)
                    dve.drain()
                    o4 = bt.rearrange("p t (u e) -> p (t u) e", u=4)[:, 0:4]
                    dve.tensor_tensor(o4, src, spread(r, 2, dvw), ALU.mult).then_inc(turns.free_sem(block, use), 1)
                    dve.drain()
                    dve.tensor_tensor(ob[:, :, g * P:g * P + P], o4[:, 0:2], o4[:, 2:4], ALU.add)
                    return
                elif g < 6:
                    dst = ob[:, :, BW:2 * BW].rearrange("p t (h e) -> p h t e", e=dvw)[:, 2 * (g - 4):2 * (g - 4) + 2]
                else:
                    dst = ob[:, :, 2 * BW:3 * BW].rearrange("p t (h e) -> p h t e", e=dvw)[:, 2 * (g - 6):2 * (g - 6) + 2]
                src = src.rearrange("p (hh t) e -> p hh t e", hh=2)
                r = r.rearrange("p (hh t) -> p hh t", hh=2)
                for hh in range(2):
                    ins = dve.tensor_tensor(dst[:, hh], src[:, hh], spread(r[:, hh], 2, dvw), ALU.mult)
                ins.then_inc(turns.free_sem(block, use), 1)

            dve.wait_ge(consts_in, 16 * N_CONSTS)
            dve.wait_ge(c_exp, 1)
            dve.tensor_scalar(csg, csg, 1.0, None, ALU.add)
            dve.tensor_copy(posf[:, :, 0], posi.bitcast(I32))
            dve.tensor_copy(posf[:, :, 1], posi2.bitcast(I32))
            dve.drain()
            dve.reciprocal(csg, csg)
            dve.drain()
            dve.tensor_tensor(cac, cT, csg, ALU.mult)
            for t in range(T):
                dve.tensor_scalar(ang[:, 8 * t:8 * t + 8], freqs[:, 0:8], posf[:, t, 0:1], None, ALU.mult)
                dve.tensor_scalar(ang[:, 16 + 16 * t:32 + 16 * t], freqs[:, 8:24], posf[:, t, 1:2], None, ALU.mult)
            dve.drain()
            dve.tensor_scalar(turnsN, ang, 1.0 / (2 * np.pi), None, ALU.mult)
            dve.drain()
            dve.tensor_scalar(turnsN, turnsN, ROUND_MAGIC, None, ALU.add)
            dve.drain()
            dve.tensor_scalar(turnsN, turnsN, ROUND_MAGIC, None, ALU.subtract)
            dve.drain()
            for part in (TWO_PI_HI, TWO_PI_MID, TWO_PI_LO):
                dve.scalar_tensor_tensor(ang, turnsN, -part, ang, ALU.mult, ALU.add)
                dve.drain()
            dve.tensor_scalar(redu, ang, 3.1415925, -3.1415925, ALU.min, ALU.max)
            dve.drain()
            dve.tensor_scalar(absr, redu, -1.0, None, ALU.mult)
            dve.drain()
            dve.tensor_tensor(absr, absr, redu, ALU.min)
            dve.drain()
            dve.tensor_scalar(absr, absr, float(np.pi / 2), None, ALU.add).then_inc(angle_ready, 1)
            dve.wait_ge(trig_done, 1)
            dve.wait_ge(x_in, 16)

            with dve.Fori(0, DEPTH) as l:
                dve.tensor_copy(cbc, spread(cac, 2, P)).then_inc(c_ready.sem, 1)
                mean_squares(x, hn, D).then_inc(var_ready.sem, 1)
                dve.wait_ge(*mod_bias.at("a", l, 1))
                for i in range(12):
                    use = f"ada{i}"
                    dve.wait_ge(*accs.full_at("a", l, use))
                    m = mod[:, i // 2, (i % 2) * 512:(i % 2) * 512 + 512]
                    dve.tensor_tensor(m, acc_nat(accs.buf("a", use))[:, 0, :], m, ALU.add)\
                        .then_inc(accs.free_sem("a", use), 1)
                dve.drain()
                dve.wait_ge(*params.at("a", l, params.per["a"]))
                for gain, sc in ((gain1, mod[:, 1]), (gain2, mod[:, 4])):
                    dve.scalar_tensor_tensor(gain, sc, 1.0, gain, ALU.add, ALU.mult)
                dve.tensor_copy(gate2, mod[:, 5])
                dve.drain()
                modulated("a", l, 1, gain1, mod[:, 0])
                for g in (1, 3):
                    keep_turned(dve, "a", l, f"h1_{g}", hT[:, 2 * g:2 * g + 2, :])
                dve.memset(conv_u[:, :, 0:1], 0.0)
                dve.memset(conv_u[:, :, S + 1:S + 2], 0.0)
                dve.wait_ge(*accs.emptied_at("a", l, "in0"))
                dve.wait_ge(*accs.emptied_at("a", l, "in1"))
                square_means(sq_a, z[:, :, 0:QKH * HD], T * QKH, HD).then_inc(var_ready.sem, 1)
                dve.wait_ge(*rstd_ready.at("a", l, 2))
                heads = z[:, :, 0:QKH * HD].rearrange("p t (h e) -> p t h e", e=HD)
                for t in range(T):
                    dve.tensor_tensor(heads[:, t], heads[:, t], spread(rstd[:, t * QKH:(t + 1) * QKH], 2, HD), ALU.mult)
                dve.drain()
                for t in range(T):
                    dve.tensor_tensor(heads[:, t, 0:8], heads[:, t, 0:8], spread(qg, 1, 8), ALU.mult)
                    dve.tensor_tensor(heads[:, t, 8:10], heads[:, t, 8:10], spread(kg, 1, 2), ALU.mult)
                dve.drain()
                rt = [rope_t[:, i].rearrange("p t (h e) -> p t h e", e=8) for i in range(4)]
                rotate(heads[:, :, :, 0:8], heads[:, :, :, 8:16], cosA, sinA, rt).then_inc(qk_ready.sem, 1)
                keep_turned(dve, "a", l, "q1", qT[:, 2:4])
                dve.wait_ge(*accs.emptied_at("a", l, "in2"))
                dve.tensor_tensor(conv_u[:, :, 1:S + 1], zT[:, 0:2], zT[:, 4:6], ALU.mult)
                dve.drain()
                for c in range(2):
                    dve.tensor_scalar(conv_a[:, c], conv_u[:, c, 0:S], conv_w[:, c, 0:1], None, ALU.mult)
                dve.drain()
                for k in (1, 2):
                    for c in range(2):
                        dve.scalar_tensor_tensor(conv_a[:, c], conv_u[:, c, k:k + S], conv_w[:, c, k:k + 1], conv_a[:, c],
                                                 ALU.mult, ALU.add)
                    dve.drain()
                dve.tensor_tensor(mixT[:, 4:6], conv_a, zT[:, 2:4], ALU.mult).then_inc(conv_ready.sem, 1)
                masked("a", l, 0)
                masked("a", l, 1)
                for g in range(4):
                    sums("a", l, g)
                    if g + 2 < 4:
                        masked("a", l, g + 2)
                    attended("a", l, g)
                dve.drain().then_inc(mix_ready.sem, 1)
                keep_turned(dve, "a", l, "mix1", mixT[:, 2:4])
                for n in range(GC):
                    use, cols = f"out{n}", slice(512 * n, 512 * n + 512)
                    dve.wait_ge(*accs.full_at("a", l, use))
                    dve.tensor_tensor(hn[:, :, cols], acc_nat(accs.buf("a", use)), spread(mod[:, 2, cols], 1, T), ALU.mult)\
                        .then_inc(accs.free_sem("a", use), 1)
                    dve.drain()
                    dve.tensor_tensor(x[:, :, cols], x[:, :, cols], hn[:, :, cols], ALU.add)
                dve.drain()
                mean_squares(x, hn, D).then_inc(var_ready.sem, 1)
                modulated("a", l, 3, gain2, mod[:, 3])
                for g in (1, 3):
                    keep_turned(dve, "a", l, f"h2_{g}", hT[:, 2 * g:2 * g + 2, :])

                def best16(rows):
                    for s, v, i in rows:
                        dve.max(v[:, 0:8], s)
                    dve.drain()
                    for s, v, i in rows:
                        dve.max_index(i[:, 0:8], v[:, 0:8], s)
                    dve.drain()
                    for s, v, i in rows:
                        dve.match_replace(s, v[:, 0:8], s, -3.4e38)
                    dve.drain()
                    for s, v, i in rows:
                        dve.max(v[:, 8:16], s)
                    dve.drain()
                    for s, v, i in rows:
                        dve.max_index(i[:, 8:16], v[:, 8:16], s)
                    dve.drain()

                bu, tu = best_p.bitcast(U32), top_i.bitcast(U32)
                bh = best_h.bitcast(U32)
                tv = top_v.rearrange("p t (h f) k -> p t h f k", f=2)
                tf = top_f.rearrange("p t (h f) k -> p t h f k", f=2)
                io16 = iota[:, 0:PK]
                for c in range(4):
                    lists, hs, ks = range(4 * c, 4 * c + 4), range(2 * c, 2 * c + 2), slice(2 * c * PK, (2 * c + 2) * PK)
                    dve.wait_ge(*accs.emptied_at("a", l, f"s{c}"))
                    dve.sem_inc(passed["dve"], 1)
                    best16([(scores[:, t, b], top_v[:, t, b], tu[:, t, b]) for t in range(T) for b in lists])
                    for t in range(T):
                        dve.tensor_copy(top_f[:, t, 4 * c:4 * c + 4], tu[:, t, 4 * c:4 * c + 4])
                        for h in hs:
                            dve.tensor_tensor(cand[:, t, h].rearrange("p (i j) -> p i j", i=PK),
                                              spread(tv[:, t, h, 0], 2, PK), spread(tv[:, t, h, 1], 1, PK), ALU.add)
                    dve.drain()
                    best16([(cand[:, t, h], best[:, t, h], bu[:, t, h * PK:(h + 1) * PK]) for t in range(T) for h in hs])
                    dve.tensor_scalar(bh[:, 0, :, ks], bu[:, :, ks], 4, None, ALU.logical_shift_right)
                    dve.tensor_scalar(bh[:, 1, :, ks], bu[:, :, ks], 15, None, ALU.bitwise_and)
                    dve.drain()
                    for f in range(2):
                        dve.tensor_copy(best_hf[:, f, :, ks], bh[:, f, :, ks])
                    dve.drain()
                    p5 = pick.rearrange("p (f t) (a m) -> p f t a m", f=2, m=PK)
                    for f in range(2):
                        for t in range(T):
                            dve.tensor_tensor(p5[:, f, t], spread(best_hf[:, f, t, ks], 2, PK), spread(io16, 1, 2 * PK),
                                              ALU.is_equal)
                    dve.drain()
                    for f in range(2):
                        for t in range(T):
                            p4 = p5[:, f, t].rearrange("p (h k) m -> p h k m", h=2)
                            dve.tensor_tensor(p4, p4, spread(tf[:, t, 2 * c:2 * c + 2, f], 2, PK), ALU.mult)
                    dve.drain()
                    for f in range(2):
                        ins = dve.tensor_reduce(pairs[:, f, :, ks], p5[:, f], X, ALU.add)
                    if c < 3:
                        dve.drain()
                ins.then_inc(pairs_ready.sem, 1)
                bflat = best.rearrange("p t h k -> p (t h) k")
                gflat = pairs[:, 2].rearrange("p t (h k) -> p (t h) k", k=PK)
                dve.tensor_tensor(gflat, bflat, bflat[:, :, 0:1].broadcast_to([P, T * PH, PK]), ALU.subtract)\
                    .then_inc(top_ready.sem, 1)
                dve.wait_ge(*htr_hi.at("a", l, 1))
                dve.tensor_tensor(hTr[:, 1], hT[:], hTr[:, 0].bitcast(F32), ALU.subtract).then_inc(htr_lo.sem, 1)
                dve.wait_ge(*top_exp.at("a", l, 1))
                dve.tensor_reduce(dsum, gflat, X, ALU.add)
                dve.drain()
                dve.reciprocal(dsum, dsum)
                dve.drain()
                dve.tensor_tensor(gflat, gflat, spread(dsum, 2, PK), ALU.mult).then_inc(pairs_ready.sem, 1)
                keep_turned(dve, "a", l, "pairs1", pairsT[:, 2], n=S)
                dve.wait_ge(*turns.emptied_at("a", l, "pairs0"))
                dve.sem_inc(passed["dve"], 1)
                dve.drain()
                with dve.Fori(0, S // TOKG // STEP) as it:
                    dve.tensor_copy(turn_keys, pairsT[:, :, bass.ds(it * (STEP * TOKG), STEP * TOKG)])
                    dve.drain()
                    for j in range(STEP):
                        n = it * STEP + j
                        dve.wait_ge(*gates_full.two_before("a", l, n + 1))
                        for q in range(TOKG):
                            tok = j * TOKG + q
                            dve.tensor_scalar(rows[:, j % 2, 0, q, :], iota[:], turn_keys[:, 0, tok:tok + 1],
                                              turn_keys[:, 2, tok:tok + 1], ALU.is_equal, ALU.mult)
                        second = turn_keys[:, 1, j * TOKG + POOLQ:(j + 1) * TOKG]
                        dve.tensor_tensor(rows[:, j % 2, 1, POOLQ:TOKG], spread(iota[:], 1, TOKG - POOLQ), spread(second, 2, P),
                                          ALU.is_equal).then_inc(gated_rows.sem, 1)
                    dve.drain()
                dve.wait_ge(*gates_kept.at("a", l, S // TOKG))

                def u_low(i, m):
                    dve.wait_ge(*ut_act.at("a", l, i + 1))
                    dve.tensor_tensor(utr[:, m % 2, 1], turn_ps[:].rearrange("p b s -> p (b s)"),
                                      utr[:, m % 2, 0].bitcast(F32), ALU.subtract).then_inc(ut_dve.sem, 1)

                def weighted(i, m):
                    dve.wait_ge(*gelu_done.at("a", l, i + 1))
                    row = G[:, i, :] if isinstance(i, int) else G[:, bass.ds(i, 1), :].rearrange("p a s -> p (a s)")
                    g = ga[:, m % 2, :]
                    dve.tensor_tensor(g, g, row, ALU.mult)
                    dve.drain()
                    dve.tensor_copy(wtr[:, m % 2, 0], g)
                    dve.drain()
                    dve.tensor_tensor(wtr[:, m % 2, 1], g, wtr[:, m % 2, 0].bitcast(F32), ALU.subtract)\
                        .then_inc(wt_ready.sem, 1)

                def v_low(i, m):
                    dve.wait_ge(*v_hi.at("a", l, i + 1))
                    dve.tensor_tensor(vr[:, 1], expert_v[:, m % 2], vr[:, 0].bitcast(F32), ALU.subtract)\
                        .then_inc(v_lo.sem, 1)

                u_low(0, 0)
                for i in range(3):
                    u_low(i + 1, i + 1)
                    weighted(i, i)
                    v_low(i, i)
                with dve.Fori(0, NKEYS // 4 - 1) as it:
                    for j in range(4):
                        i = it * 4 + (3 + j)
                        u_low(i + 1, j)
                        weighted(i, (3 + j) % 4)
                        v_low(i, (3 + j) % 4)
                weighted(NKEYS - 1, 3)
                v_low(NKEYS - 1, 3)
                dve.wait_ge(*y_full.at("a", l, 1))
                yflat = y_ps.rearrange("p t n s -> p t (n s)")
                dve.tensor_tensor(hn[:, :, :], yflat, spread(gate2, 1, T), ALU.mult)
                dve.drain()
                dve.tensor_tensor(x[:], x[:], hn[:, :, :], ALU.add).then_inc(layer_done.sem, 1)
                dve.drain()

            dve.wait_ge(t5_in, 64)
            dve.wait_ge(t5_row, 1)
            dve.tensor_copy(t5row[0:8, :], acc_nat(0)[0:8, 0, :]).then_inc(t5_kept, 1)
            for h in range(8):
                dve.wait_ge(t5_flip, h + 1)
                dve.tensor_tensor(bias[:, h].rearrange("p t s -> p (t s)"), t5_bank(h),
                                  causal.rearrange("p t s -> p (t s)"), ALU.add).then_inc(t5_done, 1)
            dve.drain()

            with dve.Fori(0, DEPTH) as l:
                mean_squares(x, bn, D).then_inc(var_ready.sem, 1)
                dve.wait_ge(*pre_gain.at("b", l, 1))
                scaled("b", l, 1, bn, x, wpre).then_inc(h_ready.sem, 1)
                for g in (1, 3):
                    keep_turned(dve, "b", l, f"h_{g}", hT[:, 2 * g:2 * g + 2, :])
                dve.wait_ge(*params.at("b", l, params.per["b"]))
                d4 = dlam.rearrange("p (a b) e -> p a b e", a=2)
                prod = bt[:, 0, 0:2 * HD].rearrange("p (a e) -> p a e", a=2)
                dve.tensor_tensor(prod, d4[:, :, 0], d4[:, :, 1], ALU.mult)
                dve.drain()
                dve.tensor_reduce(ldot, prod, X, ALU.add).then_inc(lam_dot.sem, 1)
                dve.tensor_scalar(subln, subln, lamc[:, 1:2], None, ALU.mult)
                dve.wait_ge(*lam_exp.at("b", l, 1))
                dve.tensor_tensor(neglam, lexp[:, 1:2], lexp[:, 0:1], ALU.subtract)
                dve.drain()
                dve.tensor_tensor(neglam, neglam, lamc[:, 0:1], ALU.subtract)
                masked("b", l, 0)
                for g in range(4):
                    sums("b", l, g)
                    masked("b", l, g + 1)
                    attended("b", l, g)
                sums("b", l, 4)
                masked("b", l, 5)
                dve.wait_ge(*accs.emptied_at("b", l, "misc0"))
                mean_squares(cc[:, :, 0:QR], bt2, QR)
                mean_squares(cc[:, :, QR:QR + KVR], bt[:, :, 0:KVR], KVR, at=T).then_inc(var_ready.sem, 1)
                dve.wait_ge(*rstd_ready.at("b", l, 2))
                for t in range(T):
                    ins = dve.scalar_tensor_tensor(bt2[:, t], cc[:, t, 0:QR], rstd[:, t:t + 1], cqg, ALU.mult, ALU.mult)
                ins.then_inc(qk_ready.sem, 1)
                for t in range(T):
                    ins = dve.scalar_tensor_tensor(bt[:, t, 0:KVR], cc[:, t, QR:QR + KVR], rstd[:, T + t:T + t + 1], ckvg,
                                                   ALU.mult, ALU.mult)
                ins.then_inc(qk_ready.sem, 1)
                keep_turned(dve, "b", l, "ckv", ckvT, n=S)
                attended("b", l, 4)
                sums("b", l, 5)
                attended("b", l, 5)
                dve.drain()
                sq3 = bn[:, :, 0:512]
                square_means(sq3, ob[:, :, 0:BW], T * DH, P).then_inc(var_ready.sem, 1)
                dve.wait_ge(*rstd_ready.at("b", l, 3))
                oh = ob[:, :, 0:BW].rearrange("p t (h e) -> p t h e", e=P)
                for t in range(T):
                    dve.tensor_tensor(oh[:, t], oh[:, t], spread(rstd[:, t * DH:(t + 1) * DH], 2, P), ALU.mult)
                dve.drain()
                for t in range(T):
                    ins = dve.tensor_tensor(oh[:, t], oh[:, t], spread(subln, 1, DH), ALU.mult)
                ins.then_inc(mix_ready.sem, 1)
                dve.drain().then_inc(mix_ready.sem, 1)
                dve.wait_ge(*accs.emptied_at("b", l, "uq0"))
                dve.wait_ge(*accs.emptied_at("b", l, "uq1"))
                q4 = qn.rearrange("p t (h e) -> p t h e", e=LQ)
                rt = [bn[:, i // 2, 256 * (i % 2):256 * (i % 2) + 256].rearrange("p (t h e) -> p t h e", t=T, h=LH) for i in range(4)]
                rotate(q4[:, :, :, NOPE:NOPE + 16], q4[:, :, :, NOPE + 16:LQ], cosB, sinB, rt).then_inc(qk_ready.sem, 1)
                dve.wait_ge(*accs.emptied_at("b", l, "misc1"))
                k1 = cc[:, :, 384:400].unsqueeze(2)
                k2 = cc[:, :, 400:416].unsqueeze(2)
                rt = [bn[:, i // 2, 512 + 32 * (i % 2):512 + 32 * (i % 2) + 32].rearrange("p (t h e) -> p t h e", t=T, h=1) for i in range(4)]
                rotate(k1, k2, cosB, sinB, rt)
                dve.wait_ge(*accs.emptied_at("b", l, "ukv0"))
                dve.wait_ge(*accs.emptied_at("b", l, "ukv1"))
                dve.sem_inc(passed["dve"], 1)
                kf4 = kf.rearrange("p t (h e) -> p t h e", e=LQ)
                kv4 = kv.rearrange("p t (h e) -> p t h e", e=128)
                dve.drain()
                for t in range(T):
                    dve.tensor_copy(kf4[:, t, :, 0:NOPE], kv4[:, t, :, 0:NOPE])
                    ins = dve.tensor_copy(kf4[:, t, :, NOPE:LQ], spread(cc[:, t, 384:416], 1, LH))
                ins.then_inc(qk_ready.sem, 1)
                for i in (1, 3):
                    keep_turned(dve, "b", l, f"qm{i}", qmT[0:LQ, 2 * i:2 * i + 2], rows=LQ)
                for i in (1, 3):
                    keep_turned(dve, "b", l, f"km{i}", kmT[0:LQ, 2 * i:2 * i + 2], rows=LQ)
                masked("b", l, 6)
                for g in range(6, 10):
                    sums("b", l, g)
                    if g < 9:
                        masked("b", l, g + 1)
                    attended("b", l, g)
                dve.drain().then_inc(mix_ready.sem, 1)
                for c in range(NB):
                    keep_turned(dve, "b", l, f"bt{2 * c + 1}", brT[:, 4 * c + 2:4 * c + 4])
                for c in range(NB):
                    for n in range(GC):
                        use, cols = f"br{c}_{n}", slice(512 * n, 512 * n + 512)
                        dve.wait_ge(*accs.full_at("b", l, use))
                        if c == 0 and n == 0:
                            dve.wait_ge(*accs.emptied_at("b", l, "g5"))
                        gcol = gates[:, :, c * D + 512 * n:c * D + 512 * n + 512]
                        for t in range(T):
                            ins = dve.scalar_tensor_tensor(bt[:, t], gcol[:, t], 1.0, acc_nat(accs.buf("b", use))[:, t],
                                                           ALU.add, ALU.mult)
                        ins.then_inc(accs.free_sem("b", use), 1)
                        dve.drain()
                        for t in range(T):
                            if c == 0:
                                ins = dve.tensor_scalar(bn[:, t, cols], bt[:, t], 0.5, None, ALU.mult)
                            else:
                                ins = dve.scalar_tensor_tensor(bn[:, t, cols], bt[:, t], 0.5, bn[:, t, cols], ALU.mult, ALU.add)
                        if c == NB - 1 and n == GC - 1:
                            ins.then_inc(mix_ready.sem, 1)
                        dve.drain()

                def add_normed(k, gain):
                    btf = bt.rearrange("p t e -> p (t e)")
                    for t in range(T):
                        dve.tensor_tensor_reduce(btf, bn[:, t], bn[:, t], 1.0 / D, EPS, ALU.mult, ALU.add, var[:, t:t + 1])
                        dve.drain()
                    dve.drain().then_inc(var_ready.sem, 1)
                    dve.wait_ge(*rstd_ready.at("b", l, k))
                    for t in range(T):
                        dve.scalar_tensor_tensor(bn[:, t], bn[:, t], rstd[:, t:t + 1], gain, ALU.mult, ALU.mult)
                    dve.drain()
                    return dve.tensor_tensor(x[:], x[:], bn[:, :, :], ALU.add)

                for g in (1, 3):
                    keep_turned(dve, "b", l, f"mx_{g}", hT[:, 2 * g:2 * g + 2, :])
                dve.wait_ge(*accs.emptied_at("b", l, "wo0"))
                dve.wait_ge(*accs.emptied_at("b", l, "wo1"))
                add_normed(4, wpost)
                dve.drain()
                mean_squares(x, bn, D).then_inc(var_ready.sem, 1)
                scaled("b", l, 5, bn, x, wmpre).then_inc(h_ready.sem, 1)

                def slab_low(i):
                    for u in (2 * i, 2 * i + 1):
                        dve.wait_ge(*mlp_hi.at("b", l, u + 1))
                        dve.tensor_tensor(mlp_operand(u, 1), mlp_raw(MLP[i])(u % 2), mlp_high(u).bitcast(F32),
                                          ALU.subtract).then_inc(mlp_lo.sem, 1)

                slab_low(0)
                for g in range(4):
                    dve.wait_ge(*hm_hi.at("b", l, g + 1))
                    hi, lo = (r[:, 2 * g:2 * g + 2].rearrange("p k s -> p (k s)") for r in hm_r)
                    dve.tensor_tensor(lo, turn_ps[:, turns.buf("b", f"hm_{g}"), :], hi.bitcast(F32), ALU.subtract)\
                        .then_inc(turns.free_sem("b", f"hm_{g}"), 1)
                for i in range(16):
                    if i < 15:
                        slab_low(i + 1)
                    if i < 8:
                        r = relu_b[:, i % 2]
                        uh, ul = (uTr[:, part, 4 * i:4 * i + 4] for part in range(2))
                        dve.wait_ge(*accs.emptied_at("b", l, f"up{i}"))
                        dve.tensor_tensor(r, r, r, ALU.mult)
                        dve.drain()
                        dve.tensor_copy(uh, r)
                        dve.drain()
                        dve.tensor_tensor(ul, r, uh.bitcast(F32), ALU.subtract).then_inc(u_ready.sem, 1)
                dve.wait_ge(*accs.emptied_at("b", l, "dn0"))
                dve.wait_ge(*accs.emptied_at("b", l, "dn1"))
                add_normed(6, wmpost).then_inc(layer_done.sem, 1)
                dve.drain()


def constants():
    tok = np.arange(S)
    rel = tok[:, None] - tok[None, :]

    def tiles(m):
        return np.ascontiguousarray(m.reshape(T, P, S).transpose(1, 0, 2)).astype(np.float32)

    pool = np.zeros((S, 4, S), np.float32)
    for g, w in enumerate((2, 4, 8, 16)):
        for t in range(S):
            lo, hi = max(t - w // 2, 0), min(t + w // 2, S)
            pool[lo:hi, g, t] = 1.0 / (hi - lo)
            pool[t, g, t] -= 1.0
    n = np.arange(S)
    nf = np.maximum(n, 1).astype(np.float32)
    large = 16 + (np.log(nf / np.float32(16)) / np.float32(np.log(64.0)) * np.float32(16)).astype(np.int32)
    bucket = np.where(n < 16, n, np.minimum(large, BUCKETS - 1))
    onehot = np.zeros((BUCKETS, 512), np.float32)
    for r in range(511):
        onehot[bucket[max(255 - r, 0)], r] = 1.0
    lam = [0.8 - 0.6 * np.exp(-0.3 * l) for l in range(DEPTH)]
    return {
        "k_ident": np.eye(P, dtype=np.float32),
        "k_flip": np.ascontiguousarray(np.eye(P, dtype=np.float32)[::-1]),
        "k_iota": np.broadcast_to(np.arange(P, dtype=np.float32), (P, P)).copy(),
        "k_window": tiles(np.where(np.abs(rel) <= 128, 0.0, NEG)),
        "k_causal": tiles(np.where(rel >= 0, 0.0, NEG)),
        "k_pool": np.ascontiguousarray(pool.reshape(T, P, 4 * S).transpose(1, 0, 2)).reshape(P, T * 4 * S),
        "k_onehot": onehot,
        "k_freqs": np.concatenate([500000.0 ** (-np.arange(0, 16, 2) / 16), 10000.0 ** (-np.arange(16) * 2.0 / 32)]).astype(np.float32),
        "k_neghalf": np.full(32, -0.5, np.float32),
        "k_lam": np.array([[v, 1.0 - v] for v in lam], np.float32),
    }


def kernel(**inputs):
    import concourse.bacc as bacc
    from concourse.bass_utils import run_bass_kernel_spmd

    nc = bacc.Bacc("TRN2", target_bir_lowering=False, num_devices=1)
    arrays, io = {}, {}
    for name, a in {**inputs, **constants()}.items():
        a = np.ascontiguousarray(a)
        arrays[f"in_{name}"] = a
        io[name] = nc.dram_tensor(f"in_{name}", a.shape, mybir.dt.from_np(a.dtype), kind="ExternalInput").ap()
    out = nc.dram_tensor("out_x", (1, S, D), F32, kind="ExternalOutput").ap()
    two_blocks(nc, io, out)
    r = run_bass_kernel_spmd(nc, [arrays], core_ids=[0])
    return r.results[0]["out_x"]
```
